# Optimizing a Trainium2 kernel written in Bass

```python
import math
import jax
import jax.numpy as jnp
from jax import lax
import numpy as np

D_MODEL = 1024
BATCH = 1
SEQ = 512
DEPTH = 1
DEC_BATCH = 8
DEC_SEQ = 4
PAST_LEN = 512
PAGE_SIZE = 128

ATTN_W = D_MODEL // 2
POOL_W = D_MODEL - ATTN_W
HEAD_DIM = 64
QK_HEAD = 2 * HEAD_DIM
VAL_DIM = 2 * HEAD_DIM
N_HEADS = ATTN_W // VAL_DIM
QK_W = N_HEADS * QK_HEAD
POOL_WINDOWS = (2, 4, 8, 16)
N_POOL_GROUPS = len(POOL_WINDOWS)
POOL_GROUP_W = POOL_W // N_POOL_GROUPS
POOL_BUF = max(POOL_WINDOWS) - 1
IN_W = POOL_W + 2 * QK_W + N_HEADS * VAL_DIM
MIX_W = POOL_W + N_HEADS * VAL_DIM
N_EXPERTS = 32
TOP_K = 4
D_FF = D_MODEL
SWIGLU_LIMIT = 7.0
SWIGLU_ALPHA = 1.702
EXPERT_BLOCK = 128
Q_BLOCK = 128
RMS_EPS = 1e-6
NEG_INF = -1e30

kernel_name = 'hymba_pool_diffattn_moe_step'

def _rmsnorm(x, g):
    xf = x.astype(jnp.float32)
    y = xf * lax.rsqrt(jnp.mean(xf * xf, axis=-1, keepdims=True) + RMS_EPS)
    return (y * g.astype(jnp.float32)).astype(x.dtype)

def _pool_mix(u_ext, pos0, n_out, pool_w, pool_scale):
    B, L, _ = u_ext.shape
    ug = u_ext.astype(jnp.float32).reshape(B, L, N_POOL_GROUPS, POOL_GROUP_W)
    cs = jnp.cumsum(ug, axis=1)
    pos = (pos0 + jnp.arange(L)).astype(jnp.float32)
    diffs = []
    for g, w in enumerate(POOL_WINDOWS):
        c = cs[:, :, g]
        c_prev = jnp.pad(c, ((0, 0), (w, 0), (0, 0)))[:, :L]
        cnt = jnp.minimum(float(w), pos + 1.0)
        diffs.append((c - c_prev) / cnt[None, :, None] - ug[:, :, g])
    d = jnp.stack(diffs, axis=2)[:, L - n_out:]
    out = jnp.einsum('btgc,gce->btge', d.astype(pool_w.dtype), pool_w)
    return (out.reshape(B, n_out, POOL_W) * pool_scale).astype(u_ext.dtype)

def _diff_attn_block(q, qpos, k, v, kpos, slopes, lam):
    s = jnp.einsum('bqhcd,bkhcd->bhcqk', q, k, preferred_element_type=jnp.float32) * (HEAD_DIM ** -0.5)
    dist = (qpos[:, None] - kpos[None, :]).astype(jnp.float32)
    s = s - slopes[None, :, None, None, None] * dist
    s = jnp.where(dist >= 0.0, s, NEG_INF)
    p = jax.nn.softmax(s, axis=-1)
    a = p[:, :, 0] - lam * p[:, :, 1]
    return jnp.einsum('bhqk,bkhe->bqhe', a.astype(v.dtype), v, preferred_element_type=jnp.float32)

def _diff_attention(q, k, v, qpos, kpos, slopes, lam):
    B, T = q.shape[0], q.shape[1]
    qb = Q_BLOCK if T % Q_BLOCK == 0 else T
    nb = T // qb
    qs = q.reshape(B, nb, qb, N_HEADS, 2, HEAD_DIM).swapaxes(0, 1)
    ps = qpos.reshape(nb, qb)
    out = lax.map(lambda a: _diff_attn_block(a[0], a[1], k, v, kpos, slopes, lam), (qs, ps))
    return out.swapaxes(0, 1).reshape(B, T, N_HEADS, VAL_DIM)

def _moe(h, router_w, router_b, w1, b1, w2, b2):
    N, D = h.shape
    logits = jnp.matmul(h, router_w, preferred_element_type=jnp.float32) + router_b.astype(jnp.float32)
    top_v, top_e = lax.top_k(logits, TOP_K)
    gates = jax.nn.softmax(top_v, axis=-1)
    A = N * TOP_K
    e_flat = top_e.reshape(A)
    g_flat = gates.reshape(A)
    tok_flat = jnp.arange(A, dtype=jnp.int32) // TOP_K
    order = jnp.argsort(e_flat)
    e_sorted = e_flat[order]
    counts = jnp.bincount(e_flat, length=N_EXPERTS)
    padded = (counts + EXPERT_BLOCK - 1) // EXPERT_BLOCK * EXPERT_BLOCK
    starts = jnp.cumsum(counts) - counts
    pad_ends = jnp.cumsum(padded)
    pad_starts = pad_ends - padded
    dest = pad_starts[e_sorted] + jnp.arange(A, dtype=jnp.int32) - starts[e_sorted]
    n_blocks = -(-A // EXPERT_BLOCK) + N_EXPERTS
    P = n_blocks * EXPERT_BLOCK
    row_tok = jnp.full((P,), N, jnp.int32).at[dest].set(tok_flat[order])
    row_gate = jnp.zeros((P,), jnp.float32).at[dest].set(g_flat[order])
    block_e = jnp.minimum(jnp.searchsorted(pad_ends, jnp.arange(n_blocks, dtype=jnp.int32) * EXPERT_BLOCK, side='right'), N_EXPERTS - 1)
    h_pad = jnp.concatenate([h, jnp.zeros((1, D), h.dtype)], axis=0)
    xb = h_pad[row_tok].reshape(n_blocks, EXPERT_BLOCK, D)

    def expert_block(args):
        xe, e = args
        a = xe @ w1[e] + b1[e]
        glu = jnp.minimum(a[:, 0::2], SWIGLU_LIMIT)
        lin = jnp.clip(a[:, 1::2], -SWIGLU_LIMIT, SWIGLU_LIMIT)
        act = glu * jax.nn.sigmoid(SWIGLU_ALPHA * glu) * (lin + 1.0)
        return act @ w2[e] + b2[e]

    yb = lax.map(expert_block, (xb, block_e)).reshape(P, D)
    y = jnp.zeros((N + 1, D), jnp.float32).at[row_tok].add(yb.astype(jnp.float32) * row_gate[:, None])
    return y[:N].astype(h.dtype)

def _layer(x, pos0, pool_prefix, k_prefix, v_prefix, lambda_init,
           norm1_g, w_in, pool_w, pool_scale, lq1, lk1, lq2, lk2, subln_g,
           w_out, norm2_g, router_w, router_b, w1, b1, w2, b2):
    B, T, D = x.shape
    xn = _rmsnorm(x, norm1_g)
    z = xn @ w_in
    u = z[..., :POOL_W]
    q = z[..., POOL_W:POOL_W + QK_W].reshape(B, T, N_HEADS, 2, HEAD_DIM)
    k_new = z[..., POOL_W + QK_W:POOL_W + 2 * QK_W].reshape(B, T, N_HEADS, QK_HEAD)
    v_new = z[..., POOL_W + 2 * QK_W:].reshape(B, T, N_HEADS, VAL_DIM)
    u_ext = u if pool_prefix is None else jnp.concatenate([pool_prefix.astype(u.dtype), u], axis=1)
    pool_pos0 = pos0 - (u_ext.shape[1] - T)
    pool_out = _pool_mix(u_ext, pool_pos0, T, pool_w, pool_scale)
    new_pool = u_ext[:, u_ext.shape[1] - POOL_BUF:]
    k_all = k_new if k_prefix is None else jnp.concatenate([k_prefix.astype(k_new.dtype), k_new], axis=1)
    v_all = v_new if v_prefix is None else jnp.concatenate([v_prefix.astype(v_new.dtype), v_new], axis=1)
    Lk = k_all.shape[1]
    qpos = pos0 + jnp.arange(T, dtype=jnp.int32)
    kpos = jnp.arange(Lk, dtype=jnp.int32)
    slopes = jnp.exp2(-8.0 * (jnp.arange(N_HEADS, dtype=jnp.float32) + 1.0) / N_HEADS)
    f32 = jnp.float32
    lam = (jnp.exp(jnp.sum(lq1.astype(f32) * lk1.astype(f32)))
           - jnp.exp(jnp.sum(lq2.astype(f32) * lk2.astype(f32))) + lambda_init)
    o = _diff_attention(q, k_all.reshape(B, Lk, N_HEADS, 2, HEAD_DIM), v_all, qpos, kpos, slopes, lam)
    o = (_rmsnorm(o, subln_g) * (1.0 - lambda_init)).astype(x.dtype).reshape(B, T, N_HEADS * VAL_DIM)
    mix = jnp.concatenate([pool_out, o], axis=-1) @ w_out
    h = x + mix
    ff = _moe(_rmsnorm(h, norm2_g).reshape(B * T, D), router_w, router_b, w1, b1, w2, b2)
    h = h + ff.reshape(B, T, D)
    return h, new_pool, k_new, v_new

def setup_inputs(seed: int = 0) -> dict:
    key = jax.random.key(seed)
    ks = jax.random.split(key, 26)
    f32 = jnp.float32
    n_pages = PAST_LEN // PAGE_SIZE
    n_used = DEC_BATCH * n_pages
    n_phys = n_used + max(1, n_used // 4)

    def nrm(k, shape, s):
        return jax.random.normal(k, shape, f32) * s

    page_table = jax.random.permutation(ks[5], n_phys)[:n_used].reshape(DEC_BATCH, n_pages).astype(jnp.int32)
    return {
        'x_prompt': nrm(ks[0], (BATCH, SEQ, D_MODEL), 1.0),
        'x_sample': nrm(ks[1], (DEC_BATCH, DEC_SEQ, D_MODEL), 1.0),
        'state_pool': nrm(ks[2], (DEPTH, DEC_BATCH, POOL_BUF, POOL_W), 1.0),
        'cache_k': nrm(ks[3], (DEPTH, n_phys, PAGE_SIZE, N_HEADS, QK_HEAD), 1.0),
        'cache_v': nrm(ks[4], (DEPTH, n_phys, PAGE_SIZE, N_HEADS, VAL_DIM), 1.0),
        'page_table': page_table,
        'norm1_g': 1.0 + nrm(ks[6], (DEPTH, D_MODEL), 0.02),
        'w_in': nrm(ks[7], (DEPTH, D_MODEL, IN_W), D_MODEL ** -0.5),
        'pool_w': nrm(ks[8], (DEPTH, N_POOL_GROUPS, POOL_GROUP_W, POOL_GROUP_W), POOL_GROUP_W ** -0.5),
        'pool_scale': 1.0 + nrm(ks[9], (DEPTH, POOL_W), 0.1),
        'lambda_q1': nrm(ks[10], (DEPTH, HEAD_DIM), 0.1),
        'lambda_k1': nrm(ks[11], (DEPTH, HEAD_DIM), 0.1),
        'lambda_q2': nrm(ks[12], (DEPTH, HEAD_DIM), 0.1),
        'lambda_k2': nrm(ks[13], (DEPTH, HEAD_DIM), 0.1),
        'subln_g': 1.0 + nrm(ks[14], (DEPTH, VAL_DIM), 0.02),
        'w_out': nrm(ks[15], (DEPTH, MIX_W, D_MODEL), MIX_W ** -0.5),
        'norm2_g': 1.0 + nrm(ks[16], (DEPTH, D_MODEL), 0.02),
        'router_w': nrm(ks[17], (DEPTH, D_MODEL, N_EXPERTS), D_MODEL ** -0.5),
        'router_b': nrm(ks[18], (DEPTH, N_EXPERTS), 0.01),
        'w1': nrm(ks[19], (DEPTH, N_EXPERTS, D_MODEL, 2 * D_FF), D_MODEL ** -0.5),
        'b1': nrm(ks[20], (DEPTH, N_EXPERTS, 2 * D_FF), 0.01),
        'w2': nrm(ks[21], (DEPTH, N_EXPERTS, D_FF, D_MODEL), D_FF ** -0.5),
        'b2': nrm(ks[22], (DEPTH, N_EXPERTS, D_MODEL), 0.01),
        'normf_g': 1.0 + nrm(ks[23], (D_MODEL,), 0.02),
    }

def reference(x_prompt, x_sample, state_pool, cache_k, cache_v, page_table,
              norm1_g, w_in, pool_w, pool_scale, lambda_q1, lambda_k1, lambda_q2, lambda_k2,
              subln_g, w_out, norm2_g, router_w, router_b, w1, b1, w2, b2, normf_g):
    dec_batch, n_pages = page_table.shape
    past_len = n_pages * cache_k.shape[2]
    hp = x_prompt
    hs = x_sample
    pool_p, pool_s, kp_l, vp_l, ks_l, vs_l = [], [], [], [], [], []
    for l in range(DEPTH):
        lambda_init = 0.8 - 0.6 * math.exp(-0.3 * l)
        params = (norm1_g[l], w_in[l], pool_w[l], pool_scale[l], lambda_q1[l], lambda_k1[l],
                  lambda_q2[l], lambda_k2[l], subln_g[l], w_out[l], norm2_g[l],
                  router_w[l], router_b[l], w1[l], b1[l], w2[l], b2[l])
        hp, pp, kp, vp = _layer(hp, 0, None, None, None, lambda_init, *params)
        k_past = cache_k[l][page_table].reshape(dec_batch, past_len, N_HEADS, QK_HEAD)
        v_past = cache_v[l][page_table].reshape(dec_batch, past_len, N_HEADS, VAL_DIM)
        hs, ps, kss, vss = _layer(hs, past_len, state_pool[l], k_past, v_past, lambda_init, *params)
        pool_p.append(pp)
        pool_s.append(ps)
        kp_l.append(kp)
        vp_l.append(vp)
        ks_l.append(kss)
        vs_l.append(vss)
    y_prompt = _rmsnorm(hp, normf_g)
    y_sample = _rmsnorm(hs, normf_g)
    return (y_prompt, y_sample, jnp.stack(pool_p), jnp.stack(pool_s), jnp.stack(kp_l), jnp.stack(vp_l), jnp.stack(ks_l), jnp.stack(vs_l))


_drawn_inputs = setup_inputs


def setup_inputs(seed=0):
    import zlib

    import numpy as np

    out = dict(_drawn_inputs(seed))
    spreads = {}
    factors = {'lambda_q1': 3.948, 'b1': 8.0, 'b2': 8.0, 'normf_g': 2.903}
    for name, (base, spread) in spreads.items():
        noise = np.random.default_rng([zlib.crc32(name.encode()), seed]).standard_normal(out[name].shape)
        drawn = base * np.exp(spread * noise) if base else spread * noise
        out[name] = jnp.asarray(drawn.astype(out[name].dtype))
    for name, factor in factors.items():
        out[name] = (out[name] * factor).astype(out[name].dtype)
    return out
```

```python
from contextlib import ExitStack

import numpy as np
import concourse.bass as bass
from concourse import mybir

ALU = mybir.AluOpType
ACT = mybir.ActivationFunctionType
F32 = mybir.dt.float32
F32R = mybir.dt.float32r
I32 = mybir.dt.int32
U32 = mybir.dt.uint32
AX = mybir.AxisListType.X

P = 128
D = 1024
SEQ = 512
NB = 8
NS = 4
NTOK = SEQ + NB * NS
TILES = [(0, 128), (128, 128), (256, 128), (384, 128), (512, 32)]
NT = len(TILES)
H = 4
HD = 64
PAST = 512
PAGES = 4
POOLW = 512
BUF = 15
NE = 32
TOPK = 4
KT = D // P
EPS = 1e-6
LAMBDA_INIT = 0.2
LIMIT = 7.0
ALPHA = 1.702
WINDOWS = (2, 4, 8, 16)
SLOPES = [2.0 ** (-8.0 * (h + 1) / H) for h in range(H)]
MASKED = 1e34
RAW, RING = 4, 4
CH = 2048
W1C, W2C = 8, 4
PER = W1C + W2C
PRO = 12
TABLE = NE + 3
SPARE = NE + 2
UNUSED = 65536.0

A_V, A_QT, A_KT, A_DIST = 0, 2560, 4736, 6912
A_KN, A_BAND, A_US = 8000, 10560, 12352
A_P, A_A, A_AT, A_ON, A_SQ = 8000, 10048, 11072, 12096, 12608
A_QB, A_S, A_PT, A_OTS = 8000, 9024, 10112, 10752
A_H, A_XG, A_OH = 0, 5120, 6144
A_ACT, A_G, A_SIG, A_L, A_Y, A_TMP = 7168, 8192, 9216, 10240, 11264, 12288
A_G2, A_H2T, A_H2, A_RW = 8192, 9216, 11264, 5120
A_RT, A_TRI = 5376, 5888
A_LAM, A_GSUB = 12864, 13120
ARENA = 13312
C_ID, C_IOTA = 0, 128
C_TOK = C_IOTA + 640
C_NEGM, C_M0, C_M1, C_SLOPE = C_TOK + 5, C_TOK + 6, C_TOK + 7, C_TOK + 8
C_EYE = C_TOK + 9
NCONST = C_EYE + NE


def constants():
    c = np.zeros((P, NCONST), np.float32)
    p = np.arange(P)
    c[:, C_ID:C_ID + P] = np.eye(P)
    c[:, C_IOTA:C_IOTA + 640] = np.arange(640)
    c[:, C_TOK:C_TOK + 5] = p[:, None] + P * np.arange(5)
    c[:, C_NEGM] = np.where(p >= NE, -1, 0)
    second = (p // NS) % 2
    c[:, C_M0], c[:, C_M1] = 1 - second, second
    c[:, C_SLOPE] = [-SLOPES[(i // 8) % H] for i in p]
    c[:, C_EYE:C_EYE + NE] = (p[:, None] % NE) == np.arange(NE)
    d = np.full((P, 512 + 576), MASKED, np.float32)
    dist = p[:, None] - np.arange(512)[None, :] + 384
    d[:, :512] = np.where(dist >= 0, dist, MASKED)
    q = p % NS
    d[:, 512:1024] = PAST + q[:, None] - np.arange(PAST)[None, :]
    for t in range(2):
        for i in range(P):
            b = 4 * t + i // 32
            for j in range(q[i] + 1):
                d[i, 1024 + 32 * t + NS * b + j] = q[i] - j
    band = np.zeros((P, 4, 3, P), np.float32)
    sband = np.zeros((P, 4, 2, 32), np.float32)
    t, s = np.arange(P)[None, :], p[:, None]
    for g, w in enumerate(WINDOWS):
        here = (t - s >= 0) & (t - s < w)
        band[:, g, 0] = here / np.minimum(w, t + 1.0) - (t == s)
        band[:, g, 1] = here / float(w) - (t == s)
        band[:, g, 2] = ((t + P - s) < w) / float(w)
        for b in range(NB):
            for n in range(NS):
                for j in range(BUF):
                    sband[b * BUF + j, g, 0, b * NS + n] = (BUF + n - j < w) / w
                for j in range(n + 1):
                    sband[b * NS + j, g, 1, b * NS + n] = (n - j < w) / w - (n == j)
    bands = np.concatenate([band.reshape(P, -1), sband.reshape(P, -1)], 1)
    tri = np.concatenate([p[:, None] < p[None, :], np.ones((P, P), bool)], 1).astype(np.float32)
    return {"c_misc": c, "c_dist": d, "c_band": bands, "c_tri": tri}


def units():
    out = []
    for c in range(8):
        if c in (2, 3):
            out += [(c, "q", hh, part) for hh in range(2) for part in range(2)]
        else:
            out += [(c, "u" if c < 2 else "k" if c < 6 else "v", t, 0) for t in range(NT)]
    return out


UNITS = units()
LAST_UNIT = [max(i for i, u in enumerate(UNITS) if u[0] == c) + 1 for c in range(8)]


def build(nc, a):
    x_in = [(a["x_prompt"].rearrange("b t d -> (b t) d"), 128 * t) for t in range(4)]
    x_in.append((a["x_sample"].rearrange("b t d -> (b t) d"), 0))
    w_in = a["w_in"][0].rearrange("(k p) n -> p k n", p=P)
    w_out = a["w_out"][0].rearrange("(k p) n -> p k n", p=P)
    h2_dram = nc.dram_tensor("h2_rows", [NTOK, D], F32).ap()
    y_dram = nc.dram_tensor("expert_rows", [NTOK * TOPK, D], F32).ap()

    with ExitStack() as ctx:
        def sb(name, shape, dt=F32):
            return ctx.enter_context(nc.sbuf_tensor(name, shape, dt))

        def sem(name):
            return ctx.enter_context(nc.semaphore(name))

        raw = sb("raw", [P, RAW, CH])
        hi = sb("hi", [P, RING, CH], F32R)
        lo = sb("lo", [P, RING, CH], F32R)
        t_hi = sb("t_hi", [P, KT, 640], F32R)
        t_lo = sb("t_lo", [P, KT, 640], F32R)
        ar = sb("arena", [P, ARENA])
        bias_r = sb("bias_r", [2 * NE, 3 * D], F32R)
        sel_w1 = sb("sel_w1", [2 * NE, P], F32R)
        sel_w2 = sb("sel_w2", [2 * NE, P], F32R)
        cst = sb("cst", [P, NCONST])
        st = sb("stats", [P, 64])
        psc = sb("psc", [P, 4])
        pt = sb("pt", [1, NB * PAGES], I32)
        top = sb("top", [P, 8])
        topi = sb("topi", [P, 8], U32)
        topf = sb("topf", [P, 4])
        gate = sb("gate", [P, NT, 4])
        rank = sb("rank", [P, NT, TABLE])
        vals = sb("vals", [P, NT, TABLE, 2])
        rank_c = sb("rank_c", [P, NT])
        vals_c = sb("vals_c", [P, NT, 2])
        unused = sb("unused", [P, 2])
        idx = sb("idx", [P, TABLE, 2], U32)
        idx_g = sb("idx_g", [P, 1], U32)
        idx_s = sb("idx_s", [P, 1], U32)
        cnt = sb("cnt", [1, NE + 8], I32)
        cntf = sb("cntf", [1, 8])
        ps = ctx.enter_context(nc.psum_tensor("ps", [P, 8, 512], F32))

        def A(at, *shape):
            n = int(np.prod(shape))
            v = ar[:, at:at + n]
            if len(shape) == 2:
                v = v.rearrange("p (a b) -> p a b", a=shape[0])
            if len(shape) == 3:
                v = v.rearrange("p (a b c) -> p a b c", a=shape[0], b=shape[1])
            return v

        ident = cst[:, C_ID:C_ID + P]
        lamv, gsub = A(A_LAM, 4 * HD), A(A_GSUB, P)
        slots = A(6784, P)
        rbias, lgt, sel, oh4, kv4 = A(A_RT, NE), A(A_RT + 32, NE), A(A_RT + 64, NT, NE), A(A_RT + 224, 4, NE), A(A_RT + 352, 4, NE)
        tri, ones = A(A_TRI, P), A(A_TRI + P, P)
        iota = cst[:, C_IOTA:C_IOTA + 640]
        v_nat, q_t, k_t = A(A_V, NT, 512), A(A_QT, H, NTOK), A(A_KT, H, NTOK)
        dist, dist_s = A(A_DIST, 512), A(A_DIST + 512, 576)
        k_nat, u_smp = A(A_KN, NT, 512), A(A_US, 512)
        u_nat = raw[:, 3, :].rearrange("p (t n) -> p t n", t=4)
        band = A(A_BAND, 4, 3, P)
        sband = A(A_BAND + 1536, 4, 2, 32)
        x_buf = raw[:, 1, :].rearrange("p (a n) -> p a n", a=2)
        xn, g1 = raw[:, 2, 0:D], raw[:, 2, D:2 * D]
        state, pw = raw[:, 1, 0:512], raw[:, 1, 512:1024].rearrange("p (g n) -> p g n", g=4)
        d_t = [raw[:, 1, 1024:1568], raw[:, 2, 0:544]]
        page = raw[:, 1:3, :].rearrange("p s (a n) -> p (s a) n", a=4)
        kt_s = raw[:, 3, 0:1536].rearrange("p (a n) -> p a n", a=3)
        pr = A(A_P, 4, 512)
        aa, at_sb = A(A_A, 2, 512), A(A_AT, 2, 512)
        o_nat, o_sq = A(A_ON, 512), A(A_SQ, 512)
        q_blk, s_smp, p_t, o_ts = A(A_QB, 32, 32), A(A_S, 2, 544), A(A_PT, 2, 5, 64), A(A_OTS, 128)
        h_res, xg, onehot = A(A_H, NT, D), A(A_XG, D), A(A_OH, NT, P)
        act, glu, sig, lin, y_sb, tmp = (A(v, D) for v in (A_ACT, A_G, A_SIG, A_L, A_Y, A_TMP))
        g2, h2_t, h2, rw = A(A_G2, D), A(A_H2T, 2, D), A(A_H2, 2, D), A(A_RW, KT, NE)
        junk = A(A_ACT, D)
        x_hi, x_lo = t_hi[:, :, 0:P], t_lo[:, :, 0:P]
        act_hi, act_lo = t_hi[:, :, P:2 * P], t_lo[:, :, P:2 * P]

        neglam = st[:, 0:1]

        s_x = [sem(f"x_loaded{i}") for i in range(2)]
        s_cst = sem("constants_loaded")
        s_g1 = sem("g1_loaded")
        s_late = sem("pool_inputs_loaded")
        s_raw = [sem(f"raw_loaded{i}") for i in range(RAW)]
        s_hi, s_lo = sem("hi_done"), sem("lo_done")
        s_pad, s_ss, s_rt, s_xn, s_tp = sem("pads_zeroed"), sem("squares_summed"), sem("root_done"), sem("xn_done"), sem("xn_transposed")
        s_th, s_tl = sem("xt_hi_done"), sem("xt_lo_done")
        s_dve, s_act_c, s_pool_c = sem("dve_chain"), sem("act_chain"), sem("pool_chain")
        s_bh, s_lam, s_lame = sem("bias_rounded"), sem("lambda_dots"), sem("lambda_exps")
        s_z, s_ze = sem("z_unit_done"), sem("z_unit_out")
        s_kt, s_kte = sem("k_transposed"), sem("kt_out")
        s_d, s_de, s_po, s_ph, s_pl = sem("pool_diff"), sem("pool_diff_out"), sem("pool_lin"), sem("pool_hi"), sem("pool_lo")
        s_sc, s_sb, s_mx, s_e = sem("scores_done"), sem("scores_biased"), sem("max_done"), sem("exp_done")
        s_a, s_atr, s_ate, s_pv = sem("weights_done"), sem("weights_transposed"), sem("weights_t_out"), sem("pv_done")
        s_os, s_or, s_on, s_ot, s_oh_, s_ol = (sem(n) for n in ("o_squares", "o_root", "o_normed", "o_transposed", "o_hi", "o_lo"))
        s_pg, s_vg = [sem(f"k_pages{i}") for i in range(2)], [sem(f"v_pages{i}") for i in range(2)]
        s_qb, s_kp, s_kc, s_sss = sem("q_blocks"), sem("page_transposed"), sem("page_t_out"), sem("sample_scores")
        s_smx, s_se, s_sa, s_ptr, s_pe = (sem(n) for n in ("sample_max", "sample_exp", "sample_weights", "sample_wt", "sample_wt_out"))
        s_vb, s_oe, s_o6 = sem("sample_pv"), sem("sample_ot_out"), sem("sample_o")
        s_xr, s_w, s_he = sem("x_reloaded"), sem("w_out_unit"), sem("h_unit")
        s_n2, s_r2, s_h2, s_h2d, s_h2t, s_h2e, s_lg, s_lge = (sem(n) for n in ("n2_squares", "n2_root", "h2_done", "h2_stored", "h2_transposed", "h2t_out", "router_done", "logits_out"))
        s_gm, s_ge, s_sel, s_rk, s_tab = sem("gate_max"), sem("gate_exp"), sem("selected"), sem("ranks"), sem("tables_done")
        s_late2 = sem("router_inputs_loaded")
        s_ohd, s_ix, s_ixe, s_gat = sem("onehot_done"), sem("index_product"), sem("index_out"), sem("rows_gathered")
        s_xt, s_xh, s_xl = sem("rows_transposed"), sem("rows_hi"), sem("rows_lo")
        s_bs = sem("bias_selector")
        s_pc = sem("chunk_multiplied")
        s_g, s_s, s_l, s_t, s_ac = sem("glu_clamped"), sem("sigmoid_done"), sem("lin_clamped"), sem("gated"), sem("act_done")
        s_at, s_ah, s_al = sem("act_transposed"), sem("act_hi_done"), sem("act_lo_done")
        s_ye, s_sca = sem("y_out"), sem("rows_scattered")
        s_fy = [sem(f"choices_loaded{i}") for i in range(2)]
        s_gf, s_fs, s_fr, s_fo = sem("gf_loaded"), sem("final_squares"), sem("final_root"), sem("final_done")
        s_out, s_outp, s_ust = sem("outputs_stored"), sem("caches_stored"), sem("u_stored")
        s_fc = sem("final_chain")
        s_carry = sem("carries_waits")

        block = ctx.enter_context(nc.Block())

        def first(m):
            return PRO + W1C + PER * (m - 1)

        def second(m):
            return PRO + W1C + PER * m + W1C

        EXTRA = PRO + PER * NE
        assert EXTRA % RAW == 0 and EXTRA % RING == 0 and PRO % RAW == 0

        def slot_count(g, off):
            return g * 2, off

        class Chunks:

            def __init__(self, base, step):
                self.base, self.step = base, step

            def raw_slot(self, j):
                return (self.base + j) % RAW

            def slot(self, j):
                return (self.base + j) % RING

            def number(self, j):
                return self.step * PER + (self.base + j)

            def loaded(self, j):
                before = PRO if self.raw_slot(j) == 0 else 0
                return self.step * (16 * PER // RAW) + 16 * (before + (self.base + j - PRO) // RAW + 1)

        def further_blocks(eng, body):
            most = eng.value_load(cnt[0:1, NE:NE + 1], min_val=0, max_val=NTOK)
            with eng.If(most > P):
                ran = eng.alloc_register("blocks_ran")
                eng.reg_mov(ran, 0)
                with eng.Fori(0, NE) as e:
                    many = eng.value_load(cnt[0:1, bass.ds(e, 1)], min_val=0, max_val=NTOK)
                    with eng.Fori(0, 4) as r:
                        with eng.If(many > r * P + P):
                            body(e, r, eng.snap(ran, min_val=0, max_val=NTOK * TOPK // P))
                            eng.reg_add(ran, ran, 1)
                        eng.nop()

        @block.sync
        def _(sp):
            def load_x(t):
                src, r = x_in[t]
                n = TILES[t][1]
                if t >= 2:
                    sp.wait_ge(s_xn, t - 1)
                sp.dma_start(x_buf[0:n, t % 2, :], src[r:r + n, :]).then_inc(s_x[t % 2], 16)

            def load_pro(g):
                if g:
                    sp.wait_ge(s_lo, g)
                src = w_in[:, :, 256 * g:256 * g + 256] if g < 8 else w_out[:, :, 256 * (g - 8):256 * (g - 8) + 256]
                sp.dma_start(raw[:, 0, :].rearrange("p (k n) -> p k n", k=KT), src).then_inc(s_raw[0], 16)

            load_x(0)
            sp.dma_start(g1, a["norm1_g"].to_broadcast([P, D])).then_inc(s_g1, 16)
            load_x(1)
            sp.dma_start(cst[:], a["c_misc"]).then_inc(s_g1, 16)
            load_pro(0)
            load_x(2)
            for half in range(2):
                rows = slice(NE * half, NE * half + NE)
                sp.dma_start(ar[rows, 0:2 * D], a["b1"][0]).then_inc(s_cst, 16)
                sp.dma_start(ar[rows, 2 * D:3 * D], a["b2"][0]).then_inc(s_cst, 16)
            for i, n in enumerate(("lambda_q1", "lambda_k1", "lambda_q2", "lambda_k2")):
                sp.dma_start(lamv[:, i * HD:(i + 1) * HD], a[n].to_broadcast([P, HD])).then_inc(s_cst, 16)
            sp.dma_start(gsub, a["subln_g"].to_broadcast([P, P])).then_inc(s_cst, 16)
            with nc.allow_non_contiguous_dma("512 words"):
                sp.dma_start(psc[:], a["pool_scale"][0].rearrange("(g p) -> p g", p=P)).then_inc(s_cst, 16)
            sp.dma_start(pt[:], a["page_table"].rearrange("b n -> (b n)").rearrange("(a n) -> a n", a=1)).then_inc(s_cst, 16)
            sp.dma_start(ar[:, A_DIST:A_DIST + 1088], a["c_dist"]).then_inc(s_cst, 16)
            sp.dma_start(ar[:, A_BAND:A_BAND + 1792], a["c_band"]).then_inc(s_cst, 16)
            load_pro(1)
            load_x(3)
            load_pro(2)
            load_x(4)
            sp.wait_ge(s_xn, NT)
            sp.dma_start(state[0:NB * BUF, :], a["state_pool"][0].rearrange("b t n -> (b t) n")).then_inc(s_late, 16)
            sp.dma_start(pw, a["pool_w"][0].rearrange("g c e -> c g e")).then_inc(s_late, 16)
            for g in range(3, PRO):
                load_pro(g)

            sp.wait_ge(s_po, 4)
            sp.wait_ge(s_ust, 32)
            sp.wait_ge(s_cst, 16 * 13)

            def load_pages(cache, b, parity, signal):
                for n in range(PAGES):
                    pg = sp.value_load(pt[0:1, bass.ds(b * PAGES + n, 1)], min_val=0, max_val=a[cache].shape[1] - 1)
                    sp.dma_start(page[:, PAGES * parity + n, :],
                                 a[cache][0][bass.ds(pg, 1)].rearrange("a t h d -> (a t) (h d)")).then_inc(signal, 16)

            for b in range(2):
                load_pages("cache_k", b, b, s_pg[b])
            with sp.Fori(1, NB // 2) as bb:
                for b in range(2):
                    sp.wait_ge(s_kp, bb * 8 + (H * (b + 1) - 8))
                    load_pages("cache_k", bb * 2 + b, b, s_pg[b])
            for b in range(2):
                sp.wait_ge(s_kp, H * (NB - 1 + b))
                load_pages("cache_v", b, b, s_vg[b])
            with sp.Fori(1, NB // 2) as bb:
                for b in range(2):
                    sp.wait_ge(s_vb, bb * 2 + (b - 1))
                    load_pages("cache_v", bb * 2 + b, b, s_vg[b])

            sp.wait_ge(s_ol, NT)
            for t in range(NT):
                src, r = x_in[t]
                n = TILES[t][1]
                sp.dma_start(h_res[0:n, t, :], src[r:r + n, :]).then_inc(s_xr, 16)
            sp.dma_start(g2, a["norm2_g"].to_broadcast([P, D])).then_inc(s_late2, 16)
            sp.dma_start(rbias, a["router_b"].to_broadcast([P, NE])).then_inc(s_late2, 16)
            sp.dma_start(ar[:, A_TRI:A_TRI + 2 * P], a["c_tri"]).then_inc(s_late2, 16)
            sp.dma_start(rw, a["router_w"][0].rearrange("(k p) e -> p k e", p=P)).then_inc(s_late2, 16)

            def load_expert(ck, j, e, k, second_half):
                if second_half:
                    src = a["w2"][0][bass.ds(e, 1), 256 * k:256 * k + 256, :].rearrange("a (k p) n -> p (a k) n", p=P)
                    dst = raw[:, ck.raw_slot(j), :].rearrange("p (k n) -> p k n", k=2)
                else:
                    src = a["w1"][0][bass.ds(e, 1), P * k:P * k + P, :].rearrange("a p n -> (a p) n")
                    dst = raw[:, ck.raw_slot(j), :]
                return sp.dma_start(dst, src).then_inc(s_raw[ck.raw_slot(j)], 16)

            start = Chunks(PRO, 0)
            for j in range(W1C):
                if j >= RAW:
                    sp.wait_ge(s_lo, PRO + j - RAW + 1)
                load_expert(start, j, 0, j, False)

            def body_loads(n):
                ck = Chunks(PRO + W1C, n)
                for j in range(PER):
                    sp.wait_ge(s_lo, ck.number(j) - RAW + 1)
                    if j < W1C:
                        load_expert(ck, j, n + 1, j, False)
                    else:
                        load_expert(ck, j, n, j - W1C, True)

            body_loads(0)
            with sp.Fori(1, NE - 1) as n:
                body_loads(n)
            tail = Chunks(PRO + W1C + PER * (NE - 1), 0)
            for j in range(W2C):
                sp.wait_ge(s_lo, tail.number(j) - RAW + 1)
                load_expert(tail, j, NE - 1, j, True)

            sp.wait_ge(s_tab, 3)
            def further(e, r, i):
                ck = Chunks(EXTRA, i)
                for j in range(PER):
                    sp.wait_ge(s_lo, ck.number(j) - RAW + 1)
                    load_expert(ck, j, e, j % W1C, j >= W1C)
                sp.wait_ge(s_sca, i * 16 + 16 * (NE + 1))
                sp.sem_inc(s_carry, 1)

            further_blocks(sp, further)
            sp.wait_ge(s_pc, PER * NE)
            sp.wait_ge(s_gat, 16 * (NE + 2))
            sp.wait_ge(s_sca, 16 * NE)
            sp.dma_start(raw[:, 3, 0:D], a["normf_g"].rearrange("(a n) -> a n", a=1).to_broadcast([P, D])).then_inc(s_gf, 16)
            y_rows = y_dram.rearrange("(t k) d -> t (k d)", k=TOPK)
            for t, (r, n) in enumerate(TILES):
                if t >= 2:
                    sp.wait_ge(s_fo, t - 1)
                sp.dma_start(ar[0:n, 5120 + 4096 * (t % 2):5120 + 4096 * (t % 2) + 4096], y_rows[r:r + n, :]).then_inc(s_fy[t % 2], 16)
            y_out = [(a["y_prompt"].rearrange("b t d -> (b t) d"), 128 * t) for t in range(4)] + [(a["y_sample"].rearrange("b t d -> (b t) d"), 0)]
            for t, (r, n) in enumerate(TILES):
                sp.wait_ge(s_fo, t + 1)
                dst, o = y_out[t]
                sp.dma_start(dst[o:o + n, :], raw[0:n, t // 2, D * (t % 2):D * (t % 2) + D]).then_inc(s_out, 16)
            sp.wait_ge(s_out, 16 * NT)
            sp.wait_ge(s_outp, 16 * 5)

        @block.gpsimd
        def _(pool):
            pool.memset(t_hi[:, :, NTOK:640].bitcast(F32), 0.0)
            pool.memset(t_lo[:, :, NTOK:640].bitcast(F32), 0.0)
            pool.memset(gate[:], 0.0)
            pool.memset(rank[:], -1.0)
            pool.memset(vals[:], 0.0).then_inc(s_pad, 1)

            pool.wait_ge(s_ze, LAST_UNIT[1])
            pool.dma_start(a["new_pool_prompt"][0, 0], u_nat[P - BUF:P, 3, :]).then_inc(s_ust, 16)
            pool.dma_start(a["new_pool_sample"][0, :, BUF - NS:BUF, :], u_smp[0:32, :]).then_inc(s_ust, 16)
            pool.dma_start(a["new_pool_sample"][0, :, 0:BUF - NS, :], a["state_pool"][0, :, NS:BUF, :]).then_inc(s_outp, 16)

            def store(nat, prompt, sample):
                pool.dma_start(a[prompt][0, 0].rearrange("(t p) h d -> p t (h d)", p=P), nat[:, 0:4, :]).then_inc(s_outp, 16)
                pool.dma_start(a[sample][0].rearrange("b t h d -> (b t) (h d)"), nat[0:32, 4, :]).then_inc(s_outp, 16)

            pool.wait_ge(s_ze, LAST_UNIT[5])
            store(k_nat, "new_k_prompt", "new_k_sample")
            pool.wait_ge(s_ze, LAST_UNIT[7])
            store(v_nat, "new_v_prompt", "new_v_sample")
            pool.wait_ge(s_a, 16)
            pool.wait_ge(s_pv, 16)
            pool.wait_ge(s_ate, 16)
            pool.wait_ge(s_outp, 16 * 5)
            pool.memset(q_blk, 0.0).then_inc(s_qb, 1)

            for t, (r, n) in enumerate(TILES):
                pool.wait_ge(s_h2, t + 1)
                if t:
                    pool.wait_ge(s_h2d, 16 * t)
                pool.dma_start(h2_dram[r:r + n, :], h2[0:n, t % 2, :]).then_inc(s_h2d, 16)
            pool.wait_ge(s_lge, NT)
            pool.wait_ge(s_tab, 3)
            pool.memset(xg, 0.0).then_inc(s_pool_c, 1)
            pool.wait_ge(s_pool_c, 1)
            pool.wait_ge(s_h2d, 16 * NT)

            def alone():
                pool.sem_inc(s_carry, 1)

            def make_onehot(m, column, rows, chain):
                if not isinstance(m, int) or m > 0:
                    pool.wait_ge(s_ix, m)
                alone()
                pool.tensor_copy(rank_c[:], rank[:, :, bass.ds(column, 1)].rearrange("p t a -> p (t a)")).then_inc(s_pool_c, 1)
                pool.tensor_copy(vals_c[:], vals[:, :, bass.ds(column, 1), :].rearrange("p t a b -> p t (a b)")).then_inc(s_pool_c, 1)
                pool.wait_ge(s_pool_c, chain + 2)
                alone()
                for t in range(NT):
                    last = pool.tensor_scalar(onehot[:, t, :], rows, rank_c[:, t:t + 1], None, ALU.is_equal)
                last.then_inc(s_ohd, 1)

            def gather(m, column, chain, before):
                pool.wait_ge(s_ixe, m + 1)
                if not isinstance(m, int) or m > 0:
                    pool.wait_ge(s_xt, before)
                    pool.wait_ge(s_gat, m * 16)
                alone()
                pool.tensor_copy(idx_g[:], idx[:, bass.ds(column, 1), 0]).then_inc(s_pool_c, 1)
                pool.wait_ge(s_pool_c, chain + 3)
                alone()
                pool.indirect_dma_start(out=xg, out_offset=None, in_=h2_dram,
                                        in_offset=bass.IndirectOffsetOnAxis(ap=idx_g[:, 0:1], axis=0),
                                        bounds_check=NTOK - 1, oob_is_err=False).then_inc(s_gat, 16)

            def gated(m, half):
                cols = slice(512 * half, 512 * half + 512)
                pool.wait_ge(s_l, m * 2 + (half + 1))
                alone()
                pool.tensor_scalar(lin[:, cols], lin[:, cols], 1.0, None, ALU.add).then_inc(s_t, 1)
                pool.wait_ge(s_s, m * 2 + (half + 1))
                pool.tensor_tensor(tmp[:, cols], glu[:, cols], sig[:, cols], ALU.mult).then_inc(s_t, 1)
                pool.wait_ge(s_t, m * 4 + (2 * half + 2))
                if not isinstance(m, int) or m > 0:
                    pool.wait_ge(s_at, m)
                pool.tensor_tensor(act[:, cols], tmp[:, cols], lin[:, cols], ALU.mult).then_inc(s_ac, 1)

            def scatter(m, column, chain):
                if not isinstance(m, int) or m > 0:
                    pool.wait_ge(s_sca, m * 16)
                alone()
                pool.tensor_copy(idx_s[:], idx[:, bass.ds(column, 1), 1]).then_inc(s_pool_c, 1)
                pool.wait_ge(s_pool_c, chain + 1)
                pool.wait_ge(s_ye, m + 1)
                alone()
                pool.indirect_dma_start(out=y_dram, out_offset=bass.IndirectOffsetOnAxis(ap=idx_s[:, 0:1], axis=0),
                                        in_=y_sb, in_offset=None,
                                        bounds_check=NTOK * TOPK - 1, oob_is_err=False).then_inc(s_sca, 16)

            for m in range(3):
                make_onehot(m, m, iota[:, 0:P], 1 + 3 * m)
                if m == 2:
                    gated(0, 0)
                    gated(0, 1)
                gather(m, m, 1 + 3 * m, m)
            make_onehot(3, 3, iota[:, 0:P], 10)
            gather(3, 3, 10, 3)
            gated(1, 0)
            gated(1, 1)
            with pool.Fori(1, NE - 1) as n:
                scatter(n - 1, n - 1, n * 4 + 9)
                make_onehot(n + 3, n + 3, iota[:, 0:P], n * 4 + 10)
                gather(n + 3, n + 3, n * 4 + 10, n + 3)
                gated(n + 1, 0)
                gated(n + 1, 1)
            scatter(NE - 2, NE - 2, 4 * NE + 5)
            scatter(NE - 1, NE - 1, 4 * NE + 6)

            def further(e, r, i):
                chain = i * 5 + (4 * NE + 8)
                pool.wait_ge(s_ix, i + (NE + 2))
                alone()
                pool.tensor_copy(slots, iota[:, bass.ds(r * P + P, P)]).then_inc(s_pool_c, 1)
                make_onehot(i + (NE + 2), e, slots, chain)
                gather(i + (NE + 2), SPARE, chain, i + (NE + 1))
                for half in range(2):
                    gated(i + NE, half)
                scatter(i + NE, SPARE, chain + 3)
                pool.wait_ge(s_sca, i * 16 + 16 * (NE + 1))
                pool.sem_inc(s_carry, 1)

            further_blocks(pool, further)

        @block.scalar
        def _(act_e):
            def gate_exp(t):
                n = TILES[t][1]
                act_e.wait_ge(s_gm, t + 1)
                act_e.activation(gate[0:n, t, :], top[0:n, 0:4], ACT.Exp, bias=st[0:n, 44:45], accum_out=st[0:n, 45:46]).then_inc(s_ge, 1)

            def split_hi(slot_raw, slot, loaded):
                act_e.wait_ge(s_raw[slot_raw], loaded)
                act_e.activation(hi[:, slot, :], raw[:, slot_raw, :], ACT.Copy).then_inc(s_hi, 1)

            def pro_hi(g):
                if g >= RING:
                    act_e.wait_ge(s_z, LAST_UNIT[g - RING])
                split_hi(0, g % RING, 16 * (g + 1))

            for t, (_, n) in enumerate(TILES):
                act_e.wait_ge(s_x[t % 2], 16 * (t // 2 + 1))
                if t >= 1:
                    act_e.wait_ge(s_tp, t)
                act_e.activation(xn[0:n, :], x_buf[0:n, t % 2, :], ACT.Square, accum_out=st[0:n, 2 + t:3 + t]).then_inc(s_ss, 1)
                act_e.wait_ge(s_dve, 2 * t + 1)
                act_e.activation(st[0:n, 8 + t:9 + t], st[0:n, 8 + t:9 + t], ACT.Sqrt).then_inc(s_rt, 1)
                act_e.wait_ge(s_tp, t + 1)
                if t == 0:
                    act_e.wait_ge(s_pad, 1)
                src = ps[:, 2 * (t % 2):2 * (t % 2) + 2, :].rearrange("p b (k c) -> p (b k) c", c=P)[:, :, 0:n]
                act_e.activation(t_hi[:, :, P * t:P * t + n], src, ACT.Copy).then_inc(s_th, 1)
                if t < 3:
                    pro_hi(t)
            pro_hi(3)
            act_e.wait_ge(s_cst, 16 * 13)
            act_e.activation(bias_r[:], ar[0:2 * NE, 0:3 * D], ACT.Copy).then_inc(s_bh, 1)
            act_e.wait_ge(s_lam, 1)
            act_e.activation(st[:, 16:18], st[:, 14:16], ACT.Exp).then_inc(s_lame, 1)
            act_e.wait_ge(s_bh, 2)
            for i, (c, kind, t, part) in enumerate(UNITS):
                act_e.wait_ge(s_z, i + 1)
                bank = 4 + i % 4
                if kind == "q":
                    h = 2 * (c - 2) + t
                    n = 512 if part == 0 else 32
                    act_e.activation(q_t[:, h, 512 * part:512 * part + n], ps[:, bank, 0:n], ACT.Copy, scale=HD ** -0.5).then_inc(s_ze, 1)
                else:
                    n = TILES[t][1]
                    col = 256 * (c % 2)
                    dst = {"u": u_nat, "k": k_nat, "v": v_nat}[kind]
                    dst = u_smp[0:n, col:col + 256] if kind == "u" and t == 4 else dst[0:n, t, col:col + 256]
                    act_e.activation(dst, ps[0:n, bank, 0:256], ACT.Copy).then_inc(s_ze, 1)
                if i + 1 in LAST_UNIT:
                    pro_hi(LAST_UNIT.index(i + 1) + RING)
            def pool_diff(g):
                act_e.wait_ge(s_d, g + 1)
                if g >= 2:
                    act_e.wait_ge(s_po, g - 1)
                act_e.activation(d_t[g % 2][:, 0:512], ps[:, 2 * (g % 2), :], ACT.Copy)
                act_e.activation(d_t[g % 2][:, 512:544], ps[:, 2 * (g % 2) + 1, 0:32], ACT.Copy).then_inc(s_de, 1)

            def pool_hi(g):
                act_e.wait_ge(s_po, g + 1)
                b = 4 + 2 * (g % 2)
                act_e.activation(t_hi[:, g, 0:512], ps[:, b, :], ACT.Copy, scale=psc[:, g:g + 1])
                act_e.activation(t_hi[:, g, 512:544], ps[:, b + 1, 0:32], ACT.Copy, scale=psc[:, g:g + 1]).then_inc(s_ph, 1)

            act_e.wait_ge(s_late, 32)
            for g in range(4):
                pool_diff(g)
                if g >= 1:
                    pool_hi(g - 1)
            pool_hi(3)

            def o_root(i, n):
                act_e.wait_ge(s_os, i + 1)
                act_e.activation(st[0:n, 28:32], st[0:n, 28:32], ACT.Sqrt).then_inc(s_or, 1)

            def o_hi(i, n):
                act_e.wait_ge(s_ot, i + 1)
                src = ps[:, 7, :].rearrange("p (h c) -> p h c", c=P)[:, :, 0:n]
                act_e.activation(t_hi[:, 4:8, P * i:P * i + n], src, ACT.Copy).then_inc(s_oh_, 1)

            def weights_t(i):
                nk = P * (i // 4 + 1)
                act_e.wait_ge(s_atr, i + 1)
                if i >= 2:
                    act_e.wait_ge(s_pv, i - 1)
                act_e.activation(at_sb[:, i % 2, 0:nk], ps[:, 4 + i % 2, 0:nk], ACT.Copy).then_inc(s_ate, 1)

            for i in range(17):
                if i < 16:
                    nk = P * (i // 4 + 1)
                    act_e.wait_ge(s_mx, i + 1)
                    for c in range(2):
                        w = pr[:, 2 * (i % 2) + c, 0:nk]
                        e = act_e.activation(w, w, ACT.Exp, bias=st[:, 20 + 2 * (i % 2) + c:21 + 2 * (i % 2) + c],
                                             accum_out=st[:, 24 + 2 * (i % 2) + c:25 + 2 * (i % 2) + c])
                    e.then_inc(s_e, 1)
                if i >= 1:
                    weights_t(i - 1)
                    if i >= 5 and i % 4 == 1:
                        o_hi(i // 4 - 1, P)
                    if i % 4 == 0:
                        o_root(i // 4 - 1, P)
            o_hi(3, P)
            act_e.wait_ge(s_ust, 32)
            for m in range(NB * H):
                act_e.wait_ge(s_kp, m + 1)
                if m >= 3:
                    act_e.wait_ge(s_sss, m - 2)
                act_e.activation(kt_s[:, m % 3, :], ps[:, m % 3, :], ACT.Copy).then_inc(s_kc, 1)
            for t in range(2):
                act_e.wait_ge(s_smx, t + 1)
                act_e.activation(s_smp[:, t, :], s_smp[:, t, :], ACT.Exp, bias=st[:, 32 + t:33 + t], accum_out=st[:, 34 + t:35 + t]).then_inc(s_se, 1)
            act_e.wait_ge(s_vb, NB)
            act_e.activation(o_ts, ps[:, 7, 0:P], ACT.Copy).then_inc(s_oe, 1)
            o_root(4, 32)
            o_hi(4, 32)
            start = Chunks(PRO, 0)
            for t, (_, n) in enumerate(TILES):
                act_e.wait_ge(s_he, 15 + t + 1)
                act_e.activation(junk[0:n, :], h_res[0:n, t, :], ACT.Square, accum_out=st[0:n, 36 + t:37 + t]).then_inc(s_n2, 1)
                act_e.wait_ge(s_n2, t + 1)
            for t, (_, n) in enumerate(TILES):
                act_e.wait_ge(s_r2, t + 1)
                act_e.activation(st[0:n, 36 + t:37 + t], st[0:n, 36 + t:37 + t], ACT.Sqrt).then_inc(s_act_c, 1)
            for t, (_, n) in enumerate(TILES):
                act_e.wait_ge(s_h2t, t + 1)
                if t >= 2:
                    act_e.wait_ge(s_lg, t - 1)
                src = ps[:, 4 + 2 * (t % 2):6 + 2 * (t % 2), :].rearrange("p b (k c) -> p (b k) c", c=P)[:, :, 0:n]
                act_e.activation(h2_t[:, t % 2, :].rearrange("p (k c) -> p k c", c=P)[:, :, 0:n], src, ACT.Copy).then_inc(s_h2e, 1)
                if t >= 1:
                    gate_exp(t - 1)
            gate_exp(4)

            def expert_hi(ck, j):
                act_e.wait_ge(s_pc, ck.number(j) - PRO - RING + 1)
                split_hi(ck.raw_slot(j), ck.slot(j), ck.loaded(j))

            def rows_hi(m, src_sem, done, dst):
                act_e.wait_ge(src_sem, m + 1)
                src = ps[:, 6:8, :].rearrange("p b (k c) -> p (b k) c", c=P)
                act_e.activation(dst, src, ACT.Copy).then_inc(done, 1)

            def selector(dst, e):
                return act_e.activation(dst[:], cst[0:2 * NE, bass.ds(C_EYE + e, 1)].to_broadcast([2 * NE, P]), ACT.Copy)

            def sigmoid(m, half):
                cols = slice(512 * half, 512 * half + 512)
                act_e.wait_ge(s_g, m * 2 + (half + 1))
                if not isinstance(m, int) or m > 0:
                    act_e.wait_ge(s_ac, m * 2)
                act_e.activation(sig[:, cols], glu[:, cols], ACT.Sigmoid, scale=ALPHA).then_inc(s_s, 1)

            def y_out(m, done):
                act_e.wait_ge(s_pc, done)
                if not isinstance(m, int) or m > 0:
                    act_e.wait_ge(s_sca, m * 16)
                act_e.activation(y_sb, ps[:, 4:6, :].rearrange("p b n -> p (b n)"), ACT.Copy).then_inc(s_ye, 1)

            act_e.wait_ge(s_w, 20)
            for j in range(RING):
                split_hi(start.raw_slot(j), start.slot(j), start.loaded(j))
            rows_hi(0, s_xt, s_xh, x_hi)
            selector(sel_w1, 0).then_inc(s_bs, 1)
            for j in range(RING, W1C):
                expert_hi(start, j)
            head = Chunks(PRO + W1C, 0)
            for j in range(4):
                expert_hi(head, j)
            act_e.wait_ge(s_pc, W1C)
            rows_hi(1, s_xt, s_xh, x_hi)
            sigmoid(0, 0)
            sigmoid(0, 1)

            def body(n, j0=0):
                ck = Chunks(PRO + W1C, n)
                for j in range(j0, 4):
                    expert_hi(ck, j)
                    if j == 2 and not (isinstance(n, int) and n == 0):
                        y_out(n - 1, ck.number(0) - PRO)
                rows_hi(n, s_at, s_ah, act_hi)
                selector(sel_w1, n + 1)
                selector(sel_w2, n).then_inc(s_bs, 1)
                for j in range(4, PER):
                    expert_hi(ck, j)
                act_e.wait_ge(s_pc, ck.number(W1C) - PRO)
                rows_hi(n + 2, s_xt, s_xh, x_hi)
                sigmoid(n + 1, 0)
                sigmoid(n + 1, 1)

            body(0, 4)
            with act_e.Fori(1, NE - 1) as n:
                body(n)
            tail = Chunks(PRO + W1C + PER * (NE - 1), 0)
            for j in range(3):
                expert_hi(tail, j)
            y_out(NE - 2, tail.number(0) - PRO)
            rows_hi(NE - 1, s_at, s_ah, act_hi)
            selector(sel_w2, NE - 1).then_inc(s_bs, 1)
            expert_hi(tail, 3)
            y_out(NE - 1, PER * NE)

            act_e.wait_ge(s_tab, 3)
            def further(e, r, i):
                ck = Chunks(EXTRA, i)
                rows_hi(i + (NE + 1), s_xt, s_xh, x_hi)
                selector(sel_w1, e)
                selector(sel_w2, e).then_inc(s_bs, 1)
                for j in range(W1C):
                    expert_hi(ck, j)
                sigmoid(i + NE, 0)
                sigmoid(i + NE, 1)
                rows_hi(i + NE, s_at, s_ah, act_hi)
                for j in range(W1C, PER):
                    expert_hi(ck, j)
                y_out(i + NE, ck.number(PER) - PRO)
                act_e.wait_ge(s_sca, i * 16 + 16 * (NE + 1))
                act_e.sem_inc(s_carry, 1)

            further_blocks(act_e, further)
            for t, (_, n) in enumerate(TILES):
                act_e.wait_ge(s_fs, 2 * t + 1)
                act_e.activation(raw[0:n, 3, D:2 * D], h_res[0:n, t, :], ACT.Square, accum_out=st[0:n, 50 + t:51 + t]).then_inc(s_fr, 1)
                act_e.wait_ge(s_fs, 2 * t + 2)
                act_e.activation(st[0:n, 50 + t:51 + t], st[0:n, 50 + t:51 + t], ACT.Sqrt).then_inc(s_fr, 1)

        @block.vector
        def _(v):
            chain = [0]

            def link(ins):
                chain[0] += 1
                ins.then_inc(s_dve, 1)
                v.wait_ge(s_dve, chain[0])

            def split_lo(slot_raw, slot, hi_done):
                v.wait_ge(s_hi, hi_done)
                v.tensor_tensor(lo[:, slot, :], raw[:, slot_raw, :], hi[:, slot, :].bitcast(F32), ALU.subtract).then_inc(s_lo, 1)

            def pro_lo(g):
                split_lo(0, g % RING, g + 1)

            v.wait_ge(s_g1, 32)
            for t, (_, n) in enumerate(TILES):
                v.wait_ge(s_ss, t + 1)
                link(v.tensor_scalar(st[0:n, 8 + t:9 + t], st[0:n, 2 + t:3 + t], 1.0 / D, EPS, ALU.mult, ALU.add))
                v.wait_ge(s_rt, t + 1)
                link(v.reciprocal(st[0:n, 2 + t:3 + t], st[0:n, 8 + t:9 + t]))
                v.scalar_tensor_tensor(out=xn[0:n, :], in0=x_buf[0:n, t % 2, :], scalar=st[0:n, 2 + t:3 + t], in1=g1[0:n, :],
                                       op0=ALU.mult, op1=ALU.mult).then_inc(s_xn, 1)
                v.wait_ge(s_th, t + 1)
                src = ps[:, 2 * (t % 2):2 * (t % 2) + 2, :].rearrange("p b (k c) -> p (b k) c", c=P)[:, :, 0:n]
                v.tensor_tensor(t_lo[:, :, P * t:P * t + n], src, t_hi[:, :, P * t:P * t + n].bitcast(F32), ALU.subtract).then_inc(s_tl, 1)
                if t < 3:
                    pro_lo(t)
            pro_lo(3)
            v.wait_ge(s_cst, 16 * 13)
            v.wait_ge(s_bh, 1)
            v.scalar_tensor_tensor(out=bias_r[:], in0=bias_r[:].bitcast(F32), scalar=cst[0:2 * NE, C_NEGM:C_NEGM + 1],
                                   in1=ar[0:2 * NE, 0:3 * D], op0=ALU.mult, op1=ALU.add).then_inc(s_bh, 1)
            lv = lamv.rearrange("p (a b n) -> p a b n", a=2, b=2)
            link(v.tensor_tensor(lv[:, :, 0, :], lv[:, :, 0, :], lv[:, :, 1, :], ALU.mult))
            v.tensor_reduce(st[:, 14:16], lv[:, :, 0, :], AX, ALU.add).then_inc(s_lam, 1)
            v.wait_ge(s_lame, 1)
            link(v.tensor_tensor(neglam, st[:, 17:18], st[:, 16:17], ALU.subtract))
            link(v.tensor_scalar(neglam, neglam, LAMBDA_INIT, None, ALU.subtract))
            link(v.tensor_scalar(st[:, 18:19], cst[:, C_M1:C_M1 + 1], neglam, cst[:, C_M0:C_M0 + 1], ALU.mult, ALU.add))
            link(v.tensor_scalar(gsub, gsub, 1.0 - LAMBDA_INIT, None, ALU.mult))

            def k_out(hp):
                v.wait_ge(s_kt, hp + 1)
                for hh in range(2):
                    v.tensor_copy(k_t[:, 2 * hp + hh, 0:512], ps[:, 2 * hh, :])
                    last = v.tensor_copy(k_t[:, 2 * hp + hh, 512:544], ps[:, 2 * hh + 1, 0:32])
                last.then_inc(s_kte, 1)

            for g in range(RING, 10):
                pro_lo(g)
            k_out(0)
            pro_lo(10)
            k_out(1)
            pro_lo(11)

            for g in range(4):
                v.wait_ge(s_ph, g + 1)
                b = 4 + 2 * (g % 2)
                v.scalar_tensor_tensor(out=t_lo[:, g, 0:512], in0=ps[:, b, :], scalar=psc[:, g:g + 1],
                                       in1=t_hi[:, g, 0:512].bitcast(F32), op0=ALU.mult, op1=ALU.subtract)
                v.scalar_tensor_tensor(out=t_lo[:, g, 512:544], in0=ps[:, b + 1, 0:32], scalar=psc[:, g:g + 1],
                                       in1=t_hi[:, g, 512:544].bitcast(F32), op0=ALU.mult, op1=ALU.subtract).then_inc(s_pl, 1)

            def o_norm(i, n):
                src = ps[0:n, 6, :].rearrange("p (h c) -> p h c", c=P)
                ov = o_nat[0:n].rearrange("p (h c) -> p h c", c=P)
                if i > 0:
                    v.wait_ge(s_ot, i)
                link(v.tensor_copy(o_nat[0:n], ps[0:n, 6, :]))
                link(v.tensor_tensor(o_sq[0:n], o_nat[0:n], o_nat[0:n], ALU.mult))
                link(v.tensor_reduce(st[0:n, 28:32], o_sq[0:n].rearrange("p (h c) -> p h c", c=P), AX, ALU.add))
                v.tensor_scalar(st[0:n, 28:32], st[0:n, 28:32], 1.0 / P, EPS, ALU.mult, ALU.add).then_inc(s_os, 1)
                v.wait_ge(s_or, i + 1)
                link(v.reciprocal(st[0:n, 28:32], st[0:n, 28:32]))
                link(v.tensor_tensor(ov, src, st[0:n, 28:32].unsqueeze(2).to_broadcast([n, 4, P]), ALU.mult))
                v.tensor_tensor(ov, ov, gsub[0:n].unsqueeze(1).to_broadcast([n, 4, P]), ALU.mult).then_inc(s_on, 1)

            def o_lo(i, n):
                v.wait_ge(s_oh_, i + 1)
                src = ps[:, 7, :].rearrange("p (h c) -> p h c", c=P)[:, :, 0:n]
                v.tensor_tensor(t_lo[:, 4:8, P * i:P * i + n], src, t_hi[:, 4:8, P * i:P * i + n].bitcast(F32), ALU.subtract).then_inc(s_ol, 1)

            def bias_max(i):
                qt, h = i // 4, i % 4
                nk = P * (qt + 1)
                v.wait_ge(s_sc, i + 1)
                p2 = 2 * (i % 2)
                for c in range(2):
                    e = v.scalar_tensor_tensor(out=pr[:, p2 + c, 0:nk], in0=dist[:, 384 - P * qt:384 - P * qt + nk], scalar=-SLOPES[h],
                                               in1=ps[:, p2 + c, 0:nk], op0=ALU.mult, op1=ALU.add)
                e.then_inc(s_sb, 1)
                v.wait_ge(s_sb, i + 1)
                link(v.tensor_reduce(st[:, 20 + p2:22 + p2], pr[:, p2:p2 + 2, 0:nk], AX, ALU.max))
                v.tensor_scalar(st[:, 20 + p2:22 + p2], st[:, 20 + p2:22 + p2], -1.0, None, ALU.mult).then_inc(s_mx, 1)

            def weights(i):
                nk = P * (i // 4 + 1)
                p2 = 2 * (i % 2)
                v.wait_ge(s_e, i + 1)
                link(v.reciprocal(st[:, 24 + p2:26 + p2], st[:, 24 + p2:26 + p2]))
                link(v.tensor_tensor(st[:, 25 + p2:26 + p2], st[:, 25 + p2:26 + p2], neglam, ALU.mult))
                if i >= 2:
                    v.wait_ge(s_atr, i - 1)
                link(v.tensor_scalar(aa[:, i % 2, 0:nk], pr[:, p2, 0:nk], st[:, 24 + p2:25 + p2], None, ALU.mult))
                v.scalar_tensor_tensor(out=aa[:, i % 2, 0:nk], in0=pr[:, p2 + 1, 0:nk], scalar=st[:, 25 + p2:26 + p2],
                                       in1=aa[:, i % 2, 0:nk], op0=ALU.mult, op1=ALU.add).then_inc(s_a, 1)
                v.wait_ge(s_a, i + 1)

            v.wait_ge(s_outp, 16 * 5)
            v.wait_ge(s_ust, 32)
            bias_max(0)
            for i in range(16):
                if i + 1 < 16:
                    bias_max(i + 1)
                weights(i)
                if i % 4 == 0 and i >= 4:
                    v.wait_ge(s_pv, i)
                    o_norm(i // 4 - 1, P)
                if i % 4 == 2 and i >= 6:
                    o_lo(i // 4 - 1, P)
            v.wait_ge(s_pv, 16)
            o_norm(3, P)
            o_lo(3, P)

            v.wait_ge(s_qb, 1)
            for h in range(H):
                for c in range(2):
                    rows = slice(HD * c, HD * c + HD)
                    dst = q_blk.rearrange("p (b h) n -> p b h n", h=H)[rows, :, h, 8 * h + 4 * c:8 * h + 4 * c + 4]
                    last = v.tensor_copy(dst, q_t[rows, h, 512:544].rearrange("p (b q) -> p b q", q=NS))
            last.then_inc(s_qb, 1)
            for t in range(2):
                v.wait_ge(s_sss, 16 * (t + 1))
                v.scalar_tensor_tensor(out=s_smp[:, t, 0:512], in0=dist_s[:, 0:512], scalar=cst[:, C_SLOPE:C_SLOPE + 1],
                                       in1=ps[:, 4 + t, :], op0=ALU.mult, op1=ALU.add)
                link(v.scalar_tensor_tensor(out=s_smp[:, t, 512:544], in0=dist_s[:, 512 + 32 * t:544 + 32 * t], scalar=cst[:, C_SLOPE:C_SLOPE + 1],
                                            in1=ps[:, 3 + 3 * t, 0:32], op0=ALU.mult, op1=ALU.add))
                link(v.tensor_reduce(st[:, 32 + t:33 + t], s_smp[:, t, :], AX, ALU.max))
                v.tensor_scalar(st[:, 32 + t:33 + t], st[:, 32 + t:33 + t], -1.0, None, ALU.mult).then_inc(s_smx, 1)
                v.wait_ge(s_se, t + 1)
                link(v.reciprocal(st[:, 34 + t:35 + t], st[:, 34 + t:35 + t]))
                link(v.tensor_tensor(st[:, 34 + t:35 + t], st[:, 34 + t:35 + t], st[:, 18:19], ALU.mult))
                v.tensor_scalar(s_smp[:, t, :], s_smp[:, t, :], st[:, 34 + t:35 + t], None, ALU.mult).then_inc(s_sa, 1)
                v.wait_ge(s_ptr, t + 1)
                w = ps[:, 0 + t, :].rearrange("p (k x c q) -> p k x c q", k=4, c=2, q=NS)
                for k in range(4):
                    link(v.tensor_copy(p_t[:, t, k, :].rearrange("p (x q) -> p x q", q=NS), w[:, k, :, 0, :]))
                    v.tensor_tensor(p_t[:, t, k, :].rearrange("p (x q) -> p x q", q=NS), p_t[:, t, k, :].rearrange("p (x q) -> p x q", q=NS), w[:, k, :, 1, :], ALU.add)
                w = ps[0:32, 2 + 3 * t, 0:P].rearrange("p (x c q) -> p x c q", c=2, q=NS)
                pn = p_t[0:32, t, 4, :].rearrange("p (x q) -> p x q", q=NS)
                link(v.tensor_copy(pn, w[:, :, 0, :]))
                v.tensor_tensor(pn, pn, w[:, :, 1, :], ALU.add).then_inc(s_pe, 1)
            v.wait_ge(s_o6, 1)
            o_norm(4, 32)
            o_lo(4, 32)

            v.wait_ge(s_xr, 16 * NT)
            for i in range(20):
                c, t = i // 5, i % 5
                n = TILES[t][1]
                v.wait_ge(s_w, i + 1)
                dst = h_res[0:n, t, 256 * c:256 * c + 256]
                v.tensor_tensor(dst, ps[0:n, i % 4, 0:256], dst, ALU.add).then_inc(s_he, 1)
            start = Chunks(PRO, 0)
            v.wait_ge(s_late2, 64)
            link(v.memset(sel, 0.0))
            for t, (_, n) in enumerate(TILES):
                v.wait_ge(s_n2, t + 1)
                v.tensor_scalar(st[0:n, 36 + t:37 + t], st[0:n, 36 + t:37 + t], 1.0 / D, EPS, ALU.mult, ALU.add).then_inc(s_r2, 1)

            def norm2(t):
                n = TILES[t][1]
                v.wait_ge(s_act_c, t + 1)
                link(v.reciprocal(st[0:n, 36 + t:37 + t], st[0:n, 36 + t:37 + t]))
                if t >= 2:
                    v.wait_ge(s_h2t, t - 1)
                    v.wait_ge(s_h2d, 16 * (t - 1))
                v.scalar_tensor_tensor(out=h2[0:n, t % 2, :], in0=h_res[0:n, t, :], scalar=st[0:n, 36 + t:37 + t], in1=g2[0:n, :],
                                       op0=ALU.mult, op1=ALU.mult).then_inc(s_h2, 1)

            def choose(t):
                n = TILES[t][1]
                v.wait_ge(s_lg, t + 1)
                if t >= 1:
                    v.wait_ge(s_ge, t)
                v.tensor_tensor(lgt[0:n], ps[0:n, t % 2, 0:NE], rbias[0:n], ALU.add).then_inc(s_lge, 1)
                v.wait_ge(s_lge, t + 1)
                link(v.max(top[0:n], lgt[0:n]))
                v.tensor_scalar(st[0:n, 44:45], top[0:n, 0:1], -1.0, None, ALU.mult).then_inc(s_gm, 1)
                link(v.max_index(topi[0:n], top[0:n], lgt[0:n]))
                link(v.tensor_copy(topf[0:n], topi[0:n, 0:4]))
                link(v.tensor_tensor(oh4[0:n], iota[0:n, 0:NE].unsqueeze(1).to_broadcast([n, 4, NE]),
                                     topf[0:n].unsqueeze(2).to_broadcast([n, 4, NE]), ALU.is_equal))
                v.tensor_reduce(sel[0:n, t, :], oh4[0:n].rearrange("p k e -> p e k"), AX, ALU.add)
                link(v.tensor_tensor(kv4[0:n], oh4[0:n], iota[0:n, 0:4].unsqueeze(2).to_broadcast([n, 4, NE]), ALU.mult))
                link(v.tensor_reduce(vals[0:n, t, 0:NE, 1], kv4[0:n].rearrange("p k e -> p e k"), AX, ALU.add))
                link(v.tensor_scalar(topf[0:n, 0:1], cst[0:n, C_TOK + t:C_TOK + t + 1], 4.0, 1.0, ALU.mult, ALU.add))
                v.tensor_scalar(vals[0:n, t, 0:NE, 1], vals[0:n, t, 0:NE, 1], topf[0:n, 0:1], None, ALU.add)
                link(v.tensor_scalar(vals[0:n, t, 0:NE, 0], ones[0:n, 0:NE], cst[0:n, C_TOK + t:C_TOK + t + 1], None, ALU.add))
                v.wait_ge(s_ge, t + 1)
                link(v.reciprocal(st[0:n, 46:47], st[0:n, 45:46]))
                v.tensor_scalar(gate[0:n, t, :], gate[0:n, t, :], st[0:n, 46:47], None, ALU.mult).then_inc(s_sel, 1)

            for t in range(NT):
                norm2(t)
                if t >= 1:
                    choose(t - 1)
            choose(4)
            v.wait_ge(s_rk, 1)
            for t in range(NT):
                link(v.scalar_tensor_tensor(out=rank[:, t, 0:NE], in0=ps[:, t, 0:NE], scalar=1.0, in1=sel[:, t, :], op0=ALU.add, op1=ALU.mult))
                last = v.tensor_scalar(rank[:, t, 0:NE], rank[:, t, 0:NE], -1.0, None, ALU.add)
            last.then_inc(s_tab, 1)
            v.tensor_copy(cnt[0:1, 0:NE], ps[0:1, 5, 0:NE]).then_inc(s_tab, 1)
            link(v.tensor_reduce(cntf[0:1, 0:1], ps[0:1, 5, 0:NE], AX, ALU.max))
            v.tensor_copy(cnt[0:1, NE:NE + 1], cntf[0:1, 0:1]).then_inc(s_tab, 1)
            v.wait_ge(s_tab, 3)

            def expert_lo(ck, j):
                split_lo(ck.raw_slot(j), ck.slot(j), ck.number(j + 1))

            def indices(m, column, link_at):
                v.wait_ge(s_ix, m + 1)
                v.tensor_scalar(unused[:], ps[:, 6, 0:2], 0.0, UNUSED, ALU.is_equal, ALU.mult).then_inc(s_dve, 1)
                v.wait_ge(s_dve, link_at + 1)
                v.scalar_tensor_tensor(out=idx[:, bass.ds(column, 1), :].rearrange("p a b -> p (a b)"), in0=ps[:, 6, 0:2], scalar=-1.0, in1=unused[:],
                                       op0=ALU.add, op1=ALU.add).then_inc(s_ixe, 1)

            def rows_lo(m, hi_sem, done, dst, dst_hi):
                v.wait_ge(hi_sem, m + 1)
                src = ps[:, 6:8, :].rearrange("p b (k c) -> p (b k) c", c=P)
                v.tensor_tensor(dst, src, dst_hi.bitcast(F32), ALU.subtract).then_inc(done, 1)

            def clamp(m, half, w1_done):
                cols = slice(512 * half, 512 * half + 512)
                src = ps[:, 2 * half:2 * half + 2, :].rearrange("p b (n two) -> p two (b n)", two=2)
                v.wait_ge(s_pc, w1_done)
                if not isinstance(m, int) or m > 0:
                    v.wait_ge(s_ac, m * 2)
                v.tensor_scalar(glu[:, cols], src[:, 0, :], LIMIT, None, ALU.min).then_inc(s_g, 1)
                v.tensor_scalar(lin[:, cols], src[:, 1, :], LIMIT, -LIMIT, ALU.min, ALU.max).then_inc(s_l, 1)

            base = chain[0]
            indices(0, 0, base)
            for j in range(RING):
                expert_lo(start, j)
            rows_lo(0, s_xh, s_xl, x_lo, x_hi)
            indices(1, 1, base + 1)
            for j in range(RING, W1C):
                expert_lo(start, j)
            head = Chunks(PRO + W1C, 0)
            for j in range(3):
                expert_lo(head, j)
            clamp(0, 0, W1C)
            clamp(0, 1, W1C)
            expert_lo(head, 3)
            rows_lo(1, s_xh, s_xl, x_lo, x_hi)
            indices(2, 2, base + 2)

            def body(n, j0=0):
                ck = Chunks(PRO + W1C, n)
                for j in range(j0, 4):
                    expert_lo(ck, j)
                rows_lo(n, s_ah, s_al, act_lo, act_hi)
                expert_lo(ck, 4)
                indices(n + 3, n + 3, n + (base + 3))
                for j in range(5, 11):
                    expert_lo(ck, j)
                clamp(n + 1, 0, ck.number(W1C) - PRO)
                clamp(n + 1, 1, ck.number(W1C) - PRO)
                expert_lo(ck, 11)
                rows_lo(n + 2, s_xh, s_xl, x_lo, x_hi)

            body(0, 4)
            with v.Fori(1, NE - 1) as n:
                body(n)
            tail = Chunks(PRO + W1C + PER * (NE - 1), 0)
            for j in range(3):
                expert_lo(tail, j)
            rows_lo(NE - 1, s_ah, s_al, act_lo, act_hi)
            expert_lo(tail, 3)

            after = base + NE + 2
            def further(e, r, i):
                ck = Chunks(EXTRA, i)
                indices(i + (NE + 2), SPARE, i + after)
                rows_lo(i + (NE + 1), s_xh, s_xl, x_lo, x_hi)
                for j in range(W1C):
                    expert_lo(ck, j)
                for half in range(2):
                    clamp(i + NE, half, ck.number(W1C) - PRO)
                rows_lo(i + NE, s_ah, s_al, act_lo, act_hi)
                for j in range(W1C, PER):
                    expert_lo(ck, j)
                v.wait_ge(s_sca, i * 16 + 16 * (NE + 1))
                v.sem_inc(s_carry, 1)

            further_blocks(v, further)
            v.wait_ge(s_gf, 16)
            v.wait_ge(s_ol, NT)
            cf = s_fc
            for t, (_, n) in enumerate(TILES):
                v.wait_ge(s_fy[t % 2], 16 * (t // 2 + 1))
                rows = ar[:, 5120 + 4096 * (t % 2):5120 + 4096 * (t % 2) + 4096].rearrange("p (k d) -> p k d", k=TOPK)
                for k in range(TOPK):
                    e = v.scalar_tensor_tensor(out=h_res[0:n, t, :], in0=rows[0:n, k, :], scalar=gate[0:n, t, k:k + 1],
                                               in1=h_res[0:n, t, :], op0=ALU.mult, op1=ALU.add)
                    if k < TOPK - 1:
                        e.then_inc(cf, 1)
                        v.wait_ge(cf, 4 * t + k + 1)
                e.then_inc(s_fs, 1)
                v.wait_ge(s_fr, 2 * t + 1)
                v.tensor_scalar(st[0:n, 50 + t:51 + t], st[0:n, 50 + t:51 + t], 1.0 / D, EPS, ALU.mult, ALU.add).then_inc(s_fs, 1)
                v.wait_ge(s_fr, 2 * t + 2)
                v.reciprocal(st[0:n, 50 + t:51 + t], st[0:n, 50 + t:51 + t]).then_inc(cf, 1)
                v.wait_ge(cf, 4 * t + 4)
                v.scalar_tensor_tensor(out=raw[0:n, t // 2, D * (t % 2):D * (t % 2) + D], in0=h_res[0:n, t, :], scalar=st[0:n, 50 + t:51 + t],
                                       in1=raw[0:n, 3, 0:D], op0=ALU.mult, op1=ALU.mult).then_inc(s_fo, 1)

        @block.tensor
        def _(pe):
            pe.wait_ge(s_g1, 32)
            for t, (_, n) in enumerate(TILES):
                pe.wait_ge(s_xn, t + 1)
                if t >= 2:
                    pe.wait_ge(s_tl, t - 1)
                for k in range(KT):
                    last = pe.transpose(ps[:, 2 * (t % 2) + k // 4, P * (k % 4):P * (k % 4) + n], xn[0:n, P * k:P * k + P], ident[0:n, 0:n])
                last.then_inc(s_tp, 1)
            pe.wait_ge(s_tl, NT)

            def three(out, lhs, rhs, start, stop):
                for q, (l, r) in enumerate(((lhs[0], rhs[0]), (lhs[0], rhs[1]), (lhs[1], rhs[0]))):
                    last = pe.matmul(out, l, r, start=start and q == 0, stop=stop and q == 2)
                return last

            def k_transposes(hp):
                pe.wait_ge(s_ze, LAST_UNIT[4 + hp])
                if hp:
                    pe.wait_ge(s_kte, 1)
                for hh in range(2):
                    cols = slice(P * (2 * hp + hh), P * (2 * hp + hh) + P)
                    for t in range(4):
                        pe.transpose(ps[:, 2 * hh, P * t:P * t + P], k_nat[:, t, cols], ident)
                    last = pe.transpose(ps[:, 2 * hh + 1, 0:32], k_nat[0:32, 4, cols], ident[0:32, 0:32])
                last.then_inc(s_kt, 1)

            wv = [[r[:, s, :].rearrange("p (k n) -> p k n", k=KT) for s in range(RING)] for r in (hi, lo)]
            for i, (c, kind, t, part) in enumerate(UNITS):
                pe.wait_ge(s_lo, c + 1)
                if i >= 4:
                    pe.wait_ge(s_ze, i - 3)
                bank = 4 + i % 4
                w = [wv[0][c % RING], wv[1][c % RING]]
                for k in range(KT):
                    if kind == "q":
                        n = 512 if part == 0 else 32
                        last = three(ps[:, bank, 0:n], [y[:, k, P * t:P * t + P] for y in w],
                                     [y[:, k, 512 * part:512 * part + n] for y in (t_hi, t_lo)], k == 0, k == KT - 1)
                    else:
                        last = three(ps[:, bank, 0:256], [y[:, k, P * t:P * t + P] for y in (t_hi, t_lo)],
                                     [y[:, k, :] for y in w], k == 0, k == KT - 1)
                last.then_inc(s_z, 1)
                if i + 1 == LAST_UNIT[5]:
                    k_transposes(0)
                if i + 1 == LAST_UNIT[6]:
                    k_transposes(1)

            def diff(g):
                if g >= 2:
                    pe.wait_ge(s_de, g - 1)
                b = 2 * (g % 2)
                ch = slice(P * g, P * g + P)
                for j in range(4):
                    out = ps[:, b, P * j:P * j + P]
                    if j:
                        pe.matmul(out, u_nat[:, j - 1, ch], band[:, g, 2, :], start=True, stop=False)
                    pe.matmul(out, u_nat[:, j, ch], band[:, g, 1 if j else 0, :], start=not j, stop=True)
                pe.matmul(ps[:, b + 1, 0:32], state[0:NB * BUF, ch], sband[0:NB * BUF, g, 0, :], start=True, stop=False)
                pe.matmul(ps[:, b + 1, 0:32], u_smp[0:32, ch], sband[0:32, g, 1, :], start=False, stop=True).then_inc(s_d, 1)

            def linear(g):
                pe.wait_ge(s_de, g + 1)
                if g >= 2:
                    pe.wait_ge(s_pl, g - 1)
                b = 4 + 2 * (g % 2)
                pe.matmul(ps[:, b, :], pw[:, g, :], d_t[g % 2][:, 0:512], start=True, stop=True)
                pe.matmul(ps[:, b + 1, 0:32], pw[:, g, :], d_t[g % 2][:, 512:544], start=True, stop=True).then_inc(s_po, 1)

            pe.wait_ge(s_late, 32)
            pe.wait_ge(s_kte, 2)
            pe.wait_ge(s_ze, len(UNITS))
            diff(0)
            for g in range(1, 4):
                diff(g)
                linear(g - 1)
            linear(3)

            def scores(i):
                qt, h = i // 4, i % 4
                nk = P * (qt + 1)
                if i >= 2:
                    pe.wait_ge(s_sb, i - 1)
                for c in range(2):
                    rows = slice(HD * c, HD * c + HD)
                    last = pe.matmul(ps[:, 2 * (i % 2) + c, 0:nk], q_t[rows, h, P * qt:P * qt + P], k_t[rows, h, 0:nk], start=True, stop=True)
                last.then_inc(s_sc, 1)

            def o_transposes(i, n):
                pe.wait_ge(s_on, i + 1)
                if i:
                    pe.wait_ge(s_ol, i)
                for h in range(H):
                    last = pe.transpose(ps[:, 7, P * h:P * h + n], o_nat[0:n, P * h:P * h + P], ident[0:n, 0:n])
                last.then_inc(s_ot, 1)

            pe.wait_ge(s_pl, 4)
            scores(0)
            scores(1)
            for i in range(16):
                qt, h = i // 4, i % 4
                pe.wait_ge(s_a, i + 1)
                if i >= 2:
                    pe.wait_ge(s_ate, i - 1)
                for k in range(qt + 1):
                    last = pe.transpose(ps[:, 4 + i % 2, P * k:P * k + P], aa[:, i % 2, P * k:P * k + P], ident)
                last.then_inc(s_atr, 1)
                if i + 2 < 16:
                    scores(i + 2)
                if h == 0 and qt:
                    o_transposes(qt - 1, P)
                pe.wait_ge(s_ate, i + 1)
                for k in range(qt + 1):
                    last = pe.matmul(ps[:, 6, P * h:P * h + P], at_sb[:, i % 2, P * k:P * k + P], v_nat[:, k, P * h:P * h + P], start=k == 0, stop=k == qt)
                last.then_inc(s_pv, 1)
            o_transposes(3, P)

            def page_transposes(m):
                b, h = m // H, m % H
                if h == 0:
                    pe.wait_ge(s_pg[b % 2], 64 * (b // 2 + 1))
                if m >= 3:
                    pe.wait_ge(s_kc, m - 2)
                for k in range(PAGES):
                    last = pe.transpose(ps[:, m % 3, P * k:P * k + P], page[:, PAGES * (b % 2) + k, P * h:P * h + P], ident)
                last.then_inc(s_kp, 1)

            pe.wait_ge(s_qb, 2)
            pe.wait_ge(s_ol, 4)
            page_transposes(0)
            for m in range(NB * H):
                b, h = m // H, m % H
                if m + 1 < NB * H:
                    page_transposes(m + 1)
                pe.wait_ge(s_kc, m + 1)
                rows = slice(32 * (b % 4), 32 * (b % 4) + 32)
                pe.matmul(ps[rows, 4 + b // 4, :], q_blk[:, m, :], kt_s[:, m % 3, :], start=h == 0, stop=h == H - 1,
                          tile_position=(0, 32 * (b % 4)))
                pe.matmul(ps[rows, 3 + 3 * (b // 4), 0:32], q_blk[:, m, :], k_t[:, h, 512:544], start=h == 0, stop=h == H - 1,
                          tile_position=(0, 32 * (b % 4))).then_inc(s_sss, 1)
            for t in range(2):
                pe.wait_ge(s_sa, t + 1)
                pe.wait_ge(s_kc, NB * H)
                for k in range(PAGES):
                    pe.transpose(ps[:, t, P * k:P * k + P], s_smp[:, t, P * k:P * k + P], ident)
                pe.transpose(ps[0:32, 2 + 3 * t, 0:P], s_smp[:, t, 512:544], ident).then_inc(s_ptr, 1)
            for b in range(NB):
                t = b // 4
                pe.wait_ge(s_pe, t + 1)
                pe.wait_ge(s_vg[b % 2], 64 * (b // 2 + 1))
                for h in range(H):
                    x = NS * (H * (b % 4) + h)
                    out = ps[:, 7, 32 * h + NS * b:32 * h + NS * b + NS]
                    for k in range(PAGES):
                        pe.matmul(out, page[:, PAGES * (b % 2) + k, P * h:P * h + P], p_t[:, t, k, x:x + NS], start=k == 0, stop=False)
                    last = pe.matmul(out, v_nat[0:32, 4, P * h:P * h + P], p_t[0:32, t, 4, x:x + NS], start=False, stop=True)
                last.then_inc(s_vb, 1)
            pe.wait_ge(s_oe, 1)
            for h in range(H):
                last = pe.transpose(ps[0:32, 6, P * h:P * h + P], o_ts[:, 32 * h:32 * h + 32], ident)
            last.then_inc(s_o6, 1)
            o_transposes(4, 32)

            pe.wait_ge(s_ol, NT)
            for i in range(20):
                c, t = i // 5, i % 5
                pe.wait_ge(s_lo, 8 + c + 1)
                if i >= 4:
                    pe.wait_ge(s_he, i - 3)
                w = [wv[0][(8 + c) % RING], wv[1][(8 + c) % RING]]
                for k in range(KT):
                    last = three(ps[:, i % 4, 0:256], [y[:, k, P * t:P * t + P] for y in (t_hi, t_lo)],
                                 [y[:, k, :] for y in w], k == 0, k == KT - 1)
                last.then_inc(s_w, 1)
            pe.wait_ge(s_late2, 64)
            pe.wait_ge(s_he, 20)

            def router(t):
                n = TILES[t][1]
                pe.wait_ge(s_h2e, t + 1)
                if t >= 2:
                    pe.wait_ge(s_lge, t - 1)
                hv = h2_t[:, t % 2, :].rearrange("p (k c) -> p k c", c=P)
                for k in range(KT):
                    last = pe.matmul(ps[0:n, t % 2, 0:NE], hv[:, k, 0:n], rw[:, k, :], start=k == 0, stop=k == KT - 1)
                last.then_inc(s_lg, 1)

            for t, (_, n) in enumerate(TILES):
                pe.wait_ge(s_h2, t + 1)
                if t >= 2:
                    pe.wait_ge(s_h2e, t - 1)
                for k in range(KT):
                    last = pe.transpose(ps[:, 4 + 2 * (t % 2) + k // 4, P * (k % 4):P * (k % 4) + n], h2[0:n, t % 2, P * k:P * k + P], ident[0:n, 0:n])
                last.then_inc(s_h2t, 1)
                if t >= 1:
                    router(t - 1)
            router(4)
            pe.wait_ge(s_sel, NT)
            for t in range(NT):
                for b in range(t):
                    pe.matmul(ps[:, t, 0:NE], ones, sel[:, b, :], start=b == 0, stop=False)
                pe.matmul(ps[:, t, 0:NE], tri, sel[:, t, :], start=t == 0, stop=True)
            for b in range(NT):
                last = pe.matmul(ps[:, 5, 0:NE], ones, sel[:, b, :], start=b == 0, stop=b == NT - 1)
            last.then_inc(s_rk, 1)
            pe.wait_ge(s_tab, 3)

            def index_product(m):
                pe.wait_ge(s_ohd, m + 1)
                for t in range(NT):
                    last = pe.matmul(ps[:, 6, 0:2], onehot[:, t, :], vals_c[:, t, :], start=t == 0, stop=t == NT - 1)
                last.then_inc(s_ix, 1)

            def row_transposes(src, wait, value, done):
                pe.wait_ge(wait, value)
                for k in range(KT):
                    last = pe.transpose(ps[:, 6 + k // 4, P * (k % 4):P * (k % 4) + P], src[:, P * k:P * k + P], ident)
                last.then_inc(done, 1)

            def x_transposes(m, gathered):
                if not isinstance(m, int) or m > 0:
                    pe.wait_ge(s_xl, m)
                row_transposes(xg, s_gat, gathered * 16, s_xt)

            def act_transposes(m):
                row_transposes(act, s_ac, m * 2 + 2, s_at)

            def expert_chunk(ck, j, lhs, k, banks, first_k, bias):
                pe.wait_ge(s_lo, ck.number(j + 1))
                tiles = 4 // banks
                base_bank = 0 if banks == 4 else 4
                for kk in range(tiles):
                    row = tiles * k + kk
                    for q, (l, r) in enumerate(((0, hi), (0, lo), (1, hi))):
                        for b in range(banks):
                            at = 512 * (banks * kk + b)
                            last = pe.matmul(ps[:, base_bank + b, :], lhs[l][:, row, :], r[:, ck.slot(j), at:at + 512],
                                             start=first_k and kk == 0 and q == 0, stop=False)
                if bias is not None:
                    pick, col = bias
                    for b in range(banks):
                        last = pe.matmul(ps[:, base_bank + b, :], pick[:], bias_r[:, col + 512 * b:col + 512 * b + 512], start=False, stop=True)
                last.then_inc(s_pc, 1)

            def w1(ck, j, m, selected, rows_ready):
                if j == 0:
                    pe.wait_ge(s_xl, rows_ready)
                    if not isinstance(m, int) or m > 0:
                        pe.wait_ge(s_l, m * 2)
                if j == W1C - 1:
                    pe.wait_ge(s_bs, selected)
                expert_chunk(ck, j, (x_hi, x_lo), j, 4, j == 0, (sel_w1, 0) if j == W1C - 1 else None)

            def w2(ck, j, m, selected):
                k = j % 4
                if k == 0:
                    pe.wait_ge(s_al, m + 1)
                    if not isinstance(m, int) or m > 0:
                        pe.wait_ge(s_ye, m)
                if k == W2C - 1:
                    pe.wait_ge(s_bs, selected)
                expert_chunk(ck, j, (act_hi, act_lo), k, 2, k == 0, (sel_w2, 2 * D) if k == W2C - 1 else None)

            index_product(0)
            pe.wait_ge(s_ixe, 1)
            x_transposes(0, 1)
            pe.wait_ge(s_xl, 1)
            index_product(1)
            start = Chunks(PRO, 0)
            for j in range(W1C):
                if j == 1:
                    pe.wait_ge(s_ixe, 2)
                    x_transposes(1, 2)
                w1(start, j, 0, 1, 1)

            def body(n):
                ck = Chunks(PRO + W1C, n)
                for j in range(W1C):
                    if j == 2:
                        act_transposes(n)
                    if j == 4:
                        pe.wait_ge(s_al, n + 1)
                        index_product(n + 3)
                    if j == 6:
                        pe.wait_ge(s_ixe, n + 4)
                        x_transposes(n + 2, n + 3)
                    w1(ck, j, n + 1, n + 2, n + 2)
                for j in range(W1C, PER):
                    w2(ck, j, n, n + 2)

            pe.wait_ge(s_xl, 2)
            index_product(2)
            pe.wait_ge(s_ixe, 3)
            body(0)
            with pe.Fori(1, NE - 1) as n:
                body(n)
            tail = Chunks(PRO + W1C + PER * (NE - 1), 0)
            pe.wait_ge(s_xl, NE + 1)
            act_transposes(NE - 1)
            for j in range(W2C):
                w2(tail, j, NE - 1, NE + 1)

            def further(e, r, i):
                ck = Chunks(EXTRA, i)
                index_product(i + (NE + 2))
                pe.wait_ge(s_ixe, i + (NE + 3))
                x_transposes(i + (NE + 1), i + (NE + 3))
                for j in range(W1C):
                    w1(ck, j, i + NE, i + (NE + 2), i + (NE + 2))
                act_transposes(i + NE)
                for j in range(W1C, PER):
                    w2(ck, j, i + NE, i + (NE + 2))
                pe.wait_ge(s_sca, i * 16 + 16 * (NE + 1))
                pe.sem_inc(s_carry, 1)

            further_blocks(pe, further)


_OUTS = [
    ("y_prompt", (1, SEQ, D)), ("y_sample", (NB, NS, D)),
    ("new_pool_prompt", (1, 1, BUF, POOLW)), ("new_pool_sample", (1, NB, BUF, POOLW)),
    ("new_k_prompt", (1, 1, SEQ, H, P)), ("new_v_prompt", (1, 1, SEQ, H, P)),
    ("new_k_sample", (1, NB, NS, H, P)), ("new_v_sample", (1, NB, NS, H, P)),
]


def program(nc, shapes):
    aps = {n: nc.dram_tensor(n, s, mybir.dt.from_np(t), kind="ExternalInput").ap() for n, (s, t) in shapes.items()}
    for n, s in _OUTS:
        aps[n] = nc.dram_tensor("out_" + n, s, F32, kind="ExternalOutput").ap()
    build(nc, aps)


def kernel(**inputs):
    import concourse.bacc as bacc
    from concourse.bass_utils import run_bass_kernel_spmd as run

    arrays = {n: np.ascontiguousarray(v) for n, v in inputs.items()}
    arrays.update(constants())
    nc = bacc.Bacc("TRN2", target_bir_lowering=False, num_devices=1)
    program(nc, {n: (v.shape, v.dtype) for n, v in arrays.items()})
    r = run(nc, [arrays], core_ids=[0])
    return tuple(r.results[0]["out_" + n] for n, _ in _OUTS)
```

```python
from contextlib import ExitStack

import numpy as np
import concourse.bass as bass
from concourse import mybir

ALU = mybir.AluOpType
ACT = mybir.ActivationFunctionType
F32 = mybir.dt.float32
F32R = mybir.dt.float32r
I32 = mybir.dt.int32
U32 = mybir.dt.uint32
AX = mybir.AxisListType.X

P = 128
D = 1024
SEQ = 512
NB = 8
NS = 4
NTOK = SEQ + NB * NS
TILES = [(0, 128), (128, 128), (256, 128), (384, 128), (512, 32)]
NT = len(TILES)
H = 4
HD = 64
PAST = 512
PAGES = 4
POOLW = 512
BUF = 15
NE = 32
TOPK = 4
KT = D // P
EPS = 1e-6
LAMBDA_INIT = 0.2
LIMIT = 7.0
ALPHA = 1.702
WINDOWS = (2, 4, 8, 16)
SLOPES = [2.0 ** (-8.0 * (h + 1) / H) for h in range(H)]
MASKED = 1e34
RAW, RING = 4, 4
CH = 2048
W1C, W2C = 8, 4
PER = W1C + W2C
PRO = 12
TABLE = NE + 3
SPARE = NE + 2
UNUSED = 65536.0

A_V, A_QT, A_KT, A_DIST = 0, 2560, 4736, 6912
A_KN, A_BAND, A_US = 8000, 10560, 12352
A_XN, A_SQ1 = 8000, 9024
A_P, A_A, A_AT, A_ON, A_SQ = 8000, 10048, 11072, 12096, 12608
A_QB, A_S, A_PT = 9216, 10240, 11328
A_H, A_XG, A_OH = 0, 5120, 6144
A_ACT, A_G, A_SIG, A_L, A_Y, A_TMP = 7168, 8192, 9216, 10240, 11264, 12288
A_G2, A_H2T, A_SQ2, A_RW = 8192, 6144, 9216, 5120
A_RT, A_TRI = 5376, 5888
A_LAM, A_GSUB = 12864, 13120
ARENA = 13312
SLOT_H = (0, 1, 3, 4, 2)
C_ID, C_IOTA = 0, 128
C_TOK = C_IOTA + 640
C_NEGM, C_M0, C_M1, C_SLOPE = C_TOK + 5, C_TOK + 6, C_TOK + 7, C_TOK + 8
C_EYE = C_TOK + 9
C_EPS = C_EYE + NE
NCONST = C_EPS + 1


def constants():
    c = np.zeros((P, NCONST), np.float32)
    p = np.arange(P)
    c[:, C_ID:C_ID + P] = np.eye(P)
    c[:, C_IOTA:C_IOTA + 640] = np.arange(640)
    c[:, C_TOK:C_TOK + 5] = p[:, None] + P * np.arange(5)
    c[:, C_NEGM] = np.where(p >= NE, -1, 0)
    second = (p // NS) % 2
    c[:, C_M0], c[:, C_M1] = 1 - second, second
    c[:, C_SLOPE] = [-SLOPES[(i // 8) % H] for i in p]
    c[:, C_EYE:C_EYE + NE] = (p[:, None] % NE) == np.arange(NE)
    c[:, C_EPS] = EPS
    d = np.full((P, 512 + 576), MASKED, np.float32)
    dist = p[:, None] - np.arange(512)[None, :] + 384
    d[:, :512] = np.where(dist >= 0, dist, MASKED)
    q = p % NS
    d[:, 512:1024] = PAST + q[:, None] - np.arange(PAST)[None, :]
    for t in range(2):
        for i in range(P):
            b = 4 * t + i // 32
            for j in range(q[i] + 1):
                d[i, 1024 + 32 * t + NS * b + j] = q[i] - j
    band = np.zeros((P, 4, 3, P), np.float32)
    sband = np.zeros((P, 4, 2, 32), np.float32)
    t, s = np.arange(P)[None, :], p[:, None]
    for g, w in enumerate(WINDOWS):
        here = (t - s >= 0) & (t - s < w)
        band[:, g, 0] = here / np.minimum(w, t + 1.0) - (t == s)
        band[:, g, 1] = here / float(w) - (t == s)
        band[:, g, 2] = ((t + P - s) < w) / float(w)
        for b in range(NB):
            for n in range(NS):
                for j in range(BUF):
                    sband[b * BUF + j, g, 0, b * NS + n] = (BUF + n - j < w) / w
                for j in range(n + 1):
                    sband[b * NS + j, g, 1, b * NS + n] = (n - j < w) / w - (n == j)
    bands = np.concatenate([band.reshape(P, -1), sband.reshape(P, -1)], 1)
    tri = np.concatenate([p[:, None] < p[None, :], np.ones((P, P), bool)], 1).astype(np.float32)
    return {"c_misc": c, "c_dist": d, "c_band": bands, "c_tri": tri}


def units():
    out = []
    for c in range(8):
        if c in (2, 3):
            out += [(c, "q", hh, part) for hh in range(2) for part in range(2)]
        else:
            out += [(c, "u" if c < 2 else "k" if c < 6 else "v", t, 0) for t in range(NT)]
    return out


UNITS = units()
LAST_UNIT = [max(i for i, u in enumerate(UNITS) if u[0] == c) + 1 for c in range(8)]


def build(nc, a):
    x_in = [(a["x_prompt"].rearrange("b t d -> (b t) d"), 128 * t) for t in range(4)]
    x_in.append((a["x_sample"].rearrange("b t d -> (b t) d"), 0))
    w_in = a["w_in"][0].rearrange("(k p) n -> p k n", p=P)
    w_out = a["w_out"][0].rearrange("(k p) n -> p k n", p=P)
    h2_dram = nc.dram_tensor("h2_rows", [NTOK, D], F32).ap()
    y_dram = nc.dram_tensor("expert_rows", [NTOK * TOPK, D], F32).ap()

    with ExitStack() as ctx:
        def sb(name, shape, dt=F32):
            return ctx.enter_context(nc.sbuf_tensor(name, shape, dt))

        def sem(name):
            return ctx.enter_context(nc.semaphore(name))

        raw = sb("raw", [P, RAW, CH])
        hi = sb("hi", [P, RING, CH], F32R)
        lo = sb("lo", [P, RING, CH], F32R)
        t_hi = sb("t_hi", [P, KT, 640], F32R)
        t_lo = sb("t_lo", [P, KT, 640], F32R)
        ar = sb("arena", [P, ARENA])
        bias_r = sb("bias_r", [2 * NE, 3 * D], F32R)
        sel_w1 = sb("sel_w1", [2 * NE, P], F32R)
        sel_w2 = sb("sel_w2", [2 * NE, P], F32R)
        cst = sb("cst", [P, NCONST])
        st = sb("stats", [P, 64])
        psc = sb("psc", [P, 4])
        pt = sb("pt", [1, NB * PAGES], I32)
        top = sb("top", [P, 8])
        topi = sb("topi", [P, 8], U32)
        topf = sb("topf", [P, 4])
        gate = sb("gate", [P, NT, 4])
        rank = sb("rank", [P, NT, TABLE])
        vals = sb("vals", [P, NT, TABLE, 2])
        rank_c = sb("rank_c", [P, NT])
        vals_c = sb("vals_c", [P, NT, 2])
        unused = sb("unused", [P, 2])
        idx = sb("idx", [P, TABLE, 2], U32)
        idx_g = sb("idx_g", [P, 1], U32)
        idx_s = sb("idx_s", [P, 1], U32)
        cnt = sb("cnt", [1, NE + 8], I32)
        cntf = sb("cntf", [1, 8])
        ps = ctx.enter_context(nc.psum_tensor("ps", [P, 8, 512], F32))

        def A(at, *shape):
            n = int(np.prod(shape))
            v = ar[:, at:at + n]
            if len(shape) == 2:
                v = v.rearrange("p (a b) -> p a b", a=shape[0])
            if len(shape) == 3:
                v = v.rearrange("p (a b c) -> p a b c", a=shape[0], b=shape[1])
            return v

        ident = cst[:, C_ID:C_ID + P]
        lamv, gsub = A(A_LAM, 4 * HD), A(A_GSUB, P)
        slots = A(6784, P)
        rbias, lgt, sel, oh4, kv4 = A(A_RT, NE), A(A_RT + 32, NE), A(A_RT + 64, NT, NE), A(A_RT + 224, 4, NE), A(A_RT + 352, 4, NE)
        tri, ones = A(A_TRI, P), A(A_TRI + P, P)
        iota = cst[:, C_IOTA:C_IOTA + 640]
        v_nat, q_t, k_t = A(A_V, NT, 512), A(A_QT, H, NTOK), A(A_KT, H, NTOK)
        dist, dist_s = A(A_DIST, 512), A(A_DIST + 512, 576)
        k_nat, u_smp = A(A_KN, NT, 512), A(A_US, 512)
        u_nat = raw[:, 3, :].rearrange("p (t n) -> p t n", t=4)
        band = A(A_BAND, 4, 3, P)
        sband = A(A_BAND + 1536, 4, 2, 32)
        x_buf = raw[:, 1, :].rearrange("p (a n) -> p a n", a=2)
        xn, g1 = [raw[:, 2, 0:D], A(A_XN, D)], raw[:, 2, D:2 * D]
        state, pw = raw[:, 1, 0:512], raw[:, 1, 512:1024].rearrange("p (g n) -> p g n", g=4)
        d_t = [raw[:, 1, 1024:1568], raw[:, 2, 0:544]]
        page = raw[:, 0:3, :].rearrange("p s (a n) -> p (s a) n", a=4)
        kt_s = raw[:, 3, 0:1536].rearrange("p (a n) -> p a n", a=3)
        pr = A(A_P, 4, 512)
        aa, at_sb = A(A_A, 2, 512), A(A_AT, 2, 512)
        o_nat, o_sq = A(A_ON, 512), A(A_SQ, 512)
        q_blk, s_smp, p_t = A(A_QB, 32, 32), A(A_S, 2, 544), A(A_PT, 2, 5, 64)
        p_cols = A(A_PT, 2 * 5 * 64 + 32)
        h_res, xg, onehot = A(A_H, NT, D), A(A_XG, D), A(A_OH, NT, P)
        act, glu, sig, lin, y_sb, tmp = (A(v, D) for v in (A_ACT, A_G, A_SIG, A_L, A_Y, A_TMP))
        g2, h2_t, rw = A(A_G2, D), A(A_H2T, 2, D), A(A_RW, KT, NE)
        h2 = raw[:, 3, :].rearrange("p (a n) -> p a n", a=2)
        sq1, sq2 = A(A_SQ1, D), A(A_SQ2, D)
        eps = cst[:, C_EPS:C_EPS + 1]
        choices = [A(A_XG, 4 * D), A(A_XG + 4 * D, 4 * D)]
        choices += [y[:, i:i + 2, :].rearrange("p s n -> p (s n)").bitcast(F32) for y, i in ((hi, 0), (hi, 2), (lo, 0))]
        def sample_cols(y, t):
            return y[:, 4:8, 512 + 16 * t:528 + 16 * t].rearrange("p h (b q) -> p h b q", q=NS)

        def every_32(src):
            return src.rearrange("p h (b x) -> p h b x", x=32)[:, :, :, 0:NS]

        x_hi, x_lo = t_hi[:, :, 0:P], t_lo[:, :, 0:P]
        act_hi, act_lo = t_hi[:, :, P:2 * P], t_lo[:, :, P:2 * P]

        neglam = st[:, 0:1]

        s_x = [sem(f"x_loaded{i}") for i in range(2)]
        s_cst = sem("constants_loaded")
        s_g1 = sem("g1_loaded")
        s_late = sem("pool_inputs_loaded")
        s_raw = [sem(f"raw_loaded{i}") for i in range(RAW)]
        s_hi, s_lo = sem("hi_done"), sem("lo_done")
        s_pad, s_ss, s_rt, s_xn, s_tp = sem("pads_zeroed"), sem("squares_summed"), sem("root_done"), sem("xn_done"), sem("xn_transposed")
        s_th, s_tl = sem("xt_hi_done"), sem("xt_lo_done")
        s_dve, s_act_c, s_pool_c = sem("dve_chain"), sem("act_chain"), sem("pool_chain")
        s_bh, s_lam, s_lame = sem("bias_rounded"), sem("lambda_dots"), sem("lambda_exps")
        s_z, s_ze = sem("z_unit_done"), sem("z_unit_out")
        s_kt, s_kte = sem("k_transposed"), sem("kt_out")
        s_d, s_de, s_po, s_ph, s_pl = sem("pool_diff"), sem("pool_diff_out"), sem("pool_lin"), sem("pool_hi"), sem("pool_lo")
        s_sc, s_sb, s_mx, s_e = sem("scores_done"), sem("scores_biased"), sem("max_done"), sem("exp_done")
        s_a, s_atr, s_ate, s_pv = sem("weights_done"), sem("weights_transposed"), sem("weights_t_out"), sem("pv_done")
        s_os, s_or, s_on, s_ot, s_oh_, s_ol = (sem(n) for n in ("o_squares", "o_root", "o_normed", "o_transposed", "o_hi", "o_lo"))
        s_pg = [sem(f"pages_loaded{i}") for i in range(3)]
        s_qb, s_kp, s_kc, s_sss = sem("q_blocks"), sem("pages_used"), sem("page_t_out"), sem("sample_scores")
        s_smx, s_se, s_sa, s_ptr, s_pe = (sem(n) for n in ("sample_max", "sample_exp", "sample_weights", "sample_wt", "sample_wt_out"))
        s_xr, s_w, s_he = [sem(f"x_reloaded{i}") for i in range(3)], sem("w_out_unit"), sem("h_unit")
        s_n2, s_r2, s_h2, s_h2d, s_h2t, s_h2e, s_lg, s_lge = (sem(n) for n in ("n2_squares", "n2_root", "h2_done", "h2_stored", "h2_transposed", "h2t_out", "router_done", "logits_out"))
        s_gm, s_ge, s_sel, s_rk, s_tab = sem("gate_max"), sem("gate_exp"), sem("selected"), sem("ranks"), sem("tables_done")
        s_late2 = sem("router_inputs_loaded")
        s_ohd, s_ix, s_ixe, s_gat = sem("onehot_done"), sem("index_product"), sem("index_out"), sem("rows_gathered")
        s_xt, s_xh, s_xl = sem("rows_transposed"), sem("rows_hi"), sem("rows_lo")
        s_bs = sem("bias_selector")
        s_pc = sem("chunk_multiplied")
        s_g, s_s, s_l, s_t, s_ac = sem("glu_clamped"), sem("sigmoid_done"), sem("lin_clamped"), sem("gated"), sem("act_done")
        s_at, s_ah, s_al = sem("act_transposed"), sem("act_hi_done"), sem("act_lo_done")
        s_ye, s_sca = sem("y_out"), sem("rows_scattered")
        s_fy = [sem(f"choices_loaded{i}") for i in range(NT)]
        s_gf, s_fs, s_fr, s_fo = sem("gf_loaded"), sem("final_squares"), sem("final_root"), sem("final_done")
        s_out, s_outp, s_ust = sem("outputs_stored"), sem("caches_stored"), sem("u_stored")
        s_fc = sem("final_chain")
        s_carry = sem("carries_waits")

        block = ctx.enter_context(nc.Block())

        def first(m):
            return PRO + W1C + PER * (m - 1)

        def second(m):
            return PRO + W1C + PER * m + W1C

        EXTRA = PRO + PER * NE
        assert EXTRA % RAW == 0 and EXTRA % RING == 0 and PRO % RAW == 0

        def slot_count(g, off):
            return g * 2, off

        class Chunks:

            def __init__(self, base, step):
                self.base, self.step = base, step

            def raw_slot(self, j):
                return (self.base + j) % RAW

            def slot(self, j):
                return (self.base + j) % RING

            def number(self, j):
                return self.step * PER + (self.base + j)

            def loaded(self, j):
                before = PRO if self.raw_slot(j) == 0 else 0
                return self.step * (16 * PER // RAW) + 16 * (before + (self.base + j - PRO) // RAW + 1)

        def further_blocks(eng, body):
            most = eng.value_load(cnt[0:1, NE:NE + 1], min_val=0, max_val=NTOK)
            with eng.If(most > P):
                ran = eng.alloc_register("blocks_ran")
                eng.reg_mov(ran, 0)
                with eng.Fori(0, NE) as e:
                    many = eng.value_load(cnt[0:1, bass.ds(e, 1)], min_val=0, max_val=NTOK)
                    with eng.Fori(0, 4) as r:
                        with eng.If(many > r * P + P):
                            body(e, r, eng.snap(ran, min_val=0, max_val=NTOK * TOPK // P))
                            eng.reg_add(ran, ran, 1)
                        eng.nop()

        @block.sync
        def _(sp):
            def load_x(t):
                src, r = x_in[t]
                n = TILES[t][1]
                if t >= 2:
                    sp.wait_ge(s_xn, t - 1)
                sp.dma_start(x_buf[0:n, t % 2, :], src[r:r + n, :]).then_inc(s_x[t % 2], 16)

            def load_pro(g):
                if g:
                    sp.wait_ge(s_lo, g)
                src = w_in[:, :, 256 * g:256 * g + 256] if g < 8 else w_out[:, :, 256 * (g - 8):256 * (g - 8) + 256]
                sp.dma_start(raw[:, 0, :].rearrange("p (k n) -> p k n", k=KT), src).then_inc(s_raw[0], 16)

            load_x(0)
            sp.dma_start(g1, a["norm1_g"].to_broadcast([P, D])).then_inc(s_g1, 16)
            load_x(1)
            sp.dma_start(cst[:], a["c_misc"]).then_inc(s_g1, 16)
            load_pro(0)
            load_x(2)
            for half in range(2):
                rows = slice(NE * half, NE * half + NE)
                sp.dma_start(ar[rows, 0:2 * D], a["b1"][0]).then_inc(s_cst, 16)
                sp.dma_start(ar[rows, 2 * D:3 * D], a["b2"][0]).then_inc(s_cst, 16)
            for i, n in enumerate(("lambda_q1", "lambda_k1", "lambda_q2", "lambda_k2")):
                sp.dma_start(lamv[:, i * HD:(i + 1) * HD], a[n].to_broadcast([P, HD])).then_inc(s_cst, 16)
            sp.dma_start(gsub, a["subln_g"].to_broadcast([P, P])).then_inc(s_cst, 16)
            with nc.allow_non_contiguous_dma("512 words"):
                sp.dma_start(psc[:], a["pool_scale"][0].rearrange("(g p) -> p g", p=P)).then_inc(s_cst, 16)
            sp.dma_start(pt[:], a["page_table"].rearrange("b n -> (b n)").rearrange("(a n) -> a n", a=1)).then_inc(s_cst, 16)
            sp.dma_start(ar[:, A_DIST:A_DIST + 1088], a["c_dist"]).then_inc(s_cst, 16)
            sp.dma_start(ar[:, A_BAND:A_BAND + 1792], a["c_band"]).then_inc(s_cst, 16)
            load_pro(1)
            load_x(3)
            load_pro(2)
            load_x(4)
            sp.wait_ge(s_xn, NT)
            sp.dma_start(state[0:NB * BUF, :], a["state_pool"][0].rearrange("b t n -> (b t) n")).then_inc(s_late, 16)
            sp.dma_start(pw, a["pool_w"][0].rearrange("g c e -> c g e")).then_inc(s_late, 16)
            for g in range(3, PRO):
                load_pro(g)

            sp.wait_ge(s_cst, 16 * 13)

            def load_pages(cache, b, s):
                pages = [sp.value_load(pt[0:1, b * PAGES + n:b * PAGES + n + 1], min_val=0, max_val=a[cache].shape[1] - 1)
                         for n in range(PAGES)]
                if s == 0:
                    sp.wait_ge(s_lo, PRO)
                if s == 1:
                    sp.wait_ge(s_po, 4)
                if s >= 3:
                    sp.wait_ge(s_kp, H * (s - 2))
                for n in range(PAGES):
                    sp.dma_start(page[:, PAGES * (s % 3) + n, :],
                                 a[cache][0][bass.ds(pages[n], 1)].rearrange("a t h d -> (a t) (h d)")).then_inc(s_pg[s % 3], 16)

            for b in range(NB):
                load_pages("cache_k", b, b)
            for b in range(NB):
                load_pages("cache_v", b, NB + b)

            def load_expert(ck, j, e, k, second_half):
                if second_half:
                    src = a["w2"][0][bass.ds(e, 1), 256 * k:256 * k + 256, :].rearrange("a (k p) n -> p (a k) n", p=P)
                    dst = raw[:, ck.raw_slot(j), :].rearrange("p (k n) -> p k n", k=2)
                else:
                    src = a["w1"][0][bass.ds(e, 1), P * k:P * k + P, :].rearrange("a p n -> (a p) n")
                    dst = raw[:, ck.raw_slot(j), :]
                return sp.dma_start(dst, src).then_inc(s_raw[ck.raw_slot(j)], 16)

            start = Chunks(PRO, 0)
            for j in range(W1C):
                if j == 0:
                    sp.wait_ge(s_kp, 2 * NB * H)
                if j == 3:
                    sp.wait_ge(s_h2t, NT)
                    sp.wait_ge(s_h2d, 16 * NT)
                if j >= RAW:
                    sp.wait_ge(s_lo, PRO + j - RAW + 1)
                load_expert(start, j, 0, j, False)

            def body_loads(n):
                ck = Chunks(PRO + W1C, n)
                for j in range(PER):
                    sp.wait_ge(s_lo, ck.number(j) - RAW + 1)
                    if j < W1C:
                        load_expert(ck, j, n + 1, j, False)
                    else:
                        load_expert(ck, j, n, j - W1C, True)

            body_loads(0)
            with sp.Fori(1, NE - 1) as n:
                body_loads(n)
            tail = Chunks(PRO + W1C + PER * (NE - 1), 0)
            for j in range(W2C):
                sp.wait_ge(s_lo, tail.number(j) - RAW + 1)
                load_expert(tail, j, NE - 1, j, True)

            sp.wait_ge(s_tab, 3)
            def further(e, r, i):
                ck = Chunks(EXTRA, i)
                for j in range(PER):
                    sp.wait_ge(s_lo, ck.number(j) - RAW + 1)
                    load_expert(ck, j, e, j % W1C, j >= W1C)
                sp.wait_ge(s_sca, i * 16 + 16 * (NE + 1))
                sp.sem_inc(s_carry, 1)

            further_blocks(sp, further)
            sp.wait_ge(s_pc, PER * NE)
            sp.wait_ge(s_gat, 16 * (NE + 2))
            sp.wait_ge(s_sca, 16 * NE)
            sp.dma_start(raw[:, 3, 0:D], a["normf_g"].rearrange("(a n) -> a n", a=1).to_broadcast([P, D])).then_inc(s_gf, 16)
            y_rows = y_dram.rearrange("(t k) d -> t (k d)", k=TOPK)
            for t, (r, n) in enumerate(TILES):
                sp.dma_start(choices[t][0:n, :], y_rows[r:r + n, :]).then_inc(s_fy[t], 16)
            y_out = [(a["y_prompt"].rearrange("b t d -> (b t) d"), 128 * t) for t in range(4)] + [(a["y_sample"].rearrange("b t d -> (b t) d"), 0)]
            for t, (r, n) in enumerate(TILES):
                sp.wait_ge(s_fo, t + 1)
                dst, o = y_out[t]
                sp.dma_start(dst[o:o + n, :], raw[0:n, t // 2, D * (t % 2):D * (t % 2) + D]).then_inc(s_out, 16)
            sp.wait_ge(s_out, 16 * NT)
            sp.wait_ge(s_outp, 16 * 5)

        @block.gpsimd
        def _(pool):
            pool.memset(t_hi[:, :, NTOK:640].bitcast(F32), 0.0)
            pool.memset(t_lo[:, :, NTOK:640].bitcast(F32), 0.0)
            pool.memset(gate[:], 0.0)
            pool.memset(rank[:], -1.0)
            pool.memset(vals[:], 0.0).then_inc(s_pad, 1)

            pool.wait_ge(s_ze, LAST_UNIT[1])
            pool.dma_start(a["new_pool_prompt"][0, 0], u_nat[P - BUF:P, 3, :]).then_inc(s_ust, 16)
            pool.dma_start(a["new_pool_sample"][0, :, BUF - NS:BUF, :], u_smp[0:32, :]).then_inc(s_ust, 16)
            pool.dma_start(a["new_pool_sample"][0, :, 0:BUF - NS, :], a["state_pool"][0, :, NS:BUF, :]).then_inc(s_outp, 16)

            def store(nat, prompt, sample):
                pool.dma_start(a[prompt][0, 0].rearrange("(t p) h d -> p t (h d)", p=P), nat[:, 0:4, :]).then_inc(s_outp, 16)
                pool.dma_start(a[sample][0].rearrange("b t h d -> (b t) (h d)"), nat[0:32, 4, :]).then_inc(s_outp, 16)

            pool.wait_ge(s_ze, LAST_UNIT[5])
            store(k_nat, "new_k_prompt", "new_k_sample")
            pool.wait_ge(s_ze, LAST_UNIT[7])
            store(v_nat, "new_v_prompt", "new_v_sample")
            pool.wait_ge(s_a, 16)
            pool.wait_ge(s_pv, 16)
            pool.wait_ge(s_ate, 16)
            pool.wait_ge(s_outp, 16 * 5)
            pool.memset(p_cols, 0.0)
            pool.memset(q_blk, 0.0).then_inc(s_qb, 1)

            def reload_x(t, signal):
                src, r = x_in[t]
                n = TILES[t][1]
                pool.dma_start(h_res[0:n, SLOT_H[t], :], src[r:r + n, :]).then_inc(signal, 16)

            reload_x(0, s_xr[0])
            reload_x(1, s_xr[0])
            pool.wait_ge(s_qb, 2)
            pool.wait_ge(s_sss, NB * H)
            reload_x(2, s_xr[1])
            reload_x(3, s_xr[1])
            pool.dma_start(g2, a["norm2_g"].to_broadcast([P, D])).then_inc(s_late2, 16)
            pool.dma_start(rbias, a["router_b"].to_broadcast([P, NE])).then_inc(s_late2, 16)
            pool.dma_start(ar[:, A_TRI:A_TRI + 2 * P], a["c_tri"]).then_inc(s_late2, 16)
            pool.dma_start(rw, a["router_w"][0].rearrange("(k p) e -> p k e", p=P)).then_inc(s_late2, 16)
            pool.wait_ge(s_kp, 2 * NB * H)
            reload_x(4, s_xr[2])

            for t, (r, n) in enumerate(TILES):
                pool.wait_ge(s_h2, t + 1)
                if t:
                    pool.wait_ge(s_h2d, 16 * t)
                pool.dma_start(h2_dram[r:r + n, :], h2[0:n, t % 2, :]).then_inc(s_h2d, 16)
            pool.wait_ge(s_lge, NT)
            pool.wait_ge(s_tab, 3)
            pool.memset(xg, 0.0).then_inc(s_pool_c, 1)
            pool.wait_ge(s_pool_c, 1)
            pool.wait_ge(s_h2d, 16 * NT)

            def alone():
                pool.sem_inc(s_carry, 1)

            def make_onehot(m, column, rows, chain):
                if not isinstance(m, int) or m > 0:
                    pool.wait_ge(s_ix, m)
                alone()
                pool.tensor_copy(rank_c[:], rank[:, :, bass.ds(column, 1)].rearrange("p t a -> p (t a)")).then_inc(s_pool_c, 1)
                pool.tensor_copy(vals_c[:], vals[:, :, bass.ds(column, 1), :].rearrange("p t a b -> p t (a b)")).then_inc(s_pool_c, 1)
                pool.wait_ge(s_pool_c, chain + 2)
                alone()
                for t in range(NT):
                    last = pool.tensor_scalar(onehot[:, t, :], rows, rank_c[:, t:t + 1], None, ALU.is_equal)
                last.then_inc(s_ohd, 1)

            def gather(m, column, chain, before):
                pool.wait_ge(s_ixe, m + 1)
                if not isinstance(m, int) or m > 0:
                    pool.wait_ge(s_xt, before)
                    pool.wait_ge(s_gat, m * 16)
                alone()
                pool.tensor_copy(idx_g[:], idx[:, bass.ds(column, 1), 0]).then_inc(s_pool_c, 1)
                pool.wait_ge(s_pool_c, chain + 3)
                alone()
                pool.indirect_dma_start(out=xg, out_offset=None, in_=h2_dram,
                                        in_offset=bass.IndirectOffsetOnAxis(ap=idx_g[:, 0:1], axis=0),
                                        bounds_check=NTOK - 1, oob_is_err=False).then_inc(s_gat, 16)

            def gated(m, half):
                cols = slice(512 * half, 512 * half + 512)
                pool.wait_ge(s_l, m * 2 + (half + 1))
                alone()
                pool.tensor_scalar(lin[:, cols], lin[:, cols], 1.0, None, ALU.add).then_inc(s_t, 1)
                pool.wait_ge(s_s, m * 2 + (half + 1))
                pool.tensor_tensor(tmp[:, cols], glu[:, cols], sig[:, cols], ALU.mult).then_inc(s_t, 1)
                pool.wait_ge(s_t, m * 4 + (2 * half + 2))
                if not isinstance(m, int) or m > 0:
                    pool.wait_ge(s_at, m)
                pool.tensor_tensor(act[:, cols], tmp[:, cols], lin[:, cols], ALU.mult).then_inc(s_ac, 1)

            def scatter(m, column, chain):
                if not isinstance(m, int) or m > 0:
                    pool.wait_ge(s_sca, m * 16)
                alone()
                pool.tensor_copy(idx_s[:], idx[:, bass.ds(column, 1), 1]).then_inc(s_pool_c, 1)
                pool.wait_ge(s_pool_c, chain + 1)
                pool.wait_ge(s_ye, m + 1)
                alone()
                pool.indirect_dma_start(out=y_dram, out_offset=bass.IndirectOffsetOnAxis(ap=idx_s[:, 0:1], axis=0),
                                        in_=y_sb, in_offset=None,
                                        bounds_check=NTOK * TOPK - 1, oob_is_err=False).then_inc(s_sca, 16)

            for m in range(3):
                make_onehot(m, m, iota[:, 0:P], 1 + 3 * m)
                if m == 2:
                    gated(0, 0)
                    gated(0, 1)
                gather(m, m, 1 + 3 * m, m)
            make_onehot(3, 3, iota[:, 0:P], 10)
            gather(3, 3, 10, 3)
            gated(1, 0)
            gated(1, 1)
            with pool.Fori(1, NE - 1) as n:
                scatter(n - 1, n - 1, n * 4 + 9)
                make_onehot(n + 3, n + 3, iota[:, 0:P], n * 4 + 10)
                gather(n + 3, n + 3, n * 4 + 10, n + 3)
                gated(n + 1, 0)
                gated(n + 1, 1)
            scatter(NE - 2, NE - 2, 4 * NE + 5)
            scatter(NE - 1, NE - 1, 4 * NE + 6)

            def further(e, r, i):
                chain = i * 5 + (4 * NE + 8)
                pool.wait_ge(s_ix, i + (NE + 2))
                alone()
                pool.tensor_copy(slots, iota[:, bass.ds(r * P + P, P)]).then_inc(s_pool_c, 1)
                make_onehot(i + (NE + 2), e, slots, chain)
                gather(i + (NE + 2), SPARE, chain, i + (NE + 1))
                for half in range(2):
                    gated(i + NE, half)
                scatter(i + NE, SPARE, chain + 3)
                pool.wait_ge(s_sca, i * 16 + 16 * (NE + 1))
                pool.sem_inc(s_carry, 1)

            further_blocks(pool, further)

        @block.scalar
        def _(act_e):
            def gate_exp(t):
                n = TILES[t][1]
                act_e.wait_ge(s_gm, t + 1)
                act_e.activation(gate[0:n, t, :], top[0:n, 0:4], ACT.Exp, bias=st[0:n, 44:45], accum_out=st[0:n, 45:46]).then_inc(s_ge, 1)

            def split_hi(slot_raw, slot, loaded):
                act_e.wait_ge(s_raw[slot_raw], loaded)
                act_e.activation(hi[:, slot, :], raw[:, slot_raw, :], ACT.Copy).then_inc(s_hi, 1)

            def pro_hi(g):
                if g >= RING:
                    act_e.wait_ge(s_z, LAST_UNIT[g - RING])
                split_hi(0, g % RING, 16 * (g + 1))

            def norm1_sums(t):
                n = TILES[t][1]
                act_e.wait_ge(s_x[t % 2], 16 * (t // 2 + 1))
                act_e.activation(sq1[0:n, :], x_buf[0:n, t % 2, :], ACT.Square, accum_out=st[0:n, 2 + t:3 + t]).then_inc(s_ss, 1)
                act_e.wait_ge(s_ss, t + 1)
                act_e.activation(st[0:n, 8 + t:9 + t], st[0:n, 2 + t:3 + t], ACT.Sqrt, scale=1.0 / D, bias=eps[0:n]).then_inc(s_rt, 1)

            act_e.wait_ge(s_g1, 32)
            norm1_sums(0)
            for t, (_, n) in enumerate(TILES):
                if t + 1 < NT:
                    norm1_sums(t + 1)
                act_e.wait_ge(s_tp, t + 1)
                if t == 0:
                    act_e.wait_ge(s_pad, 1)
                src = ps[:, 2 * (t % 2):2 * (t % 2) + 2, :].rearrange("p b (k c) -> p (b k) c", c=P)[:, :, 0:n]
                act_e.activation(t_hi[:, :, P * t:P * t + n], src, ACT.Copy).then_inc(s_th, 1)
                if t < 3:
                    pro_hi(t)
            pro_hi(3)
            act_e.wait_ge(s_cst, 16 * 13)
            act_e.activation(bias_r[:], ar[0:2 * NE, 0:3 * D], ACT.Copy).then_inc(s_bh, 1)
            act_e.wait_ge(s_lam, 1)
            act_e.activation(st[:, 16:18], st[:, 14:16], ACT.Exp).then_inc(s_lame, 1)
            act_e.wait_ge(s_bh, 2)
            for i, (c, kind, t, part) in enumerate(UNITS):
                act_e.wait_ge(s_z, i + 1)
                bank = 4 + i % 4
                if kind == "q":
                    h = 2 * (c - 2) + t
                    n = 512 if part == 0 else 32
                    act_e.activation(q_t[:, h, 512 * part:512 * part + n], ps[:, bank, 0:n], ACT.Copy, scale=HD ** -0.5).then_inc(s_ze, 1)
                else:
                    n = TILES[t][1]
                    col = 256 * (c % 2)
                    dst = {"u": u_nat, "k": k_nat, "v": v_nat}[kind]
                    dst = u_smp[0:n, col:col + 256] if kind == "u" and t == 4 else dst[0:n, t, col:col + 256]
                    act_e.activation(dst, ps[0:n, bank, 0:256], ACT.Copy).then_inc(s_ze, 1)
                if i + 1 in LAST_UNIT:
                    pro_hi(LAST_UNIT.index(i + 1) + RING)
            def pool_diff(g):
                act_e.wait_ge(s_d, g + 1)
                if g >= 2:
                    act_e.wait_ge(s_po, g - 1)
                act_e.activation(d_t[g % 2][:, 0:512], ps[:, 2 * (g % 2), :], ACT.Copy)
                act_e.activation(d_t[g % 2][:, 512:544], ps[:, 2 * (g % 2) + 1, 0:32], ACT.Copy).then_inc(s_de, 1)

            def pool_hi(g):
                act_e.wait_ge(s_po, g + 1)
                b = 4 + 2 * (g % 2)
                act_e.activation(t_hi[:, g, 0:512], ps[:, b, :], ACT.Copy, scale=psc[:, g:g + 1])
                act_e.activation(t_hi[:, g, 512:544], ps[:, b + 1, 0:32], ACT.Copy, scale=psc[:, g:g + 1]).then_inc(s_ph, 1)

            act_e.wait_ge(s_late, 32)
            for g in range(4):
                pool_diff(g)
                if g >= 1:
                    pool_hi(g - 1)
            pool_hi(3)

            def o_root(i, n):
                act_e.wait_ge(s_os, i + 1)
                act_e.activation(st[0:n, 28:32], st[0:n, 28:32], ACT.Sqrt, scale=1.0 / P, bias=eps[0:n]).then_inc(s_or, 1)

            def o_hi(i):
                act_e.wait_ge(s_ot, i + 1)
                src = ps[:, 7, :].rearrange("p (h c) -> p h c", c=P)
                if i < 4:
                    act_e.activation(t_hi[:, 4:8, P * i:P * i + P], src, ACT.Copy).then_inc(s_oh_, 1)
                else:
                    act_e.activation(sample_cols(t_hi, i - 4), every_32(src), ACT.Copy).then_inc(s_oh_, 1)

            def weights_t(i):
                nk = P * (i // 4 + 1)
                act_e.wait_ge(s_atr, i + 1)
                if i >= 2:
                    act_e.wait_ge(s_pv, i - 1)
                act_e.activation(at_sb[:, i % 2, 0:nk], ps[:, 4 + i % 2, 0:nk], ACT.Copy).then_inc(s_ate, 1)

            for i in range(17):
                if i < 16:
                    nk = P * (i // 4 + 1)
                    act_e.wait_ge(s_mx, i + 1)
                    for c in range(2):
                        w = pr[:, 2 * (i % 2) + c, 0:nk]
                        e = act_e.activation(w, w, ACT.Exp, bias=st[:, 20 + 2 * (i % 2) + c:21 + 2 * (i % 2) + c],
                                             accum_out=st[:, 24 + 2 * (i % 2) + c:25 + 2 * (i % 2) + c])
                    e.then_inc(s_e, 1)
                if i >= 1:
                    weights_t(i - 1)
                    if i >= 5 and i % 4 == 1:
                        o_hi(i // 4 - 1)
                    if i % 4 == 0:
                        o_root(i // 4 - 1, P)
            o_hi(3)
            act_e.wait_ge(s_ust, 32)
            def sample_exp(t):
                act_e.wait_ge(s_smx, t + 1)
                act_e.activation(s_smp[:, t, :], s_smp[:, t, :], ACT.Exp, bias=st[:, 32 + t:33 + t], accum_out=st[:, 34 + t:35 + t]).then_inc(s_se, 1)

            for m in range(NB * H):
                act_e.wait_ge(s_kp, m + 1)
                if m >= 3:
                    act_e.wait_ge(s_sss, m - 2)
                act_e.activation(kt_s[:, m % 3, :], ps[:, m % 3, :], ACT.Copy).then_inc(s_kc, 1)
                if m == 20:
                    sample_exp(0)
            sample_exp(1)
            start = Chunks(PRO, 0)

            def norm2_sums(t):
                n = TILES[t][1]
                act_e.wait_ge(s_he, 4 * t + 4)
                act_e.activation(sq2[0:n, :], h_res[0:n, SLOT_H[t], :], ACT.Square, accum_out=st[0:n, 36 + t:37 + t]).then_inc(s_n2, 1)
                act_e.wait_ge(s_n2, t + 1)
                act_e.activation(st[0:n, 36 + t:37 + t], st[0:n, 36 + t:37 + t], ACT.Sqrt, scale=1.0 / D, bias=eps[0:n]).then_inc(s_r2, 1)

            def h2_out(t):
                n = TILES[t][1]
                act_e.wait_ge(s_h2t, t + 1)
                if t >= 2:
                    act_e.wait_ge(s_lg, t - 1)
                src = ps[:, 0:2, :].rearrange("p b (k c) -> p (b k) c", c=P)[:, :, 0:n]
                act_e.activation(h2_t[:, t % 2, :].rearrange("p (k c) -> p k c", c=P)[:, :, 0:n], src, ACT.Copy).then_inc(s_h2e, 1)

            o_root(4, P)
            norm2_sums(0)
            norm2_sums(1)
            o_hi(4)
            norm2_sums(2)
            h2_out(0)
            o_root(5, P)
            norm2_sums(3)
            o_hi(5)
            gate_exp(0)
            h2_out(1)
            norm2_sums(4)
            gate_exp(1)
            h2_out(2)
            h2_out(3)
            gate_exp(2)
            h2_out(4)
            gate_exp(3)
            gate_exp(4)

            def expert_hi(ck, j):
                act_e.wait_ge(s_pc, ck.number(j) - PRO - RING + 1)
                split_hi(ck.raw_slot(j), ck.slot(j), ck.loaded(j))

            def rows_hi(m, src_sem, done, dst):
                act_e.wait_ge(src_sem, m + 1)
                src = ps[:, 6:8, :].rearrange("p b (k c) -> p (b k) c", c=P)
                act_e.activation(dst, src, ACT.Copy).then_inc(done, 1)

            def selector(dst, e):
                return act_e.activation(dst[:], cst[0:2 * NE, bass.ds(C_EYE + e, 1)].to_broadcast([2 * NE, P]), ACT.Copy)

            def sigmoid(m, half):
                cols = slice(512 * half, 512 * half + 512)
                act_e.wait_ge(s_g, m * 2 + (half + 1))
                if not isinstance(m, int) or m > 0:
                    act_e.wait_ge(s_ac, m * 2)
                act_e.activation(sig[:, cols], glu[:, cols], ACT.Sigmoid, scale=ALPHA).then_inc(s_s, 1)

            def y_out(m, done):
                act_e.wait_ge(s_pc, done)
                if not isinstance(m, int) or m > 0:
                    act_e.wait_ge(s_sca, m * 16)
                act_e.activation(y_sb, ps[:, 4:6, :].rearrange("p b n -> p (b n)"), ACT.Copy).then_inc(s_ye, 1)

            act_e.wait_ge(s_w, 20)
            for j in range(RING):
                split_hi(start.raw_slot(j), start.slot(j), start.loaded(j))
            rows_hi(0, s_xt, s_xh, x_hi)
            selector(sel_w1, 0).then_inc(s_bs, 1)
            for j in range(RING, W1C):
                expert_hi(start, j)
            head = Chunks(PRO + W1C, 0)
            for j in range(4):
                expert_hi(head, j)
            act_e.wait_ge(s_pc, W1C)
            rows_hi(1, s_xt, s_xh, x_hi)
            sigmoid(0, 0)
            sigmoid(0, 1)

            def body(n, j0=0):
                ck = Chunks(PRO + W1C, n)
                for j in range(j0, 4):
                    expert_hi(ck, j)
                    if j == 2 and not (isinstance(n, int) and n == 0):
                        y_out(n - 1, ck.number(0) - PRO)
                rows_hi(n, s_at, s_ah, act_hi)
                selector(sel_w1, n + 1)
                selector(sel_w2, n).then_inc(s_bs, 1)
                for j in range(4, PER):
                    expert_hi(ck, j)
                act_e.wait_ge(s_pc, ck.number(W1C) - PRO)
                rows_hi(n + 2, s_xt, s_xh, x_hi)
                sigmoid(n + 1, 0)
                sigmoid(n + 1, 1)

            body(0, 4)
            with act_e.Fori(1, NE - 1) as n:
                body(n)
            tail = Chunks(PRO + W1C + PER * (NE - 1), 0)
            for j in range(3):
                expert_hi(tail, j)
            y_out(NE - 2, tail.number(0) - PRO)
            rows_hi(NE - 1, s_at, s_ah, act_hi)
            selector(sel_w2, NE - 1).then_inc(s_bs, 1)
            expert_hi(tail, 3)
            y_out(NE - 1, PER * NE)

            act_e.wait_ge(s_tab, 3)
            def further(e, r, i):
                ck = Chunks(EXTRA, i)
                rows_hi(i + (NE + 1), s_xt, s_xh, x_hi)
                selector(sel_w1, e)
                selector(sel_w2, e).then_inc(s_bs, 1)
                for j in range(W1C):
                    expert_hi(ck, j)
                sigmoid(i + NE, 0)
                sigmoid(i + NE, 1)
                rows_hi(i + NE, s_at, s_ah, act_hi)
                for j in range(W1C, PER):
                    expert_hi(ck, j)
                y_out(i + NE, ck.number(PER) - PRO)
                act_e.wait_ge(s_sca, i * 16 + 16 * (NE + 1))
                act_e.sem_inc(s_carry, 1)

            further_blocks(act_e, further)
            for t, (_, n) in enumerate(TILES):
                act_e.wait_ge(s_fs, t + 1)
                act_e.activation(raw[0:n, 3, D:2 * D], h_res[0:n, SLOT_H[t], :], ACT.Square, accum_out=st[0:n, 50 + t:51 + t]).then_inc(s_fr, 1)
                act_e.wait_ge(s_fr, 2 * t + 1)
                act_e.activation(st[0:n, 50 + t:51 + t], st[0:n, 50 + t:51 + t], ACT.Sqrt, scale=1.0 / D, bias=eps[0:n]).then_inc(s_fr, 1)

        @block.vector
        def _(v):
            chain = [0]

            def link(ins):
                chain[0] += 1
                ins.then_inc(s_dve, 1)
                v.wait_ge(s_dve, chain[0])

            def split_lo(slot_raw, slot, hi_done):
                v.wait_ge(s_hi, hi_done)
                v.tensor_tensor(lo[:, slot, :], raw[:, slot_raw, :], hi[:, slot, :].bitcast(F32), ALU.subtract).then_inc(s_lo, 1)

            def pro_lo(g):
                split_lo(0, g % RING, g + 1)

            def norm1_rows(t):
                n = TILES[t][1]
                v.wait_ge(s_rt, t + 1)
                link(v.reciprocal(st[0:n, 2 + t:3 + t], st[0:n, 8 + t:9 + t]))
                if t >= 2:
                    v.wait_ge(s_tp, t - 1)
                v.scalar_tensor_tensor(out=xn[t % 2][0:n, :], in0=x_buf[0:n, t % 2, :], scalar=st[0:n, 2 + t:3 + t], in1=g1[0:n, :],
                                       op0=ALU.mult, op1=ALU.mult).then_inc(s_xn, 1)

            v.wait_ge(s_g1, 32)
            norm1_rows(0)
            for t, (_, n) in enumerate(TILES):
                if t + 1 < NT:
                    norm1_rows(t + 1)
                v.wait_ge(s_th, t + 1)
                src = ps[:, 2 * (t % 2):2 * (t % 2) + 2, :].rearrange("p b (k c) -> p (b k) c", c=P)[:, :, 0:n]
                v.tensor_tensor(t_lo[:, :, P * t:P * t + n], src, t_hi[:, :, P * t:P * t + n].bitcast(F32), ALU.subtract).then_inc(s_tl, 1)
                if t < 3:
                    pro_lo(t)
            pro_lo(3)
            v.wait_ge(s_cst, 16 * 13)
            v.wait_ge(s_bh, 1)
            v.scalar_tensor_tensor(out=bias_r[:], in0=bias_r[:].bitcast(F32), scalar=cst[0:2 * NE, C_NEGM:C_NEGM + 1],
                                   in1=ar[0:2 * NE, 0:3 * D], op0=ALU.mult, op1=ALU.add).then_inc(s_bh, 1)
            lv = lamv.rearrange("p (a b n) -> p a b n", a=2, b=2)
            link(v.tensor_tensor(lv[:, :, 0, :], lv[:, :, 0, :], lv[:, :, 1, :], ALU.mult))
            v.tensor_reduce(st[:, 14:16], lv[:, :, 0, :], AX, ALU.add).then_inc(s_lam, 1)
            v.wait_ge(s_lame, 1)
            link(v.tensor_tensor(neglam, st[:, 17:18], st[:, 16:17], ALU.subtract))
            link(v.tensor_scalar(neglam, neglam, LAMBDA_INIT, None, ALU.subtract))
            link(v.tensor_scalar(st[:, 18:19], cst[:, C_M1:C_M1 + 1], neglam, cst[:, C_M0:C_M0 + 1], ALU.mult, ALU.add))
            link(v.tensor_scalar(gsub, gsub, 1.0 - LAMBDA_INIT, None, ALU.mult))

            def k_out(hp):
                v.wait_ge(s_kt, hp + 1)
                for hh in range(2):
                    v.tensor_copy(k_t[:, 2 * hp + hh, 0:512], ps[:, 2 * hh, :])
                    last = v.tensor_copy(k_t[:, 2 * hp + hh, 512:544], ps[:, 2 * hh + 1, 0:32])
                last.then_inc(s_kte, 1)

            for g in range(RING, 10):
                pro_lo(g)
            k_out(0)
            pro_lo(10)
            k_out(1)
            pro_lo(11)

            for g in range(4):
                v.wait_ge(s_ph, g + 1)
                b = 4 + 2 * (g % 2)
                v.scalar_tensor_tensor(out=t_lo[:, g, 0:512], in0=ps[:, b, :], scalar=psc[:, g:g + 1],
                                       in1=t_hi[:, g, 0:512].bitcast(F32), op0=ALU.mult, op1=ALU.subtract)
                v.scalar_tensor_tensor(out=t_lo[:, g, 512:544], in0=ps[:, b + 1, 0:32], scalar=psc[:, g:g + 1],
                                       in1=t_hi[:, g, 512:544].bitcast(F32), op0=ALU.mult, op1=ALU.subtract).then_inc(s_pl, 1)

            def o_norm(i, n):
                src = ps[0:n, 6, :].rearrange("p (h c) -> p h c", c=P)
                ov = o_nat[0:n].rearrange("p (h c) -> p h c", c=P)
                if i > 0:
                    v.wait_ge(s_ot, i)
                link(v.tensor_copy(o_nat[0:n], ps[0:n, 6, :]))
                link(v.tensor_tensor(o_sq[0:n], o_nat[0:n], o_nat[0:n], ALU.mult))
                v.tensor_reduce(st[0:n, 28:32], o_sq[0:n].rearrange("p (h c) -> p h c", c=P), AX, ALU.add).then_inc(s_os, 1)
                v.wait_ge(s_or, i + 1)
                link(v.reciprocal(st[0:n, 28:32], st[0:n, 28:32]))
                link(v.tensor_tensor(ov, src, st[0:n, 28:32].unsqueeze(2).to_broadcast([n, 4, P]), ALU.mult))
                v.tensor_tensor(ov, ov, gsub[0:n].unsqueeze(1).to_broadcast([n, 4, P]), ALU.mult).then_inc(s_on, 1)

            def o_lo(i):
                v.wait_ge(s_oh_, i + 1)
                src = ps[:, 7, :].rearrange("p (h c) -> p h c", c=P)
                if i < 4:
                    v.tensor_tensor(t_lo[:, 4:8, P * i:P * i + P], src, t_hi[:, 4:8, P * i:P * i + P].bitcast(F32), ALU.subtract).then_inc(s_ol, 1)
                else:
                    v.tensor_tensor(sample_cols(t_lo, i - 4), every_32(src), sample_cols(t_hi, i - 4).bitcast(F32), ALU.subtract).then_inc(s_ol, 1)

            def bias_max(i):
                qt, h = i // 4, i % 4
                nk = P * (qt + 1)
                v.wait_ge(s_sc, i + 1)
                p2 = 2 * (i % 2)
                for c in range(2):
                    e = v.scalar_tensor_tensor(out=pr[:, p2 + c, 0:nk], in0=dist[:, 384 - P * qt:384 - P * qt + nk], scalar=-SLOPES[h],
                                               in1=ps[:, p2 + c, 0:nk], op0=ALU.mult, op1=ALU.add)
                e.then_inc(s_sb, 1)
                v.wait_ge(s_sb, i + 1)
                v.tensor_reduce(st[:, 20 + p2:22 + p2], pr[:, p2:p2 + 2, 0:nk], AX, ALU.max, negate=True).then_inc(s_mx, 1)

            def weights(i):
                nk = P * (i // 4 + 1)
                p2 = 2 * (i % 2)
                v.wait_ge(s_e, i + 1)
                link(v.reciprocal(st[:, 24 + p2:26 + p2], st[:, 24 + p2:26 + p2]))
                link(v.tensor_tensor(st[:, 25 + p2:26 + p2], st[:, 25 + p2:26 + p2], neglam, ALU.mult))
                if i >= 2:
                    v.wait_ge(s_atr, i - 1)
                link(v.tensor_scalar(aa[:, i % 2, 0:nk], pr[:, p2, 0:nk], st[:, 24 + p2:25 + p2], None, ALU.mult))
                v.scalar_tensor_tensor(out=aa[:, i % 2, 0:nk], in0=pr[:, p2 + 1, 0:nk], scalar=st[:, 25 + p2:26 + p2],
                                       in1=aa[:, i % 2, 0:nk], op0=ALU.mult, op1=ALU.add).then_inc(s_a, 1)
                v.wait_ge(s_a, i + 1)

            v.wait_ge(s_outp, 16 * 5)
            v.wait_ge(s_ust, 32)
            bias_max(0)
            for i in range(16):
                if i + 1 < 16:
                    bias_max(i + 1)
                weights(i)
                if i % 4 == 0 and i >= 4:
                    v.wait_ge(s_pv, i)
                    o_norm(i // 4 - 1, P)
                if i % 4 == 2 and i >= 6:
                    o_lo(i // 4 - 1)
            v.wait_ge(s_pv, 16)
            o_norm(3, P)
            o_lo(3)

            v.wait_ge(s_qb, 1)
            for h in range(H):
                for c in range(2):
                    rows = slice(HD * c, HD * c + HD)
                    dst = q_blk.rearrange("p (b h) n -> p b h n", h=H)[rows, :, h, 8 * h + 4 * c:8 * h + 4 * c + 4]
                    last = v.tensor_copy(dst, q_t[rows, h, 512:544].rearrange("p (b q) -> p b q", q=NS))
            last.then_inc(s_qb, 1)
            def sample_softmax(t):
                v.wait_ge(s_sss, 16 * (t + 1))
                v.scalar_tensor_tensor(out=s_smp[:, t, 0:512], in0=dist_s[:, 0:512], scalar=cst[:, C_SLOPE:C_SLOPE + 1],
                                       in1=ps[:, 4 + t, :], op0=ALU.mult, op1=ALU.add)
                link(v.scalar_tensor_tensor(out=s_smp[:, t, 512:544], in0=dist_s[:, 512 + 32 * t:544 + 32 * t], scalar=cst[:, C_SLOPE:C_SLOPE + 1],
                                            in1=ps[:, 3 + 3 * t, 0:32], op0=ALU.mult, op1=ALU.add))
                v.tensor_reduce(st[:, 32 + t:33 + t], s_smp[:, t, :], AX, ALU.max, negate=True).then_inc(s_smx, 1)
                v.wait_ge(s_se, t + 1)
                link(v.reciprocal(st[:, 34 + t:35 + t], st[:, 34 + t:35 + t]))
                link(v.tensor_tensor(st[:, 34 + t:35 + t], st[:, 34 + t:35 + t], st[:, 18:19], ALU.mult))
                v.tensor_scalar(s_smp[:, t, :], s_smp[:, t, :], st[:, 34 + t:35 + t], None, ALU.mult).then_inc(s_sa, 1)

            def sample_weights(t):
                v.wait_ge(s_ptr, t + 1)
                w = ps[:, 0 + t, :].rearrange("p (k x c q) -> p k x c q", k=4, c=2, q=NS)
                for k in range(4):
                    e = v.tensor_copy(p_t[:, t, k, :].rearrange("p (x q) -> p x q", q=NS), w[:, k, :, 0, :])
                wn = ps[0:32, 2 + 3 * t, 0:P].rearrange("p (x c q) -> p x c q", c=2, q=NS)
                pn = p_t[0:32, t, 4, :].rearrange("p (x q) -> p x q", q=NS)
                link(v.tensor_copy(pn, wn[:, :, 0, :]))
                for k in range(4):
                    v.tensor_tensor(p_t[:, t, k, :].rearrange("p (x q) -> p x q", q=NS), p_t[:, t, k, :].rearrange("p (x q) -> p x q", q=NS), w[:, k, :, 1, :], ALU.add)
                v.tensor_tensor(pn, pn, wn[:, :, 1, :], ALU.add).then_inc(s_pe, 1)

            def residual(t):
                n = TILES[t][1]
                v.wait_ge(s_xr[t // 2], 16 if t == 4 else 32)
                for c in range(4):
                    i = 4 * t + c
                    v.wait_ge(s_w, i + 1)
                    dst = h_res[0:n, SLOT_H[t], 256 * c:256 * c + 256]
                    v.tensor_tensor(dst, ps[0:n, 3 + i % 2, 0:256], dst, ALU.add).then_inc(s_he, 1)

            def norm2(t):
                n = TILES[t][1]
                v.wait_ge(s_r2, t + 1)
                link(v.reciprocal(st[0:n, 36 + t:37 + t], st[0:n, 36 + t:37 + t]))
                if t >= 2:
                    v.wait_ge(s_h2t, t - 1)
                    v.wait_ge(s_h2d, 16 * (t - 1))
                v.scalar_tensor_tensor(out=h2[0:n, t % 2, :], in0=h_res[0:n, SLOT_H[t], :], scalar=st[0:n, 36 + t:37 + t], in1=g2[0:n, :],
                                       op0=ALU.mult, op1=ALU.mult).then_inc(s_h2, 1)

            def choose(t):
                n = TILES[t][1]
                v.wait_ge(s_lg, t + 1)
                if t >= 1:
                    v.wait_ge(s_ge, t)
                v.tensor_tensor(lgt[0:n], ps[0:n, 2 + 3 * (t % 2), 0:NE], rbias[0:n], ALU.add).then_inc(s_lge, 1)
                v.wait_ge(s_lge, t + 1)
                link(v.max(top[0:n], lgt[0:n]))
                v.tensor_scalar(st[0:n, 44:45], top[0:n, 0:1], -1.0, None, ALU.mult).then_inc(s_gm, 1)
                link(v.max_index(topi[0:n], top[0:n], lgt[0:n]))
                link(v.tensor_copy(topf[0:n], topi[0:n, 0:4]))
                link(v.tensor_tensor(oh4[0:n], iota[0:n, 0:NE].unsqueeze(1).to_broadcast([n, 4, NE]),
                                     topf[0:n].unsqueeze(2).to_broadcast([n, 4, NE]), ALU.is_equal))
                v.tensor_reduce(sel[0:n, t, :], oh4[0:n].rearrange("p k e -> p e k"), AX, ALU.add)
                link(v.tensor_tensor(kv4[0:n], oh4[0:n], iota[0:n, 0:4].unsqueeze(2).to_broadcast([n, 4, NE]), ALU.mult))
                link(v.tensor_reduce(vals[0:n, t, 0:NE, 1], kv4[0:n].rearrange("p k e -> p e k"), AX, ALU.add))
                link(v.tensor_scalar(topf[0:n, 0:1], cst[0:n, C_TOK + t:C_TOK + t + 1], 4.0, 1.0, ALU.mult, ALU.add))
                v.tensor_scalar(vals[0:n, t, 0:NE, 1], vals[0:n, t, 0:NE, 1], topf[0:n, 0:1], None, ALU.add)
                link(v.tensor_scalar(vals[0:n, t, 0:NE, 0], ones[0:n, 0:NE], cst[0:n, C_TOK + t:C_TOK + t + 1], None, ALU.add))
                v.wait_ge(s_ge, t + 1)
                link(v.reciprocal(st[0:n, 46:47], st[0:n, 45:46]))
                v.tensor_scalar(gate[0:n, t, :], gate[0:n, t, :], st[0:n, 46:47], None, ALU.mult).then_inc(s_sel, 1)

            sample_softmax(0)
            sample_softmax(1)
            sample_weights(0)
            residual(0)
            v.wait_ge(s_kp, NB * H + 4 * H)
            o_norm(4, P)
            sample_weights(1)
            residual(1)
            start = Chunks(PRO, 0)
            v.wait_ge(s_late2, 64)
            link(v.memset(sel, 0.0))
            norm2(0)
            o_lo(4)
            residual(2)
            norm2(1)
            v.wait_ge(s_kp, 2 * NB * H)
            o_norm(5, P)
            residual(3)
            o_lo(5)
            choose(0)
            norm2(2)
            residual(4)
            norm2(3)
            choose(1)
            norm2(4)
            choose(2)
            choose(3)
            choose(4)
            v.wait_ge(s_rk, 1)
            for t in range(NT):
                link(v.scalar_tensor_tensor(out=rank[:, t, 0:NE], in0=ps[:, t, 0:NE], scalar=1.0, in1=sel[:, t, :], op0=ALU.add, op1=ALU.mult))
                last = v.tensor_scalar(rank[:, t, 0:NE], rank[:, t, 0:NE], -1.0, None, ALU.add)
            last.then_inc(s_tab, 1)
            v.tensor_copy(cnt[0:1, 0:NE], ps[0:1, 5, 0:NE]).then_inc(s_tab, 1)
            link(v.tensor_reduce(cntf[0:1, 0:1], ps[0:1, 5, 0:NE], AX, ALU.max))
            v.tensor_copy(cnt[0:1, NE:NE + 1], cntf[0:1, 0:1]).then_inc(s_tab, 1)
            v.wait_ge(s_tab, 3)

            def expert_lo(ck, j):
                split_lo(ck.raw_slot(j), ck.slot(j), ck.number(j + 1))

            def indices(m, column, link_at):
                v.wait_ge(s_ix, m + 1)
                v.tensor_scalar(unused[:], ps[:, 6, 0:2], 0.0, UNUSED, ALU.is_equal, ALU.mult).then_inc(s_dve, 1)
                v.wait_ge(s_dve, link_at + 1)
                v.scalar_tensor_tensor(out=idx[:, bass.ds(column, 1), :].rearrange("p a b -> p (a b)"), in0=ps[:, 6, 0:2], scalar=-1.0, in1=unused[:],
                                       op0=ALU.add, op1=ALU.add).then_inc(s_ixe, 1)

            def rows_lo(m, hi_sem, done, dst, dst_hi):
                v.wait_ge(hi_sem, m + 1)
                src = ps[:, 6:8, :].rearrange("p b (k c) -> p (b k) c", c=P)
                v.tensor_tensor(dst, src, dst_hi.bitcast(F32), ALU.subtract).then_inc(done, 1)

            def clamp(m, half, w1_done):
                cols = slice(512 * half, 512 * half + 512)
                src = ps[:, 2 * half:2 * half + 2, :].rearrange("p b (n two) -> p two (b n)", two=2)
                v.wait_ge(s_pc, w1_done)
                if not isinstance(m, int) or m > 0:
                    v.wait_ge(s_ac, m * 2)
                v.tensor_scalar(glu[:, cols], src[:, 0, :], LIMIT, None, ALU.min).then_inc(s_g, 1)
                v.tensor_scalar(lin[:, cols], src[:, 1, :], LIMIT, -LIMIT, ALU.min, ALU.max).then_inc(s_l, 1)

            base = chain[0]
            indices(0, 0, base)
            for j in range(RING):
                expert_lo(start, j)
            rows_lo(0, s_xh, s_xl, x_lo, x_hi)
            indices(1, 1, base + 1)
            for j in range(RING, W1C):
                expert_lo(start, j)
            head = Chunks(PRO + W1C, 0)
            for j in range(3):
                expert_lo(head, j)
            clamp(0, 0, W1C)
            clamp(0, 1, W1C)
            expert_lo(head, 3)
            rows_lo(1, s_xh, s_xl, x_lo, x_hi)
            indices(2, 2, base + 2)

            def body(n, j0=0):
                ck = Chunks(PRO + W1C, n)
                for j in range(j0, 4):
                    expert_lo(ck, j)
                rows_lo(n, s_ah, s_al, act_lo, act_hi)
                expert_lo(ck, 4)
                indices(n + 3, n + 3, n + (base + 3))
                for j in range(5, 11):
                    expert_lo(ck, j)
                clamp(n + 1, 0, ck.number(W1C) - PRO)
                clamp(n + 1, 1, ck.number(W1C) - PRO)
                expert_lo(ck, 11)
                rows_lo(n + 2, s_xh, s_xl, x_lo, x_hi)

            body(0, 4)
            with v.Fori(1, NE - 1) as n:
                body(n)
            tail = Chunks(PRO + W1C + PER * (NE - 1), 0)
            for j in range(3):
                expert_lo(tail, j)
            rows_lo(NE - 1, s_ah, s_al, act_lo, act_hi)
            expert_lo(tail, 3)

            after = base + NE + 2
            def further(e, r, i):
                ck = Chunks(EXTRA, i)
                indices(i + (NE + 2), SPARE, i + after)
                rows_lo(i + (NE + 1), s_xh, s_xl, x_lo, x_hi)
                for j in range(W1C):
                    expert_lo(ck, j)
                for half in range(2):
                    clamp(i + NE, half, ck.number(W1C) - PRO)
                rows_lo(i + NE, s_ah, s_al, act_lo, act_hi)
                for j in range(W1C, PER):
                    expert_lo(ck, j)
                v.wait_ge(s_sca, i * 16 + 16 * (NE + 1))
                v.sem_inc(s_carry, 1)

            further_blocks(v, further)
            v.wait_ge(s_gf, 16)
            for t, (_, n) in enumerate(TILES):
                v.wait_ge(s_fy[t], 16)
                rows = choices[t].rearrange("p (k d) -> p k d", k=TOPK)
                h = h_res[0:n, SLOT_H[t], :]
                for k in range(TOPK):
                    e = v.scalar_tensor_tensor(out=h, in0=rows[0:n, k, :], scalar=gate[0:n, t, k:k + 1], in1=h, op0=ALU.mult, op1=ALU.add)
                    if k < TOPK - 1:
                        e.then_inc(s_fc, 1)
                        v.wait_ge(s_fc, 4 * t + k + 1)
                e.then_inc(s_fs, 1)
                v.wait_ge(s_fr, 2 * t + 2)
                v.reciprocal(st[0:n, 50 + t:51 + t], st[0:n, 50 + t:51 + t]).then_inc(s_fc, 1)
                v.wait_ge(s_fc, 4 * t + 4)
                v.scalar_tensor_tensor(out=raw[0:n, t // 2, D * (t % 2):D * (t % 2) + D], in0=h, scalar=st[0:n, 50 + t:51 + t],
                                       in1=raw[0:n, 3, 0:D], op0=ALU.mult, op1=ALU.mult).then_inc(s_fo, 1)

        @block.tensor
        def _(pe):
            pe.wait_ge(s_g1, 32)
            def x_transposed(t):
                n = TILES[t][1]
                pe.wait_ge(s_xn, t + 1)
                if t >= 2:
                    pe.wait_ge(s_tl, t - 1)
                for k in range(KT):
                    last = pe.transpose(ps[:, 2 * (t % 2) + k // 4, P * (k % 4):P * (k % 4) + n], xn[t % 2][0:n, P * k:P * k + P], ident[0:n, 0:n])
                last.then_inc(s_tp, 1)

            def three(out, lhs, rhs, start, stop):
                for q, (l, r) in enumerate(((lhs[0], rhs[0]), (lhs[0], rhs[1]), (lhs[1], rhs[0]))):
                    last = pe.matmul(out, l, r, start=start and q == 0, stop=stop and q == 2)
                return last

            def k_transposes(hp):
                pe.wait_ge(s_ze, LAST_UNIT[4 + hp])
                if hp:
                    pe.wait_ge(s_kte, 1)
                for hh in range(2):
                    cols = slice(P * (2 * hp + hh), P * (2 * hp + hh) + P)
                    for t in range(4):
                        pe.transpose(ps[:, 2 * hh, P * t:P * t + P], k_nat[:, t, cols], ident)
                    last = pe.transpose(ps[:, 2 * hh + 1, 0:32], k_nat[0:32, 4, cols], ident[0:32, 0:32])
                last.then_inc(s_kt, 1)

            wv = [[r[:, s, :].rearrange("p (k n) -> p k n", k=KT) for s in range(RING)] for r in (hi, lo)]
            x_transposed(0)
            x_transposed(1)
            for i, (c, kind, t, part) in enumerate(UNITS):
                pe.wait_ge(s_lo, c + 1)
                if i < NT:
                    pe.wait_ge(s_tl, i + 1)
                if i >= 4:
                    pe.wait_ge(s_ze, i - 3)
                bank = 4 + i % 4
                w = [wv[0][c % RING], wv[1][c % RING]]
                for k in range(KT):
                    if kind == "q":
                        n = 512 if part == 0 else 32
                        last = three(ps[:, bank, 0:n], [y[:, k, P * t:P * t + P] for y in w],
                                     [y[:, k, 512 * part:512 * part + n] for y in (t_hi, t_lo)], k == 0, k == KT - 1)
                    else:
                        last = three(ps[:, bank, 0:256], [y[:, k, P * t:P * t + P] for y in (t_hi, t_lo)],
                                     [y[:, k, :] for y in w], k == 0, k == KT - 1)
                last.then_inc(s_z, 1)
                if i + 2 < NT:
                    x_transposed(i + 2)
                if i + 1 == LAST_UNIT[5]:
                    k_transposes(0)
                if i + 1 == LAST_UNIT[6]:
                    k_transposes(1)

            def diff(g):
                if g >= 2:
                    pe.wait_ge(s_de, g - 1)
                b = 2 * (g % 2)
                ch = slice(P * g, P * g + P)
                for j in range(4):
                    out = ps[:, b, P * j:P * j + P]
                    if j:
                        pe.matmul(out, u_nat[:, j - 1, ch], band[:, g, 2, :], start=True, stop=False)
                    pe.matmul(out, u_nat[:, j, ch], band[:, g, 1 if j else 0, :], start=not j, stop=True)
                pe.matmul(ps[:, b + 1, 0:32], state[0:NB * BUF, ch], sband[0:NB * BUF, g, 0, :], start=True, stop=False)
                pe.matmul(ps[:, b + 1, 0:32], u_smp[0:32, ch], sband[0:32, g, 1, :], start=False, stop=True).then_inc(s_d, 1)

            def linear(g):
                pe.wait_ge(s_de, g + 1)
                if g >= 2:
                    pe.wait_ge(s_pl, g - 1)
                b = 4 + 2 * (g % 2)
                pe.matmul(ps[:, b, :], pw[:, g, :], d_t[g % 2][:, 0:512], start=True, stop=True)
                pe.matmul(ps[:, b + 1, 0:32], pw[:, g, :], d_t[g % 2][:, 512:544], start=True, stop=True).then_inc(s_po, 1)

            pe.wait_ge(s_late, 32)
            pe.wait_ge(s_kte, 2)
            pe.wait_ge(s_ze, len(UNITS))
            diff(0)
            for g in range(1, 4):
                diff(g)
                linear(g - 1)
            linear(3)

            def scores(i):
                qt, h = i // 4, i % 4
                nk = P * (qt + 1)
                if i >= 2:
                    pe.wait_ge(s_sb, i - 1)
                for c in range(2):
                    rows = slice(HD * c, HD * c + HD)
                    last = pe.matmul(ps[:, 2 * (i % 2) + c, 0:nk], q_t[rows, h, P * qt:P * qt + P], k_t[rows, h, 0:nk], start=True, stop=True)
                last.then_inc(s_sc, 1)

            def o_transposes(i, n):
                pe.wait_ge(s_on, i + 1)
                if i:
                    pe.wait_ge(s_ol, i)
                for h in range(H):
                    last = pe.transpose(ps[:, 7, P * h:P * h + n], o_nat[0:n, P * h:P * h + P], ident[0:n, 0:n])
                last.then_inc(s_ot, 1)

            pe.wait_ge(s_pl, 4)
            scores(0)
            scores(1)
            for i in range(16):
                qt, h = i // 4, i % 4
                pe.wait_ge(s_a, i + 1)
                if i >= 2:
                    pe.wait_ge(s_ate, i - 1)
                for k in range(qt + 1):
                    last = pe.transpose(ps[:, 4 + i % 2, P * k:P * k + P], aa[:, i % 2, P * k:P * k + P], ident)
                last.then_inc(s_atr, 1)
                if i + 2 < 16:
                    scores(i + 2)
                if h == 0 and qt:
                    o_transposes(qt - 1, P)
                pe.wait_ge(s_ate, i + 1)
                for k in range(qt + 1):
                    last = pe.matmul(ps[:, 6, P * h:P * h + P], at_sb[:, i % 2, P * k:P * k + P], v_nat[:, k, P * h:P * h + P], start=k == 0, stop=k == qt)
                last.then_inc(s_pv, 1)
            o_transposes(3, P)

            def page_transposes(m):
                b, h = m // H, m % H
                if h == 0:
                    pe.wait_ge(s_pg[b % 3], 64 * (b // 3 + 1))
                if m >= 3:
                    pe.wait_ge(s_kc, m - 2)
                for k in range(PAGES):
                    last = pe.transpose(ps[:, m % 3, P * k:P * k + P], page[:, PAGES * (b % 3) + k, P * h:P * h + P], ident)
                last.then_inc(s_kp, 1)

            pe.wait_ge(s_qb, 2)
            pe.wait_ge(s_ol, 4)
            page_transposes(0)
            for m in range(NB * H):
                b, h = m // H, m % H
                if m + 1 < NB * H:
                    page_transposes(m + 1)
                pe.wait_ge(s_kc, m + 1)
                rows = slice(32 * (b % 4), 32 * (b % 4) + 32)
                pe.matmul(ps[rows, 4 + b // 4, :], q_blk[:, m, :], kt_s[:, m % 3, :], start=h == 0, stop=h == H - 1,
                          tile_position=(0, 32 * (b % 4)))
                pe.matmul(ps[rows, 3 + 3 * (b // 4), 0:32], q_blk[:, m, :], k_t[:, h, 512:544], start=h == 0, stop=h == H - 1,
                          tile_position=(0, 32 * (b % 4))).then_inc(s_sss, 1)
            def sample_transposes(t):
                pe.wait_ge(s_sa, t + 1)
                pe.wait_ge(s_kc, NB * H)
                for k in range(PAGES):
                    pe.transpose(ps[:, t, P * k:P * k + P], s_smp[:, t, P * k:P * k + P], ident)
                pe.transpose(ps[0:32, 2 + 3 * t, 0:P], s_smp[:, t, 512:544], ident).then_inc(s_ptr, 1)

            def sample_values(b):
                t, s = b // 4, NB + b
                pe.wait_ge(s_pe, t + 1)
                pe.wait_ge(s_pg[s % 3], 64 * (s // 3 + 1))
                if b % 4 == 0:
                    pe.wait_ge(s_on, 4 + t)
                for h in range(H):
                    x = 5 * 64 * t + NS * (H * (b % 4) + h)
                    rows = slice(32 * (b % 4), 32 * (b % 4) + 32)
                    out = ps[rows, 6, P * h:P * h + P]
                    for k in range(PAGES):
                        pe.matmul(out, p_cols[:, x + 64 * k:x + 64 * k + 32], page[:, PAGES * (s % 3) + k, P * h:P * h + P],
                                  start=k == 0, stop=False, tile_position=(0, 32 * (b % 4)))
                    pe.matmul(out, p_cols[0:32, x + 256:x + 288], v_nat[0:32, 4, P * h:P * h + P],
                              start=False, stop=True, tile_position=(0, 32 * (b % 4))).then_inc(s_kp, 1)

            def out_product(t):
                pe.wait_ge(s_ol, t + 1 if t < 4 else 6)
                for c in range(4):
                    i = 4 * t + c
                    if t == 0:
                        pe.wait_ge(s_lo, 8 + c + 1)
                    if i >= 2:
                        pe.wait_ge(s_he, i - 1)
                    w = [wv[0][(8 + c) % RING], wv[1][(8 + c) % RING]]
                    for k in range(KT):
                        last = three(ps[:, 3 + i % 2, 0:256], [y[:, k, P * t:P * t + P] for y in (t_hi, t_lo)],
                                     [y[:, k, :] for y in w], k == 0, k == KT - 1)
                    last.then_inc(s_w, 1)

            def h2_transposes(t):
                n = TILES[t][1]
                pe.wait_ge(s_h2, t + 1)
                if t >= 1:
                    pe.wait_ge(s_h2e, t)
                for k in range(KT):
                    last = pe.transpose(ps[:, k // 4, P * (k % 4):P * (k % 4) + n], h2[0:n, t % 2, P * k:P * k + P], ident[0:n, 0:n])
                last.then_inc(s_h2t, 1)

            def router(t):
                n = TILES[t][1]
                pe.wait_ge(s_h2e, t + 1)
                if t >= 2:
                    pe.wait_ge(s_lge, t - 1)
                hv = h2_t[:, t % 2, :].rearrange("p (k c) -> p k c", c=P)
                for k in range(KT):
                    last = pe.matmul(ps[0:n, 2 + 3 * (t % 2), 0:NE], hv[:, k, 0:n], rw[:, k, :], start=k == 0, stop=k == KT - 1)
                last.then_inc(s_lg, 1)

            sample_transposes(0)
            out_product(0)
            for b in range(4):
                sample_values(b)
            sample_transposes(1)
            out_product(1)
            for b in range(4, NB):
                sample_values(b)
            o_transposes(4, P)
            out_product(2)
            pe.wait_ge(s_late2, 64)
            h2_transposes(0)
            out_product(3)
            router(0)
            o_transposes(5, P)
            h2_transposes(1)
            out_product(4)
            router(1)
            for t in range(2, NT):
                h2_transposes(t)
                router(t)
            pe.wait_ge(s_sel, NT)
            for t in range(NT):
                for b in range(t):
                    pe.matmul(ps[:, t, 0:NE], ones, sel[:, b, :], start=b == 0, stop=False)
                pe.matmul(ps[:, t, 0:NE], tri, sel[:, t, :], start=t == 0, stop=True)
            for b in range(NT):
                last = pe.matmul(ps[:, 5, 0:NE], ones, sel[:, b, :], start=b == 0, stop=b == NT - 1)
            last.then_inc(s_rk, 1)
            pe.wait_ge(s_tab, 3)

            def index_product(m):
                pe.wait_ge(s_ohd, m + 1)
                for t in range(NT):
                    last = pe.matmul(ps[:, 6, 0:2], onehot[:, t, :], vals_c[:, t, :], start=t == 0, stop=t == NT - 1)
                last.then_inc(s_ix, 1)

            def row_transposes(src, wait, value, done):
                pe.wait_ge(wait, value)
                for k in range(KT):
                    last = pe.transpose(ps[:, 6 + k // 4, P * (k % 4):P * (k % 4) + P], src[:, P * k:P * k + P], ident)
                last.then_inc(done, 1)

            def x_transposes(m, gathered):
                if not isinstance(m, int) or m > 0:
                    pe.wait_ge(s_xl, m)
                row_transposes(xg, s_gat, gathered * 16, s_xt)

            def act_transposes(m):
                row_transposes(act, s_ac, m * 2 + 2, s_at)

            def expert_chunk(ck, j, lhs, k, banks, first_k, bias):
                pe.wait_ge(s_lo, ck.number(j + 1))
                tiles = 4 // banks
                base_bank = 0 if banks == 4 else 4
                for kk in range(tiles):
                    row = tiles * k + kk
                    for q, (l, r) in enumerate(((0, hi), (0, lo), (1, hi))):
                        for b in range(banks):
                            at = 512 * (banks * kk + b)
                            last = pe.matmul(ps[:, base_bank + b, :], lhs[l][:, row, :], r[:, ck.slot(j), at:at + 512],
                                             start=first_k and kk == 0 and q == 0, stop=False)
                if bias is not None:
                    pick, col = bias
                    for b in range(banks):
                        last = pe.matmul(ps[:, base_bank + b, :], pick[:], bias_r[:, col + 512 * b:col + 512 * b + 512], start=False, stop=True)
                last.then_inc(s_pc, 1)

            def w1(ck, j, m, selected, rows_ready):
                if j == 0:
                    pe.wait_ge(s_xl, rows_ready)
                    if not isinstance(m, int) or m > 0:
                        pe.wait_ge(s_l, m * 2)
                if j == W1C - 1:
                    pe.wait_ge(s_bs, selected)
                expert_chunk(ck, j, (x_hi, x_lo), j, 4, j == 0, (sel_w1, 0) if j == W1C - 1 else None)

            def w2(ck, j, m, selected):
                k = j % 4
                if k == 0:
                    pe.wait_ge(s_al, m + 1)
                    if not isinstance(m, int) or m > 0:
                        pe.wait_ge(s_ye, m)
                if k == W2C - 1:
                    pe.wait_ge(s_bs, selected)
                expert_chunk(ck, j, (act_hi, act_lo), k, 2, k == 0, (sel_w2, 2 * D) if k == W2C - 1 else None)

            index_product(0)
            pe.wait_ge(s_ixe, 1)
            x_transposes(0, 1)
            pe.wait_ge(s_xl, 1)
            index_product(1)
            start = Chunks(PRO, 0)
            for j in range(W1C):
                if j == 1:
                    pe.wait_ge(s_ixe, 2)
                    x_transposes(1, 2)
                w1(start, j, 0, 1, 1)

            def body(n):
                ck = Chunks(PRO + W1C, n)
                for j in range(W1C):
                    if j == 2:
                        act_transposes(n)
                    if j == 4:
                        pe.wait_ge(s_al, n + 1)
                        index_product(n + 3)
                    if j == 6:
                        pe.wait_ge(s_ixe, n + 4)
                        x_transposes(n + 2, n + 3)
                    w1(ck, j, n + 1, n + 2, n + 2)
                for j in range(W1C, PER):
                    w2(ck, j, n, n + 2)

            pe.wait_ge(s_xl, 2)
            index_product(2)
            pe.wait_ge(s_ixe, 3)
            body(0)
            with pe.Fori(1, NE - 1) as n:
                body(n)
            tail = Chunks(PRO + W1C + PER * (NE - 1), 0)
            pe.wait_ge(s_xl, NE + 1)
            act_transposes(NE - 1)
            for j in range(W2C):
                w2(tail, j, NE - 1, NE + 1)

            def further(e, r, i):
                ck = Chunks(EXTRA, i)
                index_product(i + (NE + 2))
                pe.wait_ge(s_ixe, i + (NE + 3))
                x_transposes(i + (NE + 1), i + (NE + 3))
                for j in range(W1C):
                    w1(ck, j, i + NE, i + (NE + 2), i + (NE + 2))
                act_transposes(i + NE)
                for j in range(W1C, PER):
                    w2(ck, j, i + NE, i + (NE + 2))
                pe.wait_ge(s_sca, i * 16 + 16 * (NE + 1))
                pe.sem_inc(s_carry, 1)

            further_blocks(pe, further)


_OUTS = [
    ("y_prompt", (1, SEQ, D)), ("y_sample", (NB, NS, D)),
    ("new_pool_prompt", (1, 1, BUF, POOLW)), ("new_pool_sample", (1, NB, BUF, POOLW)),
    ("new_k_prompt", (1, 1, SEQ, H, P)), ("new_v_prompt", (1, 1, SEQ, H, P)),
    ("new_k_sample", (1, NB, NS, H, P)), ("new_v_sample", (1, NB, NS, H, P)),
]


def program(nc, shapes):
    aps = {n: nc.dram_tensor(n, s, mybir.dt.from_np(t), kind="ExternalInput").ap() for n, (s, t) in shapes.items()}
    for n, s in _OUTS:
        aps[n] = nc.dram_tensor("out_" + n, s, F32, kind="ExternalOutput").ap()
    build(nc, aps)


def kernel(**inputs):
    import concourse.bacc as bacc
    from concourse.bass_utils import run_bass_kernel_spmd as run

    arrays = {n: np.ascontiguousarray(v) for n, v in inputs.items()}
    arrays.update(constants())
    nc = bacc.Bacc("TRN2", target_bir_lowering=False, num_devices=1)
    program(nc, {n: (v.shape, v.dtype) for n, v in arrays.items()})
    r = run(nc, [arrays], core_ids=[0])
    return tuple(r.results[0]["out_" + n] for n, _ in _OUTS)
```

```python
from contextlib import ExitStack

import numpy as np
import concourse.bass as bass
from concourse import mybir

ALU = mybir.AluOpType
ACT = mybir.ActivationFunctionType
F32 = mybir.dt.float32
F32R = mybir.dt.float32r
I32 = mybir.dt.int32
U32 = mybir.dt.uint32
AX = mybir.AxisListType.X

P = 128
D = 1024
SEQ = 512
NB = 8
NS = 4
NTOK = SEQ + NB * NS
TILES = [(0, 128), (128, 128), (256, 128), (384, 128), (512, 32)]
NT = len(TILES)
H = 4
HD = 64
PAST = 512
PAGES = 4
POOLW = 512
BUF = 15
NE = 32
TOPK = 4
KT = D // P
EPS = 1e-6
LAMBDA_INIT = 0.2
LIMIT = 7.0
ALPHA = 1.702
WINDOWS = (2, 4, 8, 16)
SLOPES = [2.0 ** (-8.0 * (h + 1) / H) for h in range(H)]
MASKED = 1e34
RAW, RING = 4, 4
CH = 2048
W1C, W2C = 8, 4
PER = W1C + W2C
PRO = 12
TABLE = NE + 3
SPARE = NE + 2
UNUSED = 65536.0

A_V, A_QT, A_KT, A_DIST = 0, 2560, 4736, 6912
A_KN, A_BAND, A_US = 8000, 10560, 12352
A_XN, A_SQ1 = 8000, 9024
A_P, A_A, A_AT, A_ON, A_SQ = 8000, 10048, 11072, 12096, 12608
A_S, A_PT = 10240, 11328
A_H, A_XG, A_OH = 0, 5120, 6144
A_ACT, A_G, A_SIG, A_L, A_Y, A_TMP = 7168, 8192, 9216, 10240, 11264, 12288
A_G2, A_H2T, A_SQ2, A_RW = 8192, 6144, 9216, 5120
A_RT, A_TRI, A_CUM = 5376, 5888, 10240
A_LAM, A_GSUB = 12864, 13120
ARENA = 13312
FINAL = (4, 0, 1, 2, 3)
SLOT_H = (0, 1, 3, 4, 2)
C_ID, C_IOTA = 0, 128
C_TOK = C_IOTA + 640
C_NEGM, C_M0, C_M1, C_SLOPE = C_TOK + 5, C_TOK + 6, C_TOK + 7, C_TOK + 8
C_EYE = C_TOK + 9
C_EPS = C_EYE + NE
NCONST = C_EPS + 1


def constants():
    c = np.zeros((P, NCONST), np.float32)
    p = np.arange(P)
    c[:, C_ID:C_ID + P] = np.eye(P)
    c[:, C_IOTA:C_IOTA + 640] = np.arange(640)
    c[:, C_TOK:C_TOK + 5] = p[:, None] + P * np.arange(5)
    c[:, C_NEGM] = np.where(p >= NE, -1, 0)
    second = (p // NS) % 2
    c[:, C_M0], c[:, C_M1] = 1 - second, second
    c[:, C_SLOPE] = [-SLOPES[(i // 8) % H] for i in p]
    c[:, C_EYE:C_EYE + NE] = (p[:, None] % NE) == np.arange(NE)
    c[:, C_EPS] = EPS
    d = np.full((P, 512 + 576), MASKED, np.float32)
    dist = p[:, None] - np.arange(512)[None, :] + 384
    d[:, :512] = np.where(dist >= 0, dist, MASKED)
    q = p % NS
    d[:, 512:1024] = PAST + q[:, None] - np.arange(PAST)[None, :]
    for t in range(2):
        for i in range(P):
            b = 4 * t + i // 32
            for j in range(q[i] + 1):
                d[i, 1024 + 32 * t + NS * b + j] = q[i] - j
    band = np.zeros((P, 4, 3, P), np.float32)
    sband = np.zeros((P, 4, 2, 32), np.float32)
    t, s = np.arange(P)[None, :], p[:, None]
    for g, w in enumerate(WINDOWS):
        here = (t - s >= 0) & (t - s < w)
        band[:, g, 0] = here / np.minimum(w, t + 1.0) - (t == s)
        band[:, g, 1] = here / float(w) - (t == s)
        band[:, g, 2] = ((t + P - s) < w) / float(w)
        for b in range(NB):
            for n in range(NS):
                for j in range(BUF):
                    sband[b * BUF + j, g, 0, b * NS + n] = (BUF + n - j < w) / w
                for j in range(n + 1):
                    sband[b * NS + j, g, 1, b * NS + n] = (n - j < w) / w - (n == j)
    bands = np.concatenate([band.reshape(P, -1), sband.reshape(P, -1)], 1)
    tri = np.concatenate([p[:, None] < p[None, :], np.ones((P, P), bool)], 1).astype(np.float32)
    return {"c_misc": c, "c_dist": d, "c_band": bands, "c_tri": tri}


def units():
    out = []
    for c in range(8):
        if c in (2, 3):
            out += [(c, "q", hh, part) for hh in range(2) for part in range(2)]
        else:
            out += [(c, "u" if c < 2 else "k" if c < 6 else "v", t, 0) for t in range(NT)]
    return out


UNITS = units()
LAST_UNIT = [max(i for i, u in enumerate(UNITS) if u[0] == c) + 1 for c in range(8)]


def build(nc, a):
    x_in = [(a["x_prompt"].rearrange("b t d -> (b t) d"), 128 * t) for t in range(4)]
    x_in.append((a["x_sample"].rearrange("b t d -> (b t) d"), 0))
    w_in = a["w_in"][0].rearrange("(k p) n -> p k n", p=P)
    w_out = a["w_out"][0].rearrange("(k p) n -> p k n", p=P)
    h2_dram = nc.dram_tensor("h2_rows", [NTOK, D], F32).ap()
    y_dram = nc.dram_tensor("expert_rows", [NTOK * TOPK, D], F32).ap()

    with ExitStack() as ctx:
        def sb(name, shape, dt=F32):
            return ctx.enter_context(nc.sbuf_tensor(name, shape, dt))

        def sem(name):
            return ctx.enter_context(nc.semaphore(name))

        raw = sb("raw", [P, RAW, CH])
        hi = sb("hi", [P, RING, CH], F32R)
        lo = sb("lo", [P, RING, CH], F32R)
        t_hi = sb("t_hi", [P, KT, 640], F32R)
        t_lo = sb("t_lo", [P, KT, 640], F32R)
        ar = sb("arena", [P, ARENA])
        bias_r = sb("bias_r", [2 * NE, 3 * D], F32R)
        sel_w1 = sb("sel_w1", [2 * NE, P], F32R)
        sel_w2 = sb("sel_w2", [2 * NE, P], F32R)
        cst = sb("cst", [P, NCONST])
        st = sb("stats", [P, 64])
        psc = sb("psc", [P, 4])
        pt = sb("pt", [1, NB * PAGES], I32)
        top = sb("top", [P, 8])
        topi = sb("topi", [P, 8], U32)
        topf = sb("topf", [P, 4])
        gate = sb("gate", [P, NT, 4])
        rank = sb("rank", [P, NT, TABLE])
        vals = sb("vals", [P, NT, TABLE, 2])
        rank_c = sb("rank_c", [P, NT])
        vals_c = sb("vals_c", [P, NT, 2])
        unused = sb("unused", [P, 2])
        idx = sb("idx", [P, TABLE, 2], U32)
        idx_g = sb("idx_g", [P, 1], U32)
        idx_s = sb("idx_s", [P, 1], U32)
        cnt = sb("cnt", [1, NE + 8], I32)
        cntf = sb("cntf", [1, 8])
        ps = ctx.enter_context(nc.psum_tensor("ps", [P, 8, 512], F32))

        def A(at, *shape):
            n = int(np.prod(shape))
            v = ar[:, at:at + n]
            if len(shape) == 2:
                v = v.rearrange("p (a b) -> p a b", a=shape[0])
            if len(shape) == 3:
                v = v.rearrange("p (a b c) -> p a b c", a=shape[0], b=shape[1])
            return v

        ident = cst[:, C_ID:C_ID + P]
        lamv, gsub = A(A_LAM, 4 * HD), A(A_GSUB, P)
        slots = A(6784, P)
        rbias, lgt, sel, oh4, kv4 = A(A_RT, NE), A(A_RT + 32, NE), A(A_RT + 64, NT, NE), A(A_RT + 224, 4, NE), A(A_RT + 352, 4, NE)
        before = A(A_CUM, NT + 1, NE)
        tri, ones = A(A_TRI, P), A(A_TRI + P, P)
        iota = cst[:, C_IOTA:C_IOTA + 640]
        v_nat, q_t, k_t = A(A_V, NT, 512), A(A_QT, H, NTOK), A(A_KT, H, NTOK)
        dist, dist_s = A(A_DIST, 512), A(A_DIST + 512, 576)
        k_nat, u_smp = A(A_KN, NT, 512), A(A_US, 512)
        u_nat = raw[:, 3, :].rearrange("p (t n) -> p t n", t=4)
        band = A(A_BAND, 4, 3, P)
        sband = A(A_BAND + 1536, 4, 2, 32)
        x_buf = raw[:, 1, :].rearrange("p (a n) -> p a n", a=2)
        xn, g1 = [raw[:, 2, 0:D], A(A_XN, D)], raw[:, 2, D:2 * D]
        state, pw = raw[:, 1, 0:512], raw[:, 1, 512:1024].rearrange("p (g n) -> p g n", g=4)
        d_t = [raw[:, 1, 1024:1568], raw[:, 2, 0:544]]
        page = raw[:, 0:3, :].rearrange("p s (a n) -> p (s a) n", a=4)
        kt_s, q_blk = raw[:, 3, 0:1024].rearrange("p (a n) -> p a n", a=2), raw[:, 3, 1024:2048].rearrange("p (a n) -> p a n", a=32)
        pr = A(A_P, 4, 512)
        aa, at_sb = A(A_A, 2, 512), A(A_AT, 2, 512)
        o_nat, o_sq = A(A_ON, 512), A(A_SQ, 512)
        s_smp, p_t = A(A_S, 2, 544), A(A_PT, 2, 5, 64)
        p_cols = A(A_PT, 2 * 5 * 64 + 32)
        h_res, xg, onehot = A(A_H, NT, D), A(A_XG, D), A(A_OH, NT, P)
        act, glu, sig, lin, y_sb, tmp = (A(v, D) for v in (A_ACT, A_G, A_SIG, A_L, A_Y, A_TMP))
        g2, h2_t, rw = A(A_G2, D), A(A_H2T, 2, D), A(A_RW, KT, NE)
        h2 = raw[:, 3, :].rearrange("p (a n) -> p a n", a=2)
        sq1, sq2 = A(A_SQ1, D), A(A_SQ2, D)
        eps = cst[:, C_EPS:C_EPS + 1]
        choices = [A(A_XG, 4 * D), A(A_XG + 4 * D, 4 * D)]
        choices += [y[:, i:i + 2, :].rearrange("p s n -> p (s n)").bitcast(F32) for y, i in ((hi, 0), (hi, 2), (lo, 0))]
        def y_fin(t):
            return raw[:, t // 2, D * (t % 2):D * (t % 2) + D]

        def sample_cols(y, t):
            return y[:, 4:8, 512 + 16 * t:528 + 16 * t].rearrange("p h (b q) -> p h b q", q=NS)

        def every_32(src):
            return src.rearrange("p h (b x) -> p h b x", x=32)[:, :, :, 0:NS]

        x_hi, x_lo = t_hi[:, :, 0:P], t_lo[:, :, 0:P]
        first_hi, first_lo = t_hi[:, :, 2 * P:3 * P], t_lo[:, :, 2 * P:3 * P]
        act_hi, act_lo = t_hi[:, :, P:2 * P], t_lo[:, :, P:2 * P]

        neglam = st[:, 0:1]

        s_x = [sem(f"x_loaded{i}") for i in range(2)]
        s_cst = sem("constants_loaded")
        s_g1 = sem("g1_loaded")
        s_late = sem("pool_inputs_loaded")
        s_raw = [sem(f"raw_loaded{i}") for i in range(RAW)]
        s_hi, s_lo = sem("hi_done"), sem("lo_done")
        s_pad, s_ss, s_rt, s_xn, s_tp = sem("pads_zeroed"), sem("squares_summed"), sem("root_done"), sem("xn_done"), sem("xn_transposed")
        s_th, s_tl = sem("xt_hi_done"), sem("xt_lo_done")
        s_dve, s_pool_c = sem("dve_chain"), sem("pool_chain")
        s_bh, s_lam, s_lame = sem("bias_rounded"), sem("lambda_dots"), sem("lambda_exps")
        s_z, s_ze = sem("z_unit_done"), sem("z_unit_out")
        s_kt, s_kte = sem("k_transposed"), sem("kt_out")
        s_d, s_de, s_po, s_ph, s_pl = sem("pool_diff"), sem("pool_diff_out"), sem("pool_lin"), sem("pool_hi"), sem("pool_lo")
        s_sc, s_sb, s_mx, s_e = sem("scores_done"), sem("scores_biased"), sem("max_done"), sem("exp_done")
        s_a, s_atr, s_ate, s_pv = sem("weights_done"), sem("weights_transposed"), sem("weights_t_out"), sem("pv_done")
        s_oc = sem("o_copied")
        s_os, s_or, s_on, s_ot, s_oh_, s_ol = (sem(n) for n in ("o_squares", "o_root", "o_normed", "o_transposed", "o_hi", "o_lo"))
        s_pg = [sem(f"pages_loaded{i}") for i in range(3)]
        s_qb, s_kp, s_kc, s_sss = sem("q_blocks"), sem("pages_used"), sem("page_t_out"), sem("sample_scores")
        s_smx, s_se, s_sa, s_ptr, s_pe = (sem(n) for n in ("sample_max", "sample_exp", "sample_weights", "sample_wt", "sample_wt_out"))
        s_xr, s_w, s_he = [sem(f"x_reloaded{i}") for i in range(3)], sem("w_out_unit"), sem("h_unit")
        s_n2, s_r2, s_h2, s_h2d, s_h2t, s_h2e, s_lg, s_lge = (sem(n) for n in ("n2_squares", "n2_root", "h2_done", "h2_stored", "h2_transposed", "h2t_out", "router_done", "logits_out"))
        s_gm, s_ge, s_sel, s_rk, s_tab = sem("gate_max"), sem("gate_exp"), sem("selected"), sem("ranks"), sem("tables_done")
        s_cum = sem("selections_summed")
        s_pcz = sem("p_columns_zeroed")
        s_late2 = sem("router_inputs_loaded")
        s_ohd, s_ix, s_ixe, s_gat = sem("onehot_done"), sem("index_product"), sem("index_out"), sem("rows_gathered")
        s_xt, s_xh, s_xl = sem("rows_transposed"), sem("rows_hi"), sem("rows_lo")
        s_bs = sem("bias_selector")
        s_pc = sem("chunk_multiplied")
        s_g, s_s, s_l, s_t, s_ac = sem("glu_clamped"), sem("sigmoid_done"), sem("lin_clamped"), sem("gated"), sem("act_done")
        s_at, s_ah, s_al = sem("act_transposed"), sem("act_hi_done"), sem("act_lo_done")
        s_ye, s_sca = sem("y_out"), sem("rows_scattered")
        s_fy = [sem(f"choices_loaded{i}") for i in range(NT)]
        s_gf, s_fs, s_fr, s_fo = sem("gf_loaded"), sem("final_squares"), sem("final_root"), sem("final_done")
        s_out, s_outp, s_ust = sem("outputs_stored"), sem("caches_stored"), sem("u_stored")
        s_fd = sem("final_done_on_vector")
        s_fc, s_fk, s_fn = sem("final_reciprocal"), sem("gated_sum_chain"), sem("final_normalised")
        s_carry = sem("carries_waits")

        block = ctx.enter_context(nc.Block())

        EXTRA = PRO + PER * NE
        assert EXTRA % RAW == 0 and EXTRA % RING == 0 and PRO % RAW == 0

        class Chunks:

            def __init__(self, base, step):
                self.base, self.step = base, step

            def raw_slot(self, j):
                return (self.base + j) % RAW

            def slot(self, j):
                return (self.base + j) % RING

            def number(self, j):
                return self.step * PER + (self.base + j)

            def loaded(self, j):
                before = PRO if self.raw_slot(j) == 0 else 0
                return self.step * (16 * PER // RAW) + 16 * (before + (self.base + j - PRO) // RAW + 1)

        def further_blocks(eng, body):
            most = eng.value_load(cnt[0:1, NE:NE + 1], min_val=0, max_val=NTOK)
            with eng.If(most > P):
                ran = eng.alloc_register("blocks_ran")
                eng.reg_mov(ran, 0)
                with eng.Fori(0, NE) as e:
                    many = eng.value_load(cnt[0:1, bass.ds(e, 1)], min_val=0, max_val=NTOK)
                    with eng.Fori(0, 4) as r:
                        with eng.If(many > r * P + P):
                            body(e, r, eng.snap(ran, min_val=0, max_val=NTOK * TOPK // P))
                            eng.reg_add(ran, ran, 1)
                        eng.nop()

        @block.sync
        def _(sp):
            def load_x(t):
                src, r = x_in[t]
                n = TILES[t][1]
                if t >= 2:
                    sp.wait_ge(s_xn, t - 1)
                sp.dma_start(x_buf[0:n, t % 2, :], src[r:r + n, :]).then_inc(s_x[t % 2], 16)

            def load_pro(g):
                if g:
                    sp.wait_ge(s_lo, g)
                src = w_in[:, :, 256 * g:256 * g + 256] if g < 8 else w_out[:, :, 256 * (g - 8):256 * (g - 8) + 256]
                sp.dma_start(raw[:, 0, :].rearrange("p (k n) -> p k n", k=KT), src).then_inc(s_raw[0], 16)

            load_x(0)
            sp.dma_start(g1, a["norm1_g"].to_broadcast([P, D])).then_inc(s_g1, 16)
            load_x(1)
            sp.dma_start(cst[:], a["c_misc"]).then_inc(s_g1, 16)
            load_pro(0)
            load_x(2)
            load_x(3)
            load_pro(1)
            load_x(4)
            for half in range(2):
                rows = slice(NE * half, NE * half + NE)
                sp.dma_start(ar[rows, 0:2 * D], a["b1"][0]).then_inc(s_cst, 16)
                sp.dma_start(ar[rows, 2 * D:3 * D], a["b2"][0]).then_inc(s_cst, 16)
            for i, n in enumerate(("lambda_q1", "lambda_k1", "lambda_q2", "lambda_k2")):
                sp.dma_start(lamv[:, i * HD:(i + 1) * HD], a[n].to_broadcast([P, HD])).then_inc(s_cst, 16)
            sp.dma_start(gsub, a["subln_g"].to_broadcast([P, P])).then_inc(s_cst, 16)
            with nc.allow_non_contiguous_dma("512 words"):
                sp.dma_start(psc[:], a["pool_scale"][0].rearrange("(g p) -> p g", p=P)).then_inc(s_cst, 16)
            sp.dma_start(pt[:], a["page_table"].rearrange("b n -> (b n)").rearrange("(a n) -> a n", a=1)).then_inc(s_cst, 16)
            sp.dma_start(ar[:, A_DIST:A_DIST + 1088], a["c_dist"]).then_inc(s_cst, 16)
            sp.dma_start(ar[:, A_BAND:A_BAND + 1792], a["c_band"]).then_inc(s_cst, 16)
            load_pro(2)
            sp.wait_ge(s_xn, NT)
            sp.dma_start(state[0:NB * BUF, :], a["state_pool"][0].rearrange("b t n -> (b t) n")).then_inc(s_late, 16)
            sp.dma_start(pw, a["pool_w"][0].rearrange("g c e -> c g e")).then_inc(s_late, 16)
            for g in range(3, PRO):
                load_pro(g)

            sp.wait_ge(s_cst, 16 * 13)

            number = [sp.value_load(pt[0:1, i:i + 1], min_val=0, max_val=a["cache_k"].shape[1] - 1) for i in range(NB * PAGES)]

            def load_pages(cache, b, s):
                if s == 0:
                    sp.wait_ge(s_lo, PRO)
                if s == 1:
                    sp.wait_ge(s_po, 4)
                if s >= 3:
                    sp.wait_ge(s_kp, H * (s - 2))
                for n in range(PAGES):
                    sp.dma_start(page[:, PAGES * (s % 3) + n, :],
                                 a[cache][0][bass.ds(number[b * PAGES + n], 1)].rearrange("a t h d -> (a t) (h d)")).then_inc(s_pg[s % 3], 16)

            for b in range(NB):
                load_pages("cache_k", b, b)
            for b in range(NB):
                load_pages("cache_v", b, NB + b)

            def load_expert(ck, j, e, k, second_half):
                if second_half:
                    src = a["w2"][0][bass.ds(e, 1), 256 * k:256 * k + 256, :].rearrange("a (k p) n -> p (a k) n", p=P)
                    dst = raw[:, ck.raw_slot(j), :].rearrange("p (k n) -> p k n", k=2)
                else:
                    src = a["w1"][0][bass.ds(e, 1), P * k:P * k + P, :].rearrange("a p n -> (a p) n")
                    dst = raw[:, ck.raw_slot(j), :]
                return sp.dma_start(dst, src).then_inc(s_raw[ck.raw_slot(j)], 16)

            start = Chunks(PRO, 0)
            for j in range(W1C):
                if j == 0:
                    sp.wait_ge(s_kp, 2 * NB * H)
                if j == 3:
                    sp.wait_ge(s_h2t, NT)
                    sp.wait_ge(s_h2d, 16 * NT)
                if j == 5:
                    sp.wait_ge(s_gat, 16)
                if j >= RAW:
                    sp.wait_ge(s_lo, PRO + j - RAW + 1)
                load_expert(start, j, 0, j, False)

            def body_loads(n):
                ck = Chunks(PRO + W1C, n)
                for j in range(PER):
                    sp.wait_ge(s_lo, ck.number(j) - RAW + 1)
                    if j < W1C:
                        load_expert(ck, j, n + 1, j, False)
                    else:
                        load_expert(ck, j, n, j - W1C, True)

            body_loads(0)
            with sp.Fori(1, NE - 1) as n:
                body_loads(n)
            tail = Chunks(PRO + W1C + PER * (NE - 1), 0)
            for j in range(W2C):
                sp.wait_ge(s_lo, tail.number(j) - RAW + 1)
                load_expert(tail, j, NE - 1, j, True)

            sp.wait_ge(s_tab, 3)
            def further(e, r, i):
                ck = Chunks(EXTRA, i)
                for j in range(PER):
                    sp.wait_ge(s_lo, ck.number(j) - RAW + 1)
                    load_expert(ck, j, e, j % W1C, j >= W1C)
                sp.wait_ge(s_sca, i * 16 + 16 * (NE + 1))
                sp.sem_inc(s_carry, 1)

            further_blocks(sp, further)
            sp.wait_ge(s_pc, PER * NE)
            sp.wait_ge(s_gat, 16 * (NE + 2))
            sp.wait_ge(s_sca, 16 * NE)
            sp.dma_start(raw[:, 3, 0:D], a["normf_g"].rearrange("(a n) -> a n", a=1).to_broadcast([P, D])).then_inc(s_gf, 16)
            y_rows = y_dram.rearrange("(t k) d -> t (k d)", k=TOPK)
            for t in FINAL:
                r, n = TILES[t]
                sp.dma_start(choices[t][0:n, :], y_rows[r:r + n, :]).then_inc(s_fy[t], 16)
            y_out = [(a["y_prompt"].rearrange("b t d -> (b t) d"), 128 * t) for t in range(4)] + [(a["y_sample"].rearrange("b t d -> (b t) d"), 0)]
            for p, t in enumerate(FINAL):
                n = TILES[t][1]
                if p < 3:
                    sp.wait_ge(s_fo, p + 1)
                else:
                    sp.wait_ge(s_fd, p - 2)
                dst, o = y_out[t]
                sp.dma_start(dst[o:o + n, :], y_fin(t)[0:n, :]).then_inc(s_out, 16)
            sp.wait_ge(s_out, 16 * NT)
            sp.wait_ge(s_outp, 16 * 5)

        @block.gpsimd
        def _(pool):
            pool.memset(t_hi[:, :, NTOK:640].bitcast(F32), 0.0)
            pool.memset(t_lo[:, :, NTOK:640].bitcast(F32), 0.0)
            pool.memset(gate[:], 0.0)
            pool.memset(rank[:], -1.0)
            pool.memset(vals[:], 0.0).then_inc(s_pad, 1)

            pool.wait_ge(s_ze, LAST_UNIT[1])
            pool.dma_start(a["new_pool_prompt"][0, 0], u_nat[P - BUF:P, 3, :]).then_inc(s_ust, 16)
            pool.dma_start(a["new_pool_sample"][0, :, BUF - NS:BUF, :], u_smp[0:32, :]).then_inc(s_ust, 16)
            pool.dma_start(a["new_pool_sample"][0, :, 0:BUF - NS, :], a["state_pool"][0, :, NS:BUF, :]).then_inc(s_outp, 16)

            def store(nat, prompt, sample):
                pool.dma_start(a[prompt][0, 0].rearrange("(t p) h d -> p t (h d)", p=P), nat[:, 0:4, :]).then_inc(s_outp, 16)
                pool.dma_start(a[sample][0].rearrange("b t h d -> (b t) (h d)"), nat[0:32, 4, :]).then_inc(s_outp, 16)

            pool.wait_ge(s_ze, LAST_UNIT[5])
            store(k_nat, "new_k_prompt", "new_k_sample")
            pool.wait_ge(s_ze, LAST_UNIT[7])
            store(v_nat, "new_v_prompt", "new_v_sample")
            pool.wait_ge(s_ust, 32)
            pool.wait_ge(s_po, 4)
            pool.memset(q_blk, 0.0).then_inc(s_qb, 1)
            pool.wait_ge(s_a, 16)
            pool.wait_ge(s_pv, 16)
            pool.wait_ge(s_ate, 16)
            pool.wait_ge(s_outp, 16 * 5)
            pool.memset(p_cols, 0.0).then_inc(s_pcz, 1)

            def reload_x(t, signal):
                src, r = x_in[t]
                n = TILES[t][1]
                pool.dma_start(h_res[0:n, SLOT_H[t], :], src[r:r + n, :]).then_inc(signal, 16)

            reload_x(0, s_xr[0])
            reload_x(1, s_xr[0])
            pool.wait_ge(s_qb, 2)
            pool.wait_ge(s_sss, NB * H)
            reload_x(2, s_xr[1])
            reload_x(3, s_xr[1])
            pool.dma_start(g2, a["norm2_g"].to_broadcast([P, D])).then_inc(s_late2, 16)
            pool.dma_start(rbias, a["router_b"].to_broadcast([P, NE])).then_inc(s_late2, 16)
            pool.dma_start(ar[:, A_TRI:A_TRI + 2 * P], a["c_tri"]).then_inc(s_late2, 16)
            pool.dma_start(rw, a["router_w"][0].rearrange("(k p) e -> p k e", p=P)).then_inc(s_late2, 16)
            pool.wait_ge(s_kp, 2 * NB * H)
            reload_x(4, s_xr[2])

            for t, (r, n) in enumerate(TILES):
                pool.wait_ge(s_h2, t + 1)
                if t:
                    pool.wait_ge(s_h2d, 16 * t)
                pool.dma_start(h2_dram[r:r + n, :], h2[0:n, t % 2, :]).then_inc(s_h2d, 16)
            pool.wait_ge(s_lge, NT)
            pool.wait_ge(s_tab, 3)
            pool.wait_ge(s_h2d, 16 * NT)

            def alone():
                pool.sem_inc(s_carry, 1)

            def make_onehot(m, column, rows, chain):
                if not isinstance(m, int) or m > 0:
                    pool.wait_ge(s_ix, m)
                alone()
                pool.tensor_copy(rank_c[:], rank[:, :, bass.ds(column, 1)].rearrange("p t a -> p (t a)")).then_inc(s_pool_c, 1)
                pool.tensor_copy(vals_c[:], vals[:, :, bass.ds(column, 1), :].rearrange("p t a b -> p t (a b)")).then_inc(s_pool_c, 1)
                pool.wait_ge(s_pool_c, chain + 2)
                if isinstance(m, int) and m == 0:
                    return
                alone()
                for t in range(NT):
                    last = pool.tensor_scalar(onehot[:, t, :], rows, rank_c[:, t:t + 1], None, ALU.is_equal)
                last.then_inc(s_ohd, 1)

            def gather(m, column, chain, before):
                pool.wait_ge(s_ixe, m + 1)
                if not isinstance(m, int) or m > 0:
                    pool.wait_ge(s_xt, before)
                    pool.wait_ge(s_gat, m * 16)
                alone()
                pool.tensor_copy(idx_g[:], idx[:, bass.ds(column, 1), 0]).then_inc(s_pool_c, 1)
                pool.wait_ge(s_pool_c, chain + 3)
                alone()
                pool.indirect_dma_start(out=xg, out_offset=None, in_=h2_dram,
                                        in_offset=bass.IndirectOffsetOnAxis(ap=idx_g[:, 0:1], axis=0),
                                        bounds_check=NTOK - 1, oob_is_err=False).then_inc(s_gat, 16)

            def gated(m, half):
                cols = slice(512 * half, 512 * half + 512)
                pool.wait_ge(s_l, m * 2 + (half + 1))
                alone()
                pool.tensor_scalar(lin[:, cols], lin[:, cols], 1.0, None, ALU.add).then_inc(s_t, 1)
                pool.wait_ge(s_s, m * 2 + (half + 1))
                pool.tensor_tensor(tmp[:, cols], glu[:, cols], sig[:, cols], ALU.mult).then_inc(s_t, 1)
                pool.wait_ge(s_t, m * 4 + (2 * half + 2))
                if not isinstance(m, int) or m > 0:
                    pool.wait_ge(s_at, m)
                pool.tensor_tensor(act[:, cols], tmp[:, cols], lin[:, cols], ALU.mult).then_inc(s_ac, 1)

            def scatter(m, column, chain):
                if not isinstance(m, int) or m > 0:
                    pool.wait_ge(s_sca, m * 16)
                alone()
                pool.tensor_copy(idx_s[:], idx[:, bass.ds(column, 1), 1]).then_inc(s_pool_c, 1)
                pool.wait_ge(s_pool_c, chain + 1)
                pool.wait_ge(s_ye, m + 1)
                alone()
                pool.indirect_dma_start(out=y_dram, out_offset=bass.IndirectOffsetOnAxis(ap=idx_s[:, 0:1], axis=0),
                                        in_=y_sb, in_offset=None,
                                        bounds_check=NTOK * TOPK - 1, oob_is_err=False).then_inc(s_sca, 16)

            for m in range(3):
                make_onehot(m, m, iota[:, 0:P], 3 * m + (m > 0))
                if m == 0:
                    pool.memset(xg, 0.0).then_inc(s_pool_c, 1)
                if m == 2:
                    gated(0, 0)
                    gated(0, 1)
                gather(m, m, 1 + 3 * m, m)
            make_onehot(3, 3, iota[:, 0:P], 10)
            gather(3, 3, 10, 3)
            gated(1, 0)
            gated(1, 1)
            with pool.Fori(1, NE - 1) as n:
                scatter(n - 1, n - 1, n * 4 + 9)
                make_onehot(n + 3, n + 3, iota[:, 0:P], n * 4 + 10)
                gather(n + 3, n + 3, n * 4 + 10, n + 3)
                gated(n + 1, 0)
                gated(n + 1, 1)
            scatter(NE - 2, NE - 2, 4 * NE + 5)
            scatter(NE - 1, NE - 1, 4 * NE + 6)

            def further(e, r, i):
                chain = i * 5 + (4 * NE + 8)
                pool.wait_ge(s_ix, i + (NE + 2))
                alone()
                pool.tensor_copy(slots, iota[:, bass.ds(r * P + P, P)]).then_inc(s_pool_c, 1)
                make_onehot(i + (NE + 2), e, slots, chain)
                gather(i + (NE + 2), SPARE, chain, i + (NE + 1))
                for half in range(2):
                    gated(i + NE, half)
                scatter(i + NE, SPARE, chain + 3)
                pool.wait_ge(s_sca, i * 16 + 16 * (NE + 1))
                pool.sem_inc(s_carry, 1)

            further_blocks(pool, further)
            pool.wait_ge(s_gf, 16)
            for p, t in enumerate(FINAL[0:3]):
                n = TILES[t][1]
                pool.wait_ge(s_fn, p + 1)
                pool.tensor_tensor(y_fin(t)[0:n, :], y_fin(t)[0:n, :], raw[0:n, 3, 0:D], ALU.mult).then_inc(s_fo, 1)

        @block.scalar
        def _(act_e):
            def gate_exp(t):
                n = TILES[t][1]
                act_e.wait_ge(s_gm, t + 1)
                act_e.activation(gate[0:n, t, :], top[0:n, 0:4], ACT.Exp, bias=st[0:n, 44:45], accum_out=st[0:n, 45:46]).then_inc(s_ge, 1)

            def split_hi(slot_raw, slot, loaded):
                act_e.wait_ge(s_raw[slot_raw], loaded)
                act_e.activation(hi[:, slot, :], raw[:, slot_raw, :], ACT.Copy).then_inc(s_hi, 1)

            def pro_hi(g):
                if g >= RING:
                    act_e.wait_ge(s_z, LAST_UNIT[g - RING])
                split_hi(0, g % RING, 16 * (g + 1))

            def norm1_sums(t):
                n = TILES[t][1]
                act_e.wait_ge(s_x[t % 2], 16 * (t // 2 + 1))
                act_e.activation(sq1[0:n, :], x_buf[0:n, t % 2, :], ACT.Square, accum_out=st[0:n, 2 + t:3 + t]).then_inc(s_ss, 1)
                act_e.wait_ge(s_ss, t + 1)
                act_e.activation(st[0:n, 8 + t:9 + t], st[0:n, 2 + t:3 + t], ACT.Sqrt, scale=1.0 / D, bias=eps[0:n]).then_inc(s_rt, 1)

            act_e.wait_ge(s_g1, 32)
            norm1_sums(0)
            for t, (_, n) in enumerate(TILES):
                if t + 1 < NT:
                    norm1_sums(t + 1)
                act_e.wait_ge(s_tp, t + 1)
                if t == 0:
                    act_e.wait_ge(s_pad, 1)
                src = ps[:, 2 * (t % 2):2 * (t % 2) + 2, :].rearrange("p b (k c) -> p (b k) c", c=P)[:, :, 0:n]
                act_e.activation(t_hi[:, :, P * t:P * t + n], src, ACT.Copy).then_inc(s_th, 1)
                if t in (0, 3):
                    pro_hi(t // 3)

            def biases():
                act_e.wait_ge(s_cst, 16 * 13)
                act_e.activation(bias_r[:], ar[0:2 * NE, 0:3 * D], ACT.Copy).then_inc(s_bh, 1)

            def lambda_exps():
                act_e.wait_ge(s_lam, 1)
                act_e.activation(st[:, 16:18], st[:, 14:16], ACT.Exp).then_inc(s_lame, 1)
                act_e.wait_ge(s_bh, 2)

            for i, (c, kind, t, part) in enumerate(UNITS):
                if i in (1, 3):
                    pro_hi(2 + i // 2)
                if i == NT + 1:
                    biases()
                if i == 2 * NT:
                    lambda_exps()
                act_e.wait_ge(s_z, i + 1)
                bank = 4 + i % 4
                if kind == "q":
                    h = 2 * (c - 2) + t
                    n = NTOK // 2
                    act_e.activation(q_t[:, h, n * part:n * part + n], ps[:, bank, 0:n], ACT.Copy, scale=HD ** -0.5).then_inc(s_ze, 1)
                else:
                    n = TILES[t][1]
                    col = 256 * (c % 2)
                    dst = {"u": u_nat, "k": k_nat, "v": v_nat}[kind]
                    dst = u_smp[0:n, col:col + 256] if kind == "u" and t == 4 else dst[0:n, t, col:col + 256]
                    act_e.activation(dst, ps[0:n, bank, 0:256], ACT.Copy).then_inc(s_ze, 1)
                if i + 1 in LAST_UNIT:
                    pro_hi(LAST_UNIT.index(i + 1) + RING)
            def pool_diff(g):
                act_e.wait_ge(s_d, g + 1)
                if g >= 2:
                    act_e.wait_ge(s_po, g - 1)
                act_e.activation(d_t[g % 2][:, 0:512], ps[:, 2 * (g % 2), :], ACT.Copy)
                act_e.activation(d_t[g % 2][:, 512:544], ps[:, 2 * (g % 2) + 1, 0:32], ACT.Copy).then_inc(s_de, 1)

            def pool_hi(g):
                act_e.wait_ge(s_po, g + 1)
                b = 4 + 2 * (g % 2)
                act_e.activation(t_hi[:, g, 0:512], ps[:, b, :], ACT.Copy, scale=psc[:, g:g + 1])
                act_e.activation(t_hi[:, g, 512:544], ps[:, b + 1, 0:32], ACT.Copy, scale=psc[:, g:g + 1]).then_inc(s_ph, 1)

            act_e.wait_ge(s_late, 32)
            for g in range(4):
                pool_diff(g)
                if g >= 1:
                    pool_hi(g - 1)
            pool_hi(3)

            def o_root(i, n):
                act_e.wait_ge(s_os, i + 1)
                act_e.activation(st[0:n, 28:32], st[0:n, 28:32], ACT.Sqrt, scale=1.0 / P, bias=eps[0:n]).then_inc(s_or, 1)

            def o_hi(i):
                act_e.wait_ge(s_ot, i + 1)
                src = ps[:, 7, :].rearrange("p (h c) -> p h c", c=P)
                if i < 4:
                    act_e.activation(t_hi[:, 4:8, P * i:P * i + P], src, ACT.Copy).then_inc(s_oh_, 1)
                else:
                    act_e.activation(sample_cols(t_hi, i - 4), every_32(src), ACT.Copy).then_inc(s_oh_, 1)

            def weights_t(i):
                nk = P * (i // 4 + 1)
                act_e.wait_ge(s_atr, i + 1)
                if i >= 2:
                    act_e.wait_ge(s_pv, i - 1)
                act_e.activation(at_sb[:, i % 2, 0:nk], ps[:, 4 + i % 2, 0:nk], ACT.Copy).then_inc(s_ate, 1)

            for i in range(17):
                if i < 16:
                    nk = P * (i // 4 + 1)
                    act_e.wait_ge(s_mx, i + 1)
                    for c in range(2):
                        w = pr[:, 2 * (i % 2) + c, 0:nk]
                        e = act_e.activation(w, w, ACT.Exp, bias=st[:, 20 + 2 * (i % 2) + c:21 + 2 * (i % 2) + c],
                                             accum_out=st[:, 24 + 2 * (i % 2) + c:25 + 2 * (i % 2) + c])
                    e.then_inc(s_e, 1)
                if i >= 1:
                    weights_t(i - 1)
                    if i >= 6 and i % 4 == 2:
                        o_root(i // 4 - 1, P)
                    if i >= 8 and i % 4 == 0:
                        o_hi(i // 4 - 2)
            o_root(3, P)
            act_e.wait_ge(s_ust, 32)
            def sample_exp(t):
                act_e.wait_ge(s_smx, t + 1)
                act_e.activation(s_smp[:, t, :], s_smp[:, t, :], ACT.Exp, bias=st[:, 32 + t:33 + t], accum_out=st[:, 34 + t:35 + t]).then_inc(s_se, 1)

            for m in range(NB * H):
                act_e.wait_ge(s_kp, m + 1)
                if m >= 2:
                    act_e.wait_ge(s_sss, m - 1)
                act_e.activation(kt_s[:, m % 2, :], ps[:, m % 3, :], ACT.Copy).then_inc(s_kc, 1)
                if m == 5:
                    o_hi(3)
                if m == 20:
                    sample_exp(0)
            sample_exp(1)
            start = Chunks(PRO, 0)

            def norm2_sums(t):
                n = TILES[t][1]
                act_e.wait_ge(s_he, 4 * t + 4)
                act_e.activation(sq2[0:n, :], h_res[0:n, SLOT_H[t], :], ACT.Square, accum_out=st[0:n, 36 + t:37 + t]).then_inc(s_n2, 1)
                act_e.wait_ge(s_n2, t + 1)
                act_e.activation(st[0:n, 36 + t:37 + t], st[0:n, 36 + t:37 + t], ACT.Sqrt, scale=1.0 / D, bias=eps[0:n]).then_inc(s_r2, 1)

            def h2_out(t):
                n = TILES[t][1]
                act_e.wait_ge(s_h2t, t + 1)
                if t >= 2:
                    act_e.wait_ge(s_lg, t - 1)
                src = ps[:, 0:2, :].rearrange("p b (k c) -> p (b k) c", c=P)[:, :, 0:n]
                act_e.activation(h2_t[:, t % 2, :].rearrange("p (k c) -> p k c", c=P)[:, :, 0:n], src, ACT.Copy).then_inc(s_h2e, 1)

            o_root(4, P)
            norm2_sums(0)
            norm2_sums(1)
            o_hi(4)
            norm2_sums(2)
            h2_out(0)
            o_root(5, P)
            norm2_sums(3)
            o_hi(5)
            h2_out(1)
            gate_exp(0)
            h2_out(2)
            gate_exp(1)
            act_e.activation(st[:, 60:61], eps, ACT.Sqrt)
            norm2_sums(4)
            act_e.activation(st[:, 61:62], eps, ACT.Exp)
            h2_out(3)
            h2_out(4)
            gate_exp(2)
            gate_exp(3)
            gate_exp(4)

            def expert_hi(ck, j):
                act_e.wait_ge(s_pc, ck.number(j) - PRO - RING + 1)
                split_hi(ck.raw_slot(j), ck.slot(j), ck.loaded(j))

            def rows_hi(m, src_sem, done, dst):
                act_e.wait_ge(src_sem, m + 1)
                src = ps[:, 6:8, :].rearrange("p b (k c) -> p (b k) c", c=P)
                act_e.activation(dst, src, ACT.Copy).then_inc(done, 1)

            def selector(dst, e):
                return act_e.activation(dst[:], cst[0:2 * NE, bass.ds(C_EYE + e, 1)].to_broadcast([2 * NE, P]), ACT.Copy)

            def sigmoid(m, half):
                cols = slice(512 * half, 512 * half + 512)
                act_e.wait_ge(s_g, m * 2 + (half + 1))
                if not isinstance(m, int) or m > 0:
                    act_e.wait_ge(s_ac, m * 2)
                act_e.activation(sig[:, cols], glu[:, cols], ACT.Sigmoid, scale=ALPHA).then_inc(s_s, 1)

            def y_out(m, done):
                act_e.wait_ge(s_pc, done)
                if not isinstance(m, int) or m > 0:
                    act_e.wait_ge(s_sca, m * 16)
                act_e.activation(y_sb, ps[:, 4:6, :].rearrange("p b n -> p (b n)"), ACT.Copy).then_inc(s_ye, 1)

            act_e.wait_ge(s_w, 20)
            for j in range(RING):
                split_hi(start.raw_slot(j), start.slot(j), start.loaded(j))
            rows_hi(0, s_xt, s_xh, first_hi)
            selector(sel_w1, 0).then_inc(s_bs, 1)
            act_e.activation(st[:, 62:63], eps, ACT.Sigmoid)
            for j in range(RING, W1C):
                expert_hi(start, j)
                if j == 6:
                    rows_hi(1, s_xt, s_xh, x_hi)
            head = Chunks(PRO + W1C, 0)
            for j in range(4):
                expert_hi(head, j)
            sigmoid(0, 0)
            sigmoid(0, 1)

            def body(n, j0=0):
                ck = Chunks(PRO + W1C, n)
                before_act = 6 if j0 == 4 else 4
                for j in range(j0, before_act):
                    expert_hi(ck, j)
                    if j == 2:
                        y_out(n - 1, ck.number(0) - PRO)
                rows_hi(n, s_at, s_ah, act_hi)
                selector(sel_w1, n + 1)
                selector(sel_w2, n).then_inc(s_bs, 1)
                for j in range(before_act, PER):
                    expert_hi(ck, j)
                act_e.wait_ge(s_pc, ck.number(W1C) - PRO)
                rows_hi(n + 2, s_xt, s_xh, x_hi)
                sigmoid(n + 1, 0)
                sigmoid(n + 1, 1)

            body(0, 4)
            with act_e.Fori(1, NE - 1) as n:
                body(n)
            tail = Chunks(PRO + W1C + PER * (NE - 1), 0)
            for j in range(3):
                expert_hi(tail, j)
            y_out(NE - 2, tail.number(0) - PRO)
            rows_hi(NE - 1, s_at, s_ah, act_hi)
            selector(sel_w2, NE - 1).then_inc(s_bs, 1)
            expert_hi(tail, 3)
            y_out(NE - 1, PER * NE)

            act_e.wait_ge(s_tab, 3)
            def further(e, r, i):
                ck = Chunks(EXTRA, i)
                rows_hi(i + (NE + 1), s_xt, s_xh, x_hi)
                selector(sel_w1, e)
                selector(sel_w2, e).then_inc(s_bs, 1)
                for j in range(W1C):
                    expert_hi(ck, j)
                sigmoid(i + NE, 0)
                sigmoid(i + NE, 1)
                rows_hi(i + NE, s_at, s_ah, act_hi)
                for j in range(W1C, PER):
                    expert_hi(ck, j)
                y_out(i + NE, ck.number(PER) - PRO)
                act_e.wait_ge(s_sca, i * 16 + 16 * (NE + 1))
                act_e.sem_inc(s_carry, 1)

            further_blocks(act_e, further)
            def normalised(p):
                t = FINAL[p]
                n = TILES[t][1]
                act_e.wait_ge(s_fc, p + 1)
                act_e.activation(y_fin(t)[0:n, :], h_res[0:n, SLOT_H[t], :], ACT.Copy, scale=st[0:n, 50 + t:51 + t]).then_inc(s_fn, 1)

            for p, t in enumerate(FINAL):
                n = TILES[t][1]
                act_e.wait_ge(s_fs, p + 1)
                act_e.activation(raw[0:n, 3, D:2 * D], h_res[0:n, SLOT_H[t], :], ACT.Square, accum_out=st[0:n, 50 + t:51 + t]).then_inc(s_fr, 1)
                act_e.wait_ge(s_fr, 2 * p + 1)
                act_e.activation(st[0:n, 50 + t:51 + t], st[0:n, 50 + t:51 + t], ACT.Sqrt, scale=1.0 / D, bias=eps[0:n]).then_inc(s_fr, 1)
                if 1 <= p < 4:
                    normalised(p - 1)

        @block.vector
        def _(v):
            chain = [0]

            def link(ins):
                chain[0] += 1
                ins.then_inc(s_dve, 1)
                v.wait_ge(s_dve, chain[0])

            def split_lo(slot_raw, slot, hi_done):
                v.wait_ge(s_hi, hi_done)
                v.tensor_tensor(lo[:, slot, :], raw[:, slot_raw, :], hi[:, slot, :].bitcast(F32), ALU.subtract).then_inc(s_lo, 1)

            def pro_lo(g):
                split_lo(0, g % RING, g + 1)

            def norm1_rows(t):
                n = TILES[t][1]
                v.wait_ge(s_rt, t + 1)
                link(v.reciprocal(st[0:n, 2 + t:3 + t], st[0:n, 8 + t:9 + t]))
                if t >= 2:
                    v.wait_ge(s_tp, t - 1)
                v.scalar_tensor_tensor(out=xn[t % 2][0:n, :], in0=x_buf[0:n, t % 2, :], scalar=st[0:n, 2 + t:3 + t], in1=g1[0:n, :],
                                       op0=ALU.mult, op1=ALU.mult).then_inc(s_xn, 1)

            v.wait_ge(s_g1, 32)
            norm1_rows(0)
            for t, (_, n) in enumerate(TILES):
                if t + 1 < NT:
                    norm1_rows(t + 1)
                v.wait_ge(s_th, t + 1)
                src = ps[:, 2 * (t % 2):2 * (t % 2) + 2, :].rearrange("p b (k c) -> p (b k) c", c=P)[:, :, 0:n]
                v.tensor_tensor(t_lo[:, :, P * t:P * t + n], src, t_hi[:, :, P * t:P * t + n].bitcast(F32), ALU.subtract).then_inc(s_tl, 1)
                if t in (0, 3):
                    pro_lo(t // 3)
            pro_lo(2)
            pro_lo(3)
            v.wait_ge(s_cst, 16 * 13)
            v.wait_ge(s_bh, 1)
            v.scalar_tensor_tensor(out=bias_r[:], in0=bias_r[:].bitcast(F32), scalar=cst[0:2 * NE, C_NEGM:C_NEGM + 1],
                                   in1=ar[0:2 * NE, 0:3 * D], op0=ALU.mult, op1=ALU.add).then_inc(s_bh, 1)
            lv = lamv.rearrange("p (a b n) -> p a b n", a=2, b=2)
            link(v.tensor_tensor(lv[:, :, 0, :], lv[:, :, 0, :], lv[:, :, 1, :], ALU.mult))
            v.tensor_reduce(st[:, 14:16], lv[:, :, 0, :], AX, ALU.add).then_inc(s_lam, 1)
            pro_lo(4)
            v.wait_ge(s_lame, 1)
            link(v.tensor_tensor(neglam, st[:, 17:18], st[:, 16:17], ALU.subtract))
            link(v.tensor_scalar(neglam, neglam, LAMBDA_INIT, None, ALU.subtract))
            link(v.tensor_scalar(st[:, 18:19], cst[:, C_M1:C_M1 + 1], neglam, cst[:, C_M0:C_M0 + 1], ALU.mult, ALU.add))
            link(v.tensor_scalar(gsub, gsub, 1.0 - LAMBDA_INIT, None, ALU.mult))

            def k_out(hp):
                v.wait_ge(s_kt, hp + 1)
                for hh in range(2):
                    v.tensor_copy(k_t[:, 2 * hp + hh, 0:512], ps[:, 2 * hh, :])
                    last = v.tensor_copy(k_t[:, 2 * hp + hh, 512:544], ps[:, 2 * hh + 1, 0:32])
                last.then_inc(s_kte, 1)

            for g in range(RING + 1, 10):
                pro_lo(g)
            k_out(0)
            pro_lo(10)
            k_out(1)
            pro_lo(11)

            for g in range(4):
                v.wait_ge(s_ph, g + 1)
                b = 4 + 2 * (g % 2)
                v.scalar_tensor_tensor(out=t_lo[:, g, 0:512], in0=ps[:, b, :], scalar=psc[:, g:g + 1],
                                       in1=t_hi[:, g, 0:512].bitcast(F32), op0=ALU.mult, op1=ALU.subtract)
                v.scalar_tensor_tensor(out=t_lo[:, g, 512:544], in0=ps[:, b + 1, 0:32], scalar=psc[:, g:g + 1],
                                       in1=t_hi[:, g, 512:544].bitcast(F32), op0=ALU.mult, op1=ALU.subtract).then_inc(s_pl, 1)

            def o_squares(i):
                if i > 0:
                    v.wait_ge(s_ot, i)
                v.tensor_copy(o_nat, ps[:, 6, :]).then_inc(s_oc, 1)
                v.wait_ge(s_oc, i + 1)
                link(v.tensor_tensor(o_sq, o_nat, o_nat, ALU.mult))
                v.tensor_reduce(st[:, 28:32], o_sq.rearrange("p (h c) -> p h c", c=P), AX, ALU.add).then_inc(s_os, 1)

            def o_norm(i):
                ov = o_nat.rearrange("p (h c) -> p h c", c=P)
                v.wait_ge(s_or, i + 1)
                link(v.reciprocal(st[:, 28:32], st[:, 28:32]))
                link(v.tensor_tensor(ov, ov, st[:, 28:32].unsqueeze(2).to_broadcast([P, 4, P]), ALU.mult))
                v.tensor_tensor(ov, ov, gsub.unsqueeze(1).to_broadcast([P, 4, P]), ALU.mult).then_inc(s_on, 1)

            def o_lo(i):
                v.wait_ge(s_oh_, i + 1)
                src = ps[:, 7, :].rearrange("p (h c) -> p h c", c=P)
                if i < 4:
                    v.tensor_tensor(t_lo[:, 4:8, P * i:P * i + P], src, t_hi[:, 4:8, P * i:P * i + P].bitcast(F32), ALU.subtract).then_inc(s_ol, 1)
                else:
                    v.tensor_tensor(sample_cols(t_lo, i - 4), every_32(src), sample_cols(t_hi, i - 4).bitcast(F32), ALU.subtract).then_inc(s_ol, 1)

            def bias_max(i):
                qt, h = i // 4, i % 4
                nk = P * (qt + 1)
                v.wait_ge(s_sc, i + 1)
                p2 = 2 * (i % 2)
                for c in range(2):
                    e = v.scalar_tensor_tensor(out=pr[:, p2 + c, 0:nk], in0=dist[:, 384 - P * qt:384 - P * qt + nk], scalar=-SLOPES[h],
                                               in1=ps[:, p2 + c, 0:nk], op0=ALU.mult, op1=ALU.add)
                e.then_inc(s_sb, 1)
                v.wait_ge(s_sb, i + 1)
                v.tensor_reduce(st[:, 20 + p2:22 + p2], pr[:, p2:p2 + 2, 0:nk], AX, ALU.max, negate=True).then_inc(s_mx, 1)

            def weights(i):
                nk = P * (i // 4 + 1)
                p2 = 2 * (i % 2)
                v.wait_ge(s_e, i + 1)
                link(v.reciprocal(st[:, 24 + p2:26 + p2], st[:, 24 + p2:26 + p2]))
                link(v.tensor_tensor(st[:, 25 + p2:26 + p2], st[:, 25 + p2:26 + p2], neglam, ALU.mult))
                if i >= 2:
                    v.wait_ge(s_atr, i - 1)
                link(v.tensor_scalar(aa[:, i % 2, 0:nk], pr[:, p2, 0:nk], st[:, 24 + p2:25 + p2], None, ALU.mult))
                v.scalar_tensor_tensor(out=aa[:, i % 2, 0:nk], in0=pr[:, p2 + 1, 0:nk], scalar=st[:, 25 + p2:26 + p2],
                                       in1=aa[:, i % 2, 0:nk], op0=ALU.mult, op1=ALU.add).then_inc(s_a, 1)
                v.wait_ge(s_a, i + 1)

            def sample_queries():
                v.wait_ge(s_qb, 1)
                for h in range(H):
                    for c in range(2):
                        rows = slice(HD * c, HD * c + HD)
                        dst = q_blk.rearrange("p (b h) n -> p b h n", h=H)[rows, :, h, 8 * h + 4 * c:8 * h + 4 * c + 4]
                        last = v.tensor_copy(dst, q_t[rows, h, 512:544].rearrange("p (b q) -> p b q", q=NS))
                last.then_inc(s_qb, 1)

            v.wait_ge(s_outp, 16 * 5)
            v.wait_ge(s_ust, 32)
            bias_max(0)
            for i in range(16):
                if i + 1 < 16:
                    bias_max(i + 1)
                weights(i)
                if i == 2:
                    sample_queries()
                if i % 4 == 1 and i >= 5:
                    v.wait_ge(s_pv, i - 1)
                    o_squares(i // 4 - 1)
                if i % 4 == 2 and i >= 6:
                    o_norm(i // 4 - 1)
                if i % 4 == 0 and i >= 8:
                    o_lo(i // 4 - 2)
            o_lo(2)
            v.wait_ge(s_pv, 16)
            o_squares(3)
            o_norm(3)
            o_lo(3)

            def sample_softmax(t):
                v.wait_ge(s_sss, 16 * (t + 1))
                v.scalar_tensor_tensor(out=s_smp[:, t, 0:512], in0=dist_s[:, 0:512], scalar=cst[:, C_SLOPE:C_SLOPE + 1],
                                       in1=ps[:, 4 + t, :], op0=ALU.mult, op1=ALU.add)
                link(v.scalar_tensor_tensor(out=s_smp[:, t, 512:544], in0=dist_s[:, 512 + 32 * t:544 + 32 * t], scalar=cst[:, C_SLOPE:C_SLOPE + 1],
                                            in1=ps[:, 3 + 3 * t, 0:32], op0=ALU.mult, op1=ALU.add))
                v.tensor_reduce(st[:, 32 + t:33 + t], s_smp[:, t, :], AX, ALU.max, negate=True).then_inc(s_smx, 1)
                v.wait_ge(s_se, t + 1)
                link(v.reciprocal(st[:, 34 + t:35 + t], st[:, 34 + t:35 + t]))
                link(v.tensor_tensor(st[:, 34 + t:35 + t], st[:, 34 + t:35 + t], st[:, 18:19], ALU.mult))
                v.tensor_scalar(s_smp[:, t, :], s_smp[:, t, :], st[:, 34 + t:35 + t], None, ALU.mult).then_inc(s_sa, 1)

            def sample_weights(t):
                v.wait_ge(s_ptr, t + 1)
                v.wait_ge(s_pcz, 1)
                w = ps[:, 0 + t, :].rearrange("p (k x c q) -> p k x c q", k=4, c=2, q=NS)
                for k in range(4):
                    e = v.tensor_copy(p_t[:, t, k, :].rearrange("p (x q) -> p x q", q=NS), w[:, k, :, 0, :])
                wn = ps[0:32, 2 + 3 * t, 0:P].rearrange("p (x c q) -> p x c q", c=2, q=NS)
                pn = p_t[0:32, t, 4, :].rearrange("p (x q) -> p x q", q=NS)
                link(v.tensor_copy(pn, wn[:, :, 0, :]))
                for k in range(4):
                    v.tensor_tensor(p_t[:, t, k, :].rearrange("p (x q) -> p x q", q=NS), p_t[:, t, k, :].rearrange("p (x q) -> p x q", q=NS), w[:, k, :, 1, :], ALU.add)
                v.tensor_tensor(pn, pn, wn[:, :, 1, :], ALU.add).then_inc(s_pe, 1)

            def residual(t, chunks=range(4)):
                n = TILES[t][1]
                v.wait_ge(s_xr[t // 2], 16 if t == 4 else 32)
                for c in chunks:
                    i = 4 * t + c
                    v.wait_ge(s_w, i + 1)
                    dst = h_res[0:n, SLOT_H[t], 256 * c:256 * c + 256]
                    v.tensor_tensor(dst, ps[0:n, 3 + i % 2, 0:256], dst, ALU.add).then_inc(s_he, 1)

            def norm2(t):
                n = TILES[t][1]
                v.wait_ge(s_r2, t + 1)
                link(v.reciprocal(st[0:n, 36 + t:37 + t], st[0:n, 36 + t:37 + t]))
                if t >= 2:
                    v.wait_ge(s_h2t, t - 1)
                    v.wait_ge(s_h2d, 16 * (t - 1))
                v.scalar_tensor_tensor(out=h2[0:n, t % 2, :], in0=h_res[0:n, SLOT_H[t], :], scalar=st[0:n, 36 + t:37 + t], in1=g2[0:n, :],
                                       op0=ALU.mult, op1=ALU.mult).then_inc(s_h2, 1)

            def choose(t):
                n = TILES[t][1]
                v.wait_ge(s_lg, t + 1)
                if t >= 1:
                    v.wait_ge(s_ge, t)
                v.tensor_tensor(lgt[0:n], ps[0:n, 2 + 3 * (t % 2), 0:NE], rbias[0:n], ALU.add).then_inc(s_lge, 1)
                v.wait_ge(s_lge, t + 1)
                link(v.max(top[0:n], lgt[0:n]))
                v.tensor_scalar(st[0:n, 44:45], top[0:n, 0:1], -1.0, None, ALU.mult).then_inc(s_gm, 1)
                link(v.max_index(topi[0:n], top[0:n], lgt[0:n]))
                link(v.tensor_copy(topf[0:n], topi[0:n, 0:4]))
                link(v.tensor_tensor(oh4[0:n], iota[0:n, 0:NE].unsqueeze(1).to_broadcast([n, 4, NE]),
                                     topf[0:n].unsqueeze(2).to_broadcast([n, 4, NE]), ALU.is_equal))
                link(v.tensor_reduce(sel[0:n, t, :], oh4[0:n].rearrange("p k e -> p e k"), AX, ALU.add))
                v.tensor_tensor(before[:, t + 1, :], before[:, t, :], sel[:, t, :], ALU.add).then_inc(s_cum, 1)
                link(v.tensor_tensor(kv4[0:n], oh4[0:n], iota[0:n, 0:4].unsqueeze(2).to_broadcast([n, 4, NE]), ALU.mult))
                link(v.tensor_reduce(vals[0:n, t, 0:NE, 1], kv4[0:n].rearrange("p k e -> p e k"), AX, ALU.add))
                link(v.tensor_scalar(topf[0:n, 0:1], cst[0:n, C_TOK + t:C_TOK + t + 1], 4.0, 1.0, ALU.mult, ALU.add))
                v.tensor_scalar(vals[0:n, t, 0:NE, 1], vals[0:n, t, 0:NE, 1], topf[0:n, 0:1], None, ALU.add)
                link(v.tensor_scalar(vals[0:n, t, 0:NE, 0], ones[0:n, 0:NE], cst[0:n, C_TOK + t:C_TOK + t + 1], None, ALU.add))
                v.wait_ge(s_ge, t + 1)
                link(v.reciprocal(st[0:n, 46:47], st[0:n, 45:46]))
                v.tensor_scalar(gate[0:n, t, :], gate[0:n, t, :], st[0:n, 46:47], None, ALU.mult).then_inc(s_sel, 1)

            sample_softmax(0)
            sample_softmax(1)
            sample_weights(0)
            residual(0)
            v.wait_ge(s_kp, NB * H + 4 * H)
            o_squares(4)
            o_norm(4)
            sample_weights(1)
            residual(1)
            start = Chunks(PRO, 0)
            v.wait_ge(s_late2, 64)
            v.memset(before[:, 0, :], 0.0)
            link(v.memset(sel, 0.0))
            norm2(0)
            o_lo(4)
            residual(2)
            norm2(1)
            v.wait_ge(s_kp, 2 * NB * H)
            o_squares(5)
            o_norm(5)
            residual(3)
            o_lo(5)
            norm2(2)
            choose(0)
            residual(4, (0, 1))
            norm2(3)
            choose(1)
            residual(4, (2, 3))
            norm2(4)
            choose(2)
            choose(3)
            choose(4)
            v.wait_ge(s_rk, 1)
            ranks = rank[:, :, 0:NE]
            link(v.scalar_tensor_tensor(out=ranks, in0=ps[:, 0, 0:NT * NE].rearrange("p (t e) -> p t e", e=NE), scalar=1.0, in1=sel[:], op0=ALU.add, op1=ALU.mult))
            v.tensor_scalar(ranks, ranks, -1.0, None, ALU.add).then_inc(s_tab, 1)
            v.tensor_copy(cnt[0:1, 0:NE], ps[0:1, 0, NT * NE:(NT + 1) * NE]).then_inc(s_tab, 1)
            link(v.tensor_reduce(cntf[0:1, 0:1], ps[0:1, 0, NT * NE:(NT + 1) * NE], AX, ALU.max))
            v.tensor_copy(cnt[0:1, NE:NE + 1], cntf[0:1, 0:1]).then_inc(s_tab, 1)
            v.wait_ge(s_tab, 3)

            def expert_lo(ck, j):
                split_lo(ck.raw_slot(j), ck.slot(j), ck.number(j + 1))

            def indices(m, column, link_at):
                v.wait_ge(s_ix, m + 1)
                v.tensor_scalar(unused[:], ps[:, 6, 0:2], 0.0, UNUSED, ALU.is_equal, ALU.mult).then_inc(s_dve, 1)
                v.wait_ge(s_dve, link_at + 1)
                v.scalar_tensor_tensor(out=idx[:, bass.ds(column, 1), :].rearrange("p a b -> p (a b)"), in0=ps[:, 6, 0:2], scalar=-1.0, in1=unused[:],
                                       op0=ALU.add, op1=ALU.add).then_inc(s_ixe, 1)

            def rows_lo(m, hi_sem, done, dst, dst_hi):
                v.wait_ge(hi_sem, m + 1)
                src = ps[:, 6:8, :].rearrange("p b (k c) -> p (b k) c", c=P)
                v.tensor_tensor(dst, src, dst_hi.bitcast(F32), ALU.subtract).then_inc(done, 1)

            def clamp(m, half, w1_done):
                cols = slice(512 * half, 512 * half + 512)
                src = ps[:, 2 * half:2 * half + 2, :].rearrange("p b (n two) -> p two (b n)", two=2)
                v.wait_ge(s_pc, w1_done)
                if not isinstance(m, int) or m > 0:
                    v.wait_ge(s_ac, m * 2)
                v.tensor_scalar(glu[:, cols], src[:, 0, :], LIMIT, None, ALU.min).then_inc(s_g, 1)
                v.tensor_scalar(lin[:, cols], src[:, 1, :], LIMIT, -LIMIT, ALU.min, ALU.max).then_inc(s_l, 1)

            base = chain[0]
            v.wait_ge(s_lge, NT)
            v.tensor_tensor(onehot, iota[:, 0:P].unsqueeze(1).to_broadcast([P, NT, P]),
                            rank[:, :, 0:1].to_broadcast([P, NT, P]), ALU.is_equal).then_inc(s_ohd, 1)
            expert_lo(start, 0)
            indices(0, 0, base)
            expert_lo(start, 1)
            expert_lo(start, 2)
            rows_lo(0, s_xh, s_xl, first_lo, first_hi)
            expert_lo(start, 3)
            indices(1, 1, base + 1)
            for j in range(RING, W1C):
                expert_lo(start, j)
                if j == 6:
                    rows_lo(1, s_xh, s_xl, x_lo, x_hi)
            head = Chunks(PRO + W1C, 0)
            for j in range(3):
                expert_lo(head, j)
            clamp(0, 0, W1C)
            clamp(0, 1, W1C)
            expert_lo(head, 3)
            indices(2, 2, base + 2)

            def body(n, j0=0):
                ck = Chunks(PRO + W1C, n)
                before_act = 6 if j0 == 4 else 4
                for j in range(j0, before_act):
                    expert_lo(ck, j)
                rows_lo(n, s_ah, s_al, act_lo, act_hi)
                if before_act == 4:
                    expert_lo(ck, 4)
                indices(n + 3, n + 3, n + (base + 3))
                for j in range(max(5, before_act), 11):
                    expert_lo(ck, j)
                clamp(n + 1, 0, ck.number(W1C) - PRO)
                clamp(n + 1, 1, ck.number(W1C) - PRO)
                expert_lo(ck, 11)
                rows_lo(n + 2, s_xh, s_xl, x_lo, x_hi)

            body(0, 4)
            with v.Fori(1, NE - 1) as n:
                body(n)
            tail = Chunks(PRO + W1C + PER * (NE - 1), 0)
            for j in range(3):
                expert_lo(tail, j)
            rows_lo(NE - 1, s_ah, s_al, act_lo, act_hi)
            expert_lo(tail, 3)

            after = base + NE + 2
            def further(e, r, i):
                ck = Chunks(EXTRA, i)
                indices(i + (NE + 2), SPARE, i + after)
                rows_lo(i + (NE + 1), s_xh, s_xl, x_lo, x_hi)
                for j in range(W1C):
                    expert_lo(ck, j)
                for half in range(2):
                    clamp(i + NE, half, ck.number(W1C) - PRO)
                rows_lo(i + NE, s_ah, s_al, act_lo, act_hi)
                for j in range(W1C, PER):
                    expert_lo(ck, j)
                v.wait_ge(s_sca, i * 16 + 16 * (NE + 1))
                v.sem_inc(s_carry, 1)

            further_blocks(v, further)
            def gated_sum(p):
                t = FINAL[p]
                n = TILES[t][1]
                v.wait_ge(s_fy[t], 16)
                rows = choices[t].rearrange("p (k d) -> p k d", k=TOPK)
                h = h_res[0:n, SLOT_H[t], :]
                for k in range(TOPK):
                    e = v.scalar_tensor_tensor(out=h, in0=rows[0:n, k, :], scalar=gate[0:n, t, k:k + 1], in1=h, op0=ALU.mult, op1=ALU.add)
                    if k < TOPK - 1:
                        e.then_inc(s_fk, 1)
                        v.wait_ge(s_fk, 3 * p + k + 1)
                e.then_inc(s_fs, 1)

            gated_sum(0)
            for p, t in enumerate(FINAL):
                n = TILES[t][1]
                if p + 1 < NT:
                    gated_sum(p + 1)
                v.wait_ge(s_fr, 2 * p + 2)
                v.reciprocal(st[0:n, 50 + t:51 + t], st[0:n, 50 + t:51 + t]).then_inc(s_fc, 1)
                if p >= 3:
                    v.wait_ge(s_fc, p + 1)
                    v.wait_ge(s_gf, 16)
                    v.scalar_tensor_tensor(out=y_fin(t)[0:n, :], in0=h_res[0:n, SLOT_H[t], :], scalar=st[0:n, 50 + t:51 + t],
                                           in1=raw[0:n, 3, 0:D], op0=ALU.mult, op1=ALU.mult).then_inc(s_fd, 1)

        @block.tensor
        def _(pe):
            pe.wait_ge(s_g1, 32)
            def x_transposed(t):
                n = TILES[t][1]
                pe.wait_ge(s_xn, t + 1)
                if t >= 2:
                    pe.wait_ge(s_tl, t - 1)
                for k in range(KT):
                    last = pe.transpose(ps[:, 2 * (t % 2) + k // 4, P * (k % 4):P * (k % 4) + n], xn[t % 2][0:n, P * k:P * k + P], ident[0:n, 0:n])
                last.then_inc(s_tp, 1)

            def three(out, lhs, rhs, start, stop):
                for q, (l, r) in enumerate(((lhs[0], rhs[0]), (lhs[0], rhs[1]), (lhs[1], rhs[0]))):
                    last = pe.matmul(out, l, r, start=start and q == 0, stop=stop and q == 2)
                return last

            def k_transposes(hp):
                pe.wait_ge(s_ze, LAST_UNIT[4 + hp])
                if hp:
                    pe.wait_ge(s_kte, 1)
                for hh in range(2):
                    cols = slice(P * (2 * hp + hh), P * (2 * hp + hh) + P)
                    for t in range(4):
                        pe.transpose(ps[:, 2 * hh, P * t:P * t + P], k_nat[:, t, cols], ident)
                    last = pe.transpose(ps[:, 2 * hh + 1, 0:32], k_nat[0:32, 4, cols], ident[0:32, 0:32])
                last.then_inc(s_kt, 1)

            wv = [[r[:, s, :].rearrange("p (k n) -> p k n", k=KT) for s in range(RING)] for r in (hi, lo)]
            x_transposed(0)
            x_transposed(1)
            for i, (c, kind, t, part) in enumerate(UNITS):
                pe.wait_ge(s_lo, c + 1)
                if i < NT:
                    pe.wait_ge(s_tl, i + 1)
                if i >= 4:
                    pe.wait_ge(s_ze, i - 3)
                bank = 4 + i % 4
                w = [wv[0][c % RING], wv[1][c % RING]]
                for k in range(KT):
                    if kind == "q":
                        n = NTOK // 2
                        last = three(ps[:, bank, 0:n], [y[:, k, P * t:P * t + P] for y in w],
                                     [y[:, k, n * part:n * part + n] for y in (t_hi, t_lo)], k == 0, k == KT - 1)
                    else:
                        last = three(ps[:, bank, 0:256], [y[:, k, P * t:P * t + P] for y in (t_hi, t_lo)],
                                     [y[:, k, :] for y in w], k == 0, k == KT - 1)
                last.then_inc(s_z, 1)
                if i + 2 < NT:
                    x_transposed(i + 2)
                if i + 1 == LAST_UNIT[5]:
                    k_transposes(0)
                if i + 1 == LAST_UNIT[6]:
                    k_transposes(1)

            def diff(g):
                if g >= 2:
                    pe.wait_ge(s_de, g - 1)
                b = 2 * (g % 2)
                ch = slice(P * g, P * g + P)
                for j in range(4):
                    out = ps[:, b, P * j:P * j + P]
                    if j:
                        pe.matmul(out, u_nat[:, j - 1, ch], band[:, g, 2, :], start=True, stop=False)
                    pe.matmul(out, u_nat[:, j, ch], band[:, g, 1 if j else 0, :], start=not j, stop=True)
                pe.matmul(ps[:, b + 1, 0:32], state[0:NB * BUF, ch], sband[0:NB * BUF, g, 0, :], start=True, stop=False)
                pe.matmul(ps[:, b + 1, 0:32], u_smp[0:32, ch], sband[0:32, g, 1, :], start=False, stop=True).then_inc(s_d, 1)

            def linear(g):
                pe.wait_ge(s_de, g + 1)
                if g >= 2:
                    pe.wait_ge(s_pl, g - 1)
                b = 4 + 2 * (g % 2)
                pe.matmul(ps[:, b, :], pw[:, g, :], d_t[g % 2][:, 0:512], start=True, stop=True)
                pe.matmul(ps[:, b + 1, 0:32], pw[:, g, :], d_t[g % 2][:, 512:544], start=True, stop=True).then_inc(s_po, 1)

            pe.wait_ge(s_late, 32)
            pe.wait_ge(s_kte, 2)
            pe.wait_ge(s_ze, len(UNITS))
            diff(0)
            for g in range(1, 4):
                diff(g)
                linear(g - 1)
            linear(3)

            def scores(i):
                qt, h = i // 4, i % 4
                nk = P * (qt + 1)
                if i >= 2:
                    pe.wait_ge(s_sb, i - 1)
                for c in range(2):
                    rows = slice(HD * c, HD * c + HD)
                    last = pe.matmul(ps[:, 2 * (i % 2) + c, 0:nk], q_t[rows, h, P * qt:P * qt + P], k_t[rows, h, 0:nk], start=True, stop=True)
                last.then_inc(s_sc, 1)

            def o_transposes(i, n):
                pe.wait_ge(s_on, i + 1)
                if i:
                    pe.wait_ge(s_ol, i)
                for h in range(H):
                    last = pe.transpose(ps[:, 7, P * h:P * h + n], o_nat[0:n, P * h:P * h + P], ident[0:n, 0:n])
                last.then_inc(s_ot, 1)

            pe.wait_ge(s_pl, 4)
            scores(0)
            scores(1)
            for i in range(17):
                if i < 16:
                    if i + 2 < 16:
                        scores(i + 2)
                    pe.wait_ge(s_a, i + 1)
                    if i >= 2:
                        pe.wait_ge(s_ate, i - 1)
                    for k in range(i // 4 + 1):
                        last = pe.transpose(ps[:, 4 + i % 2, P * k:P * k + P], aa[:, i % 2, P * k:P * k + P], ident)
                    last.then_inc(s_atr, 1)
                if i >= 1:
                    qt, h = (i - 1) // 4, (i - 1) % 4
                    if h == 0 and qt:
                        pe.wait_ge(s_oc, qt)
                    if h == 2 and qt:
                        o_transposes(qt - 1, P)
                    pe.wait_ge(s_ate, i)
                    for k in range(qt + 1):
                        last = pe.matmul(ps[:, 6, P * h:P * h + P], at_sb[:, (i - 1) % 2, P * k:P * k + P], v_nat[:, k, P * h:P * h + P], start=k == 0, stop=k == qt)
                    last.then_inc(s_pv, 1)
            def page_transposes(m):
                b, h = m // H, m % H
                if h == 0:
                    pe.wait_ge(s_pg[b % 3], 64 * (b // 3 + 1))
                if m >= 3:
                    pe.wait_ge(s_kc, m - 2)
                for k in range(PAGES):
                    last = pe.transpose(ps[:, m % 3, P * k:P * k + P], page[:, PAGES * (b % 3) + k, P * h:P * h + P], ident)
                last.then_inc(s_kp, 1)

            pe.wait_ge(s_qb, 2)
            pe.wait_ge(s_sb, 16)
            pe.wait_ge(s_ate, 16)
            page_transposes(0)
            for m in range(NB * H):
                b, h = m // H, m % H
                if m == 5:
                    o_transposes(3, P)
                if m + 1 < NB * H:
                    page_transposes(m + 1)
                pe.wait_ge(s_kc, m + 1)
                rows = slice(32 * (b % 4), 32 * (b % 4) + 32)
                pe.matmul(ps[rows, 4 + b // 4, :], q_blk[:, m, :], kt_s[:, m % 2, :], start=h == 0, stop=h == H - 1,
                          tile_position=(0, 32 * (b % 4)))
                pe.matmul(ps[rows, 3 + 3 * (b // 4), 0:32], q_blk[:, m, :], k_t[:, h, 512:544], start=h == 0, stop=h == H - 1,
                          tile_position=(0, 32 * (b % 4))).then_inc(s_sss, 1)
            def sample_transposes(t):
                pe.wait_ge(s_sa, t + 1)
                pe.wait_ge(s_kc, NB * H)
                for k in range(PAGES):
                    pe.transpose(ps[:, t, P * k:P * k + P], s_smp[:, t, P * k:P * k + P], ident)
                pe.transpose(ps[0:32, 2 + 3 * t, 0:P], s_smp[:, t, 512:544], ident).then_inc(s_ptr, 1)

            def sample_values(b):
                t, s = b // 4, NB + b
                pe.wait_ge(s_pe, t + 1)
                pe.wait_ge(s_pg[s % 3], 64 * (s // 3 + 1))
                if b % 4 == 0:
                    pe.wait_ge(s_oc, 4 + t)
                for h in range(H):
                    x = 5 * 64 * t + NS * (H * (b % 4) + h)
                    rows = slice(32 * (b % 4), 32 * (b % 4) + 32)
                    out = ps[rows, 6, P * h:P * h + P]
                    for k in range(PAGES):
                        pe.matmul(out, p_cols[:, x + 64 * k:x + 64 * k + 32], page[:, PAGES * (s % 3) + k, P * h:P * h + P],
                                  start=k == 0, stop=False, tile_position=(0, 32 * (b % 4)))
                    pe.matmul(out, p_cols[0:32, x + 256:x + 288], v_nat[0:32, 4, P * h:P * h + P],
                              start=False, stop=True, tile_position=(0, 32 * (b % 4))).then_inc(s_kp, 1)

            def out_product(t, chunks=range(4)):
                pe.wait_ge(s_ol, t + 1 if t < 4 else 6)
                for c in chunks:
                    i = 4 * t + c
                    if t == 0:
                        pe.wait_ge(s_lo, 8 + c + 1)
                    if i >= 2:
                        pe.wait_ge(s_he, i - 1)
                    w = [wv[0][(8 + c) % RING], wv[1][(8 + c) % RING]]
                    for k in range(KT):
                        last = three(ps[:, 3 + i % 2, 0:256], [y[:, k, P * t:P * t + P] for y in (t_hi, t_lo)],
                                     [y[:, k, :] for y in w], k == 0, k == KT - 1)
                    last.then_inc(s_w, 1)

            def h2_transposes(t):
                n = TILES[t][1]
                pe.wait_ge(s_h2, t + 1)
                if t >= 1:
                    pe.wait_ge(s_h2e, t)
                for k in range(KT):
                    last = pe.transpose(ps[:, k // 4, P * (k % 4):P * (k % 4) + n], h2[0:n, t % 2, P * k:P * k + P], ident[0:n, 0:n])
                last.then_inc(s_h2t, 1)

            def router(t):
                n = TILES[t][1]
                pe.wait_ge(s_h2e, t + 1)
                if t >= 2:
                    pe.wait_ge(s_lge, t - 1)
                hv = h2_t[:, t % 2, :].rearrange("p (k c) -> p k c", c=P)
                for k in range(KT):
                    last = pe.matmul(ps[0:n, 2 + 3 * (t % 2), 0:NE], hv[:, k, 0:n], rw[:, k, :], start=k == 0, stop=k == KT - 1)
                last.then_inc(s_lg, 1)

            for t in range(2):
                sample_transposes(t)
                out_product(t, (0, 1))
                sample_values(4 * t)
                out_product(t, (2, 3))
                for b in range(4 * t + 1, 4 * t + 4):
                    sample_values(b)
            o_transposes(4, P)
            out_product(2)
            pe.wait_ge(s_late2, 64)
            h2_transposes(0)
            out_product(3)
            router(0)
            o_transposes(5, P)
            h2_transposes(1)
            out_product(4, (0, 1))
            router(1)
            h2_transposes(2)
            out_product(4, (2, 3))
            router(2)
            h2_transposes(3)
            h2_transposes(4)
            router(3)
            router(4)
            pe.wait_ge(s_cum, NT)
            pe.matmul(ps[:, 0, 0:(NT + 1) * NE], ones, before.rearrange("p t e -> p (t e)"), start=True, stop=False)
            last = pe.matmul(ps[:, 0, 0:NT * NE], tri, sel.rearrange("p t e -> p (t e)"), start=False, stop=True)
            last.then_inc(s_rk, 1)
            pe.wait_ge(s_tab, 3)

            def index_product(m):
                pe.wait_ge(s_ohd, m + 1)
                if isinstance(m, int) and m == 0:
                    pe.wait_ge(s_pool_c, 2)
                for t in range(NT):
                    last = pe.matmul(ps[:, 6, 0:2], onehot[:, t, :], vals_c[:, t, :], start=t == 0, stop=t == NT - 1)
                last.then_inc(s_ix, 1)

            def row_transposes(src, wait, value, done):
                pe.wait_ge(wait, value)
                for k in range(KT):
                    last = pe.transpose(ps[:, 6 + k // 4, P * (k % 4):P * (k % 4) + P], src[:, P * k:P * k + P], ident)
                last.then_inc(done, 1)

            def x_transposes(m, gathered):
                if not isinstance(m, int) or m > 0:
                    pe.wait_ge(s_xl, m)
                row_transposes(xg, s_gat, gathered * 16, s_xt)

            def act_transposes(m):
                row_transposes(act, s_ac, m * 2 + 2, s_at)

            def expert_chunk(ck, j, lhs, k, banks, first_k, bias):
                pe.wait_ge(s_lo, ck.number(j + 1))
                tiles = 4 // banks
                base_bank = 0 if banks == 4 else 4
                for kk in range(tiles):
                    row = tiles * k + kk
                    for q, (l, r) in enumerate(((0, hi), (0, lo), (1, hi))):
                        for b in range(banks):
                            at = 512 * (banks * kk + b)
                            last = pe.matmul(ps[:, base_bank + b, :], lhs[l][:, row, :], r[:, ck.slot(j), at:at + 512],
                                             start=first_k and kk == 0 and q == 0, stop=False)
                if bias is not None:
                    pick, col = bias
                    for b in range(banks):
                        last = pe.matmul(ps[:, base_bank + b, :], pick[:], bias_r[:, col + 512 * b:col + 512 * b + 512], start=False, stop=True)
                last.then_inc(s_pc, 1)

            def w1(ck, j, m, selected, rows_ready, rows=(x_hi, x_lo)):
                if j == 0:
                    pe.wait_ge(s_xl, rows_ready)
                    if not isinstance(m, int) or m > 0:
                        pe.wait_ge(s_l, m * 2)
                if j == W1C - 1:
                    pe.wait_ge(s_bs, selected)
                expert_chunk(ck, j, rows, j, 4, j == 0, (sel_w1, 0) if j == W1C - 1 else None)

            def w2(ck, j, m, selected):
                k = j % 4
                if k == 0:
                    pe.wait_ge(s_al, m + 1)
                    if not isinstance(m, int) or m > 0:
                        pe.wait_ge(s_ye, m)
                if k == W2C - 1:
                    pe.wait_ge(s_bs, selected)
                expert_chunk(ck, j, (act_hi, act_lo), k, 2, k == 0, (sel_w2, 2 * D) if k == W2C - 1 else None)

            index_product(0)
            pe.wait_ge(s_ixe, 1)
            x_transposes(0, 1)
            start = Chunks(PRO, 0)
            for j in range(W1C):
                w1(start, j, 0, 1, 1, (first_hi, first_lo))
                if j == 0:
                    index_product(1)
                if j == 2:
                    pe.wait_ge(s_ixe, 2)
                    x_transposes(1, 2)

            def body(n):
                ck = Chunks(PRO + W1C, n)
                for j in range(W1C):
                    if j == 2:
                        if isinstance(n, int):
                            pe.wait_ge(s_ixe, 3)
                        act_transposes(n)
                    if j == 4:
                        pe.wait_ge(s_al, n + 1)
                        index_product(n + 3)
                    if j == 6:
                        pe.wait_ge(s_ixe, n + 4)
                        x_transposes(n + 2, n + 3)
                    w1(ck, j, n + 1, n + 2, n + 2)
                for j in range(W1C, PER):
                    w2(ck, j, n, n + 2)

            pe.wait_ge(s_xl, 2)
            index_product(2)
            body(0)
            with pe.Fori(1, NE - 1) as n:
                body(n)
            tail = Chunks(PRO + W1C + PER * (NE - 1), 0)
            pe.wait_ge(s_xl, NE + 1)
            act_transposes(NE - 1)
            for j in range(W2C):
                w2(tail, j, NE - 1, NE + 1)

            def further(e, r, i):
                ck = Chunks(EXTRA, i)
                index_product(i + (NE + 2))
                pe.wait_ge(s_ixe, i + (NE + 3))
                x_transposes(i + (NE + 1), i + (NE + 3))
                for j in range(W1C):
                    w1(ck, j, i + NE, i + (NE + 2), i + (NE + 2))
                act_transposes(i + NE)
                for j in range(W1C, PER):
                    w2(ck, j, i + NE, i + (NE + 2))
                pe.wait_ge(s_sca, i * 16 + 16 * (NE + 1))
                pe.sem_inc(s_carry, 1)

            further_blocks(pe, further)


_OUTS = [
    ("y_prompt", (1, SEQ, D)), ("y_sample", (NB, NS, D)),
    ("new_pool_prompt", (1, 1, BUF, POOLW)), ("new_pool_sample", (1, NB, BUF, POOLW)),
    ("new_k_prompt", (1, 1, SEQ, H, P)), ("new_v_prompt", (1, 1, SEQ, H, P)),
    ("new_k_sample", (1, NB, NS, H, P)), ("new_v_sample", (1, NB, NS, H, P)),
]


def program(nc, shapes):
    aps = {n: nc.dram_tensor(n, s, mybir.dt.from_np(t), kind="ExternalInput").ap() for n, (s, t) in shapes.items()}
    for n, s in _OUTS:
        aps[n] = nc.dram_tensor("out_" + n, s, F32, kind="ExternalOutput").ap()
    build(nc, aps)


def kernel(**inputs):
    import concourse.bacc as bacc
    from concourse.bass_utils import run_bass_kernel_spmd as run

    arrays = {n: np.ascontiguousarray(v) for n, v in inputs.items()}
    arrays.update(constants())
    nc = bacc.Bacc("TRN2", target_bir_lowering=False, num_devices=1)
    program(nc, {n: (v.shape, v.dtype) for n, v in arrays.items()})
    r = run(nc, [arrays], core_ids=[0])
    return tuple(r.results[0]["out_" + n] for n, _ in _OUTS)
```
